# Optimizing a Trainium2 kernel written in Bass

```python
import math
import jax, jax.numpy as jnp
from jax import lax
import numpy as np

D_MODEL = 1024
BATCH = 1
SEQ = 256
DEPTH = 1
DEC_BATCH = 8
DEC_SEQ = 4
PAST_LEN = 2048
PAGE_SIZE = 128

D_MIX = D_MODEL
S5_WIDTH = D_MIX // 4
S5_GROUP = 16
S5_GROUPS = S5_WIDTH // S5_GROUP
S5_STATE = 64
RG_WIDTH = D_MIX // 4
RG_BLOCKS = 8
RG_BLOCK = RG_WIDTH // RG_BLOCKS
RG_CONV = 4
RG_C = 8.0
ML_WIDTH = D_MIX // 2
ML_HEADS = 4
ML_DK = ML_WIDTH // ML_HEADS
ML_DV = ML_WIDTH // ML_HEADS
ML_CHUNK = 64
N_EXPERTS = 32
TOP_K = 4
D_FF = D_MODEL
SWIGLU_LIMIT = 7.0
SWIGLU_ALPHA = 1.702
MOE_BLOCK = 128
EPS = 1e-5

IN_SIZES = (S5_WIDTH, RG_WIDTH, RG_WIDTH, ML_WIDTH, ML_WIDTH, ML_WIDTH, ML_WIDTH, ML_HEADS, ML_HEADS)
N_IN = sum(IN_SIZES)
IN_SPLITS = tuple(int(s) for s in np.cumsum(IN_SIZES)[:-1])

kernel_name = "hybrid_s5_rglru_mlstm_moe_step"

F32 = jnp.float32

def rmsnorm(x, g):
    xf = x.astype(F32)
    y = xf * lax.rsqrt(jnp.mean(xf * xf, axis=-1, keepdims=True) + EPS)
    return (y * g.astype(F32)).astype(x.dtype)

def cmul(ar, ai, br, bi):
    return ar * br - ai * bi, ar * bi + ai * br

def s5_mixer(u, s0_re, s0_im, lam_re, lam_im, log_step, b_re, b_im, c_re, c_im, d, glu_w, glu_b):
    bsz, t_len, _ = u.shape
    ug = u.reshape(bsz, t_len, S5_GROUPS, S5_GROUP).astype(F32)
    step = jnp.exp(log_step.astype(F32))[:, None]
    lr = lam_re.astype(F32)
    li = lam_im.astype(F32)
    mag = jnp.exp(lr * step)
    ab_re = mag * jnp.cos(li * step)
    ab_im = mag * jnp.sin(li * step)
    den = lr * lr + li * li
    num_re = ab_re - 1.0
    z_re = (num_re * lr + ab_im * li) / den
    z_im = (ab_im * lr - num_re * li) / den
    bb_re, bb_im = cmul(z_re[..., None], z_im[..., None], b_re.astype(F32), b_im.astype(F32))
    bu_re = jnp.einsum('gpc,btgc->btgp', bb_re, ug)
    bu_im = jnp.einsum('gpc,btgc->btgp', bb_im, ug)
    a_re = jnp.broadcast_to(ab_re, bu_re.shape)
    a_im = jnp.broadcast_to(ab_im, bu_im.shape)

    def combine(e1, e2):
        a1r, a1i, b1r, b1i = e1
        a2r, a2i, b2r, b2i = e2
        ar, ai = cmul(a2r, a2i, a1r, a1i)
        br, bi = cmul(a2r, a2i, b1r, b1i)
        return ar, ai, br + b2r, bi + b2i

    acr, aci, sr, si = lax.associative_scan(combine, (a_re, a_im, bu_re, bu_im), axis=1)
    pr, pi = cmul(acr, aci, s0_re.astype(F32)[:, None], s0_im.astype(F32)[:, None])
    sr = sr + pr
    si = si + pi
    y = jnp.einsum('gcp,btgp->btgc', c_re.astype(F32), sr) - jnp.einsum('gcp,btgp->btgc', c_im.astype(F32), si)
    y = y.reshape(bsz, t_len, S5_WIDTH) + d.astype(F32) * u.astype(F32)
    g = jax.nn.gelu(y)
    out = g * jax.nn.sigmoid(g @ glu_w.astype(F32) + glu_b.astype(F32))
    return out.astype(u.dtype), sr[:, -1], si[:, -1]

def causal_conv(x, buf, w, b):
    t_len = x.shape[1]
    xp = jnp.concatenate([buf.astype(x.dtype), x], axis=1)
    y = sum(xp[:, j:j + t_len] * w[j] for j in range(RG_CONV)) + b
    return y, xp[:, -(RG_CONV - 1):]

def rglru_mixer(x, gate, h0, conv_buf, conv_w, conv_b, wa, ba, wx, bx, lam):
    bsz, t_len, _ = x.shape
    xc, new_buf = causal_conv(x, conv_buf, conv_w, conv_b)
    xc = xc.astype(F32)
    xb = xc.reshape(bsz, t_len, RG_BLOCKS, RG_BLOCK)
    r = jax.nn.sigmoid(jnp.einsum('btni,nij->btnj', xb, wa.astype(F32)).reshape(bsz, t_len, RG_WIDTH) + ba)
    i = jax.nn.sigmoid(jnp.einsum('btni,nij->btnj', xb, wx.astype(F32)).reshape(bsz, t_len, RG_WIDTH) + bx)
    log_a = -RG_C * r * jax.nn.softplus(-lam.astype(F32))
    a = jnp.exp(log_a)
    bt = jnp.sqrt(-jnp.expm1(2.0 * log_a)) * (i * xc)

    def combine(e1, e2):
        a1, b1 = e1
        a2, b2 = e2
        return a1 * a2, a2 * b1 + b2

    acum, hs = lax.associative_scan(combine, (a, bt), axis=1)
    h = hs + acum * h0.astype(F32)[:, None]
    y = h * jax.nn.gelu(gate.astype(F32))
    return y.astype(x.dtype), h[:, -1], new_buf

def mlstm_mixer(q, k, v, ig, fg, o, c0, n0, m0, norm_g):
    bsz, t_len, _ = q.shape
    L = math.gcd(t_len, ML_CHUNK)
    nc = t_len // L

    def heads(z):
        return z.reshape(bsz, nc, L, ML_HEADS, -1).transpose(1, 0, 3, 2, 4).astype(F32)

    def gates(z):
        return z.reshape(bsz, nc, L, ML_HEADS).transpose(1, 0, 3, 2).astype(F32)

    qh = heads(q)
    kh = heads(k) * (ML_DK ** -0.5)
    vh = heads(v)
    igh = gates(ig)
    lfh = jax.nn.log_sigmoid(gates(fg))
    causal = jnp.tril(jnp.ones((L, L), bool))

    def chunk(carry, inp):
        cm, nv, m = carry
        qc, kc, vc, ic, fc = inp
        b = jnp.cumsum(fc, axis=-1)
        dmat = b[..., :, None] - b[..., None, :] + ic[..., None, :]
        dmat = jnp.where(causal, dmat, -jnp.inf)
        inter = b + m[..., None]
        mt = jnp.maximum(inter, jnp.max(dmat, axis=-1))
        s = jnp.einsum('bhtd,bhsd->bhts', qc, kc) * jnp.exp(dmat - mt[..., None])
        sc = jnp.exp(inter - mt)
        num = jnp.einsum('bhts,bhsd->bhtd', s, vc) + sc[..., None] * jnp.einsum('bhtk,bhkv->bhtv', qc, cm)
        den = jnp.sum(s, axis=-1) + sc * jnp.einsum('bhtk,bhk->bht', qc, nv)
        h = num / jnp.maximum(jnp.abs(den), jnp.exp(-mt))[..., None]
        bl = b[..., -1]
        m_new = mt[..., -1]
        ws = jnp.exp(bl[..., None] - b + ic - m_new[..., None])
        decay = jnp.exp(bl + m - m_new)
        c_new = decay[..., None, None] * cm + jnp.einsum('bhs,bhsk,bhsv->bhkv', ws, kc, vc)
        n_new = decay[..., None] * nv + jnp.einsum('bhs,bhsk->bhk', ws, kc)
        return (c_new, n_new, m_new), h

    (cf, nf, mf), hs = lax.scan(chunk, (c0.astype(F32), n0.astype(F32), m0.astype(F32)), (qh, kh, vh, igh, lfh))
    h = hs.transpose(1, 0, 3, 2, 4).reshape(bsz, t_len, ML_HEADS, ML_DV)
    h = h * lax.rsqrt(jnp.mean(h * h, axis=-1, keepdims=True) + EPS) * norm_g.astype(F32).reshape(ML_HEADS, ML_DV)
    y = h.reshape(bsz, t_len, ML_WIDTH) * jax.nn.sigmoid(o.astype(F32))
    return y.astype(q.dtype), cf, nf, mf

def moe(x, router_w, router_b, w1, b1, w2, b2):
    bsz, t_len, dm = x.shape
    xf = x.reshape(-1, dm)
    ntok = xf.shape[0]
    logits = (xf @ router_w + router_b).astype(F32)
    top_val, top_idx = lax.top_k(logits, TOP_K)
    gates = jax.nn.softmax(top_val, axis=-1)
    n_assign = ntok * TOP_K
    flat_e = top_idx.reshape(-1)
    order = jnp.argsort(flat_e)
    sorted_e = flat_e[order]
    counts = jnp.bincount(flat_e, length=N_EXPERTS)
    padded = (counts + MOE_BLOCK - 1) // MOE_BLOCK * MOE_BLOCK
    pad_end = jnp.cumsum(padded)
    pad_start = pad_end - padded
    start = jnp.cumsum(counts) - counts
    dest = pad_start[sorted_e] + jnp.arange(n_assign) - start[sorted_e]
    n_blocks = -(-n_assign // MOE_BLOCK) + N_EXPERTS
    n_slots = n_blocks * MOE_BLOCK
    slot_tok = jnp.full((n_slots,), ntok, jnp.int32).at[dest].set((order // TOP_K).astype(jnp.int32))
    slot_gate = jnp.zeros((n_slots,), F32).at[dest].set(gates.reshape(-1)[order])
    block_e = jnp.minimum(jnp.searchsorted(pad_end, jnp.arange(n_blocks) * MOE_BLOCK, side='right'), N_EXPERTS - 1)
    x_pad = jnp.concatenate([xf, jnp.zeros((1, dm), xf.dtype)], axis=0)

    def expert_block(args):
        tok, e = args
        hb = x_pad[tok] @ w1[e] + b1[e]
        g = jnp.minimum(hb[:, :D_FF], SWIGLU_LIMIT)
        u = jnp.clip(hb[:, D_FF:], -SWIGLU_LIMIT, SWIGLU_LIMIT)
        act = g * jax.nn.sigmoid(SWIGLU_ALPHA * g) * (u + 1.0)
        return act @ w2[e] + b2[e]

    yb = lax.map(expert_block, (slot_tok.reshape(n_blocks, MOE_BLOCK), block_e))
    y = jnp.zeros((ntok + 1, dm), F32).at[slot_tok].add(yb.reshape(n_slots, dm).astype(F32) * slot_gate[:, None])
    return y[:ntok].reshape(bsz, t_len, dm).astype(x.dtype)

def setup_inputs(seed: int = 0) -> dict:
    key = jax.random.key(seed)
    ks = iter(jax.random.split(key, 48))
    nrm = lambda shape, s: jax.random.normal(next(ks), shape, F32) * s
    uni = lambda shape, lo, hi: jax.random.uniform(next(ks), shape, F32, lo, hi)
    G, P = S5_GROUPS, S5_STATE
    inp = {}
    inp['x_prompt'] = nrm((BATCH, SEQ, D_MODEL), 1.0)
    inp['x_sample'] = nrm((DEC_BATCH, DEC_SEQ, D_MODEL), 1.0)
    inp['state_s5_re'] = nrm((DEPTH, DEC_BATCH, G, P), 0.3)
    inp['state_s5_im'] = nrm((DEPTH, DEC_BATCH, G, P), 0.3)
    inp['state_rg_h'] = nrm((DEPTH, DEC_BATCH, RG_WIDTH), 0.5)
    inp['state_rg_conv'] = nrm((DEPTH, DEC_BATCH, RG_CONV - 1, RG_WIDTH), 1.0)
    inp['state_ml_c'] = nrm((DEPTH, DEC_BATCH, ML_HEADS, ML_DK, ML_DV), 0.3)
    inp['state_ml_n'] = nrm((DEPTH, DEC_BATCH, ML_HEADS, ML_DK), 0.3)
    inp['state_ml_m'] = uni((DEPTH, DEC_BATCH, ML_HEADS), 0.0, 4.0)
    inp['norm1_g'] = 1.0 + nrm((DEPTH, D_MODEL), 0.02)
    inp['w_in'] = nrm((DEPTH, D_MODEL, N_IN), D_MODEL ** -0.5)
    inp['s5_lambda_re'] = -0.5 + nrm((DEPTH, G, P), 0.01)
    inp['s5_lambda_im'] = jnp.pi * jnp.arange(P, dtype=F32) + nrm((DEPTH, G, P), 0.01)
    inp['s5_log_step'] = uni((DEPTH, G), math.log(1e-3), math.log(1e-1))
    inp['s5_b_re'] = nrm((DEPTH, G, P, S5_GROUP), (2 * S5_GROUP) ** -0.5)
    inp['s5_b_im'] = nrm((DEPTH, G, P, S5_GROUP), (2 * S5_GROUP) ** -0.5)
    inp['s5_c_re'] = nrm((DEPTH, G, S5_GROUP, P), (2 * P) ** -0.5)
    inp['s5_c_im'] = nrm((DEPTH, G, S5_GROUP, P), (2 * P) ** -0.5)
    inp['s5_d'] = nrm((DEPTH, S5_WIDTH), 0.5)
    inp['s5_glu_w'] = nrm((DEPTH, S5_WIDTH, S5_WIDTH), S5_WIDTH ** -0.5)
    inp['s5_glu_b'] = nrm((DEPTH, S5_WIDTH), 0.02)
    inp['rg_conv_w'] = nrm((DEPTH, RG_CONV, RG_WIDTH), RG_CONV ** -0.5)
    inp['rg_conv_b'] = nrm((DEPTH, RG_WIDTH), 0.02)
    inp['rg_wa'] = nrm((DEPTH, RG_BLOCKS, RG_BLOCK, RG_BLOCK), RG_BLOCK ** -0.5)
    inp['rg_ba'] = nrm((DEPTH, RG_WIDTH), 0.02)
    inp['rg_wx'] = nrm((DEPTH, RG_BLOCKS, RG_BLOCK, RG_BLOCK), RG_BLOCK ** -0.5)
    inp['rg_bx'] = nrm((DEPTH, RG_WIDTH), 0.02)
    a_c = uni((DEPTH, RG_WIDTH), 0.9, 0.999)
    p_a = a_c ** (1.0 / RG_C)
    inp['rg_lambda'] = jnp.log(p_a) - jnp.log1p(-p_a)
    f_bias = jnp.broadcast_to(jnp.linspace(3.0, 6.0, ML_HEADS, dtype=F32), (DEPTH, ML_HEADS))
    inp['ml_gate_bias'] = jnp.concatenate([jnp.zeros((DEPTH, ML_HEADS), F32), f_bias], axis=-1) + nrm((DEPTH, 2 * ML_HEADS), 0.1)
    inp['ml_norm_g'] = 1.0 + nrm((DEPTH, ML_WIDTH), 0.02)
    inp['w_out'] = nrm((DEPTH, D_MIX, D_MODEL), (2 * D_MIX) ** -0.5)
    inp['norm2_g'] = 1.0 + nrm((DEPTH, D_MODEL), 0.02)
    inp['router_w'] = nrm((DEPTH, D_MODEL, N_EXPERTS), D_MODEL ** -0.5)
    inp['router_b'] = nrm((DEPTH, N_EXPERTS), 0.01)
    inp['exp_w1'] = nrm((DEPTH, N_EXPERTS, D_MODEL, 2 * D_FF), D_MODEL ** -0.5)
    inp['exp_b1'] = nrm((DEPTH, N_EXPERTS, 2 * D_FF), 0.02)
    inp['exp_w2'] = nrm((DEPTH, N_EXPERTS, D_FF, D_MODEL), (2 * D_FF) ** -0.5)
    inp['exp_b2'] = nrm((DEPTH, N_EXPERTS, D_MODEL), 0.02)
    inp['final_norm_g'] = 1.0 + nrm((D_MODEL,), 0.02)
    return inp

def reference(x_prompt, x_sample, state_s5_re, state_s5_im, state_rg_h, state_rg_conv, state_ml_c, state_ml_n, state_ml_m,
              norm1_g, w_in, s5_lambda_re, s5_lambda_im, s5_log_step, s5_b_re, s5_b_im, s5_c_re, s5_c_im, s5_d,
              s5_glu_w, s5_glu_b, rg_conv_w, rg_conv_b, rg_wa, rg_ba, rg_wx, rg_bx, rg_lambda, ml_gate_bias, ml_norm_g,
              w_out, norm2_g, router_w, router_b, exp_w1, exp_b1, exp_w2, exp_b2, final_norm_g):

    def trunk(x, s5r, s5i, rgh, rgc, mlc, mln, mlm):
        outs = [[] for _ in range(7)]
        for l in range(DEPTH):
            h = rmsnorm(x, norm1_g[l])
            z = h @ w_in[l]
            u_s5, x_rg, g_rg, q, k, v, o, gi, gf = jnp.split(z, IN_SPLITS, axis=-1)
            y1, nr, ni = s5_mixer(u_s5, s5r[l], s5i[l], s5_lambda_re[l], s5_lambda_im[l], s5_log_step[l],
                                  s5_b_re[l], s5_b_im[l], s5_c_re[l], s5_c_im[l], s5_d[l], s5_glu_w[l], s5_glu_b[l])
            y2, nh, ncv = rglru_mixer(x_rg, g_rg, rgh[l], rgc[l], rg_conv_w[l], rg_conv_b[l], rg_wa[l], rg_ba[l],
                                      rg_wx[l], rg_bx[l], rg_lambda[l])
            y3, nC, nn, nm = mlstm_mixer(q, k, v, gi + ml_gate_bias[l, :ML_HEADS], gf + ml_gate_bias[l, ML_HEADS:], o,
                                         mlc[l], mln[l], mlm[l], ml_norm_g[l])
            mix = jnp.concatenate([y1.astype(x.dtype), y2.astype(x.dtype), y3.astype(x.dtype)], axis=-1)
            x = x + mix @ w_out[l]
            x = x + moe(rmsnorm(x, norm2_g[l]), router_w[l], router_b[l], exp_w1[l], exp_b1[l], exp_w2[l], exp_b2[l])
            for lst, val in zip(outs, (nr, ni, nh, ncv, nC, nn, nm)):
                lst.append(val)
        return rmsnorm(x, final_norm_g), [jnp.stack(s) for s in outs]

    bp = x_prompt.shape[0]
    zeros = lambda *shape: jnp.zeros((DEPTH, bp) + shape, F32)
    y_prompt, sp = trunk(x_prompt, zeros(S5_GROUPS, S5_STATE), zeros(S5_GROUPS, S5_STATE), zeros(RG_WIDTH),
                         zeros(RG_CONV - 1, RG_WIDTH), zeros(ML_HEADS, ML_DK, ML_DV), zeros(ML_HEADS, ML_DK), zeros(ML_HEADS))
    y_sample, ss = trunk(x_sample, state_s5_re, state_s5_im, state_rg_h, state_rg_conv, state_ml_c, state_ml_n, state_ml_m)
    return (y_prompt, y_sample, sp[0], sp[1], sp[2], sp[3], sp[4], sp[5], sp[6], ss[0], ss[1], ss[2], ss[3], ss[4], ss[5], ss[6])


_drawn_inputs = setup_inputs


def setup_inputs(seed=0):
    import zlib

    import numpy as np

    out = dict(_drawn_inputs(seed))
    spreads = {}
    factors = {'s5_lambda_re': 18.281,
     's5_glu_b': 25.328,
     'rg_ba': 8.0,
     'rg_bx': 7.181,
     'ml_norm_g': 3.018,
     'exp_b1': 6.942,
     'exp_b2': 5.644,
     'final_norm_g': 8.249,
     's5_c_re': 2.705,
     's5_c_im': 2.8,
     's5_glu_w': 4.738,
     'router_b': 4.37}
    for name, (base, spread) in spreads.items():
        noise = np.random.default_rng([zlib.crc32(name.encode()), seed]).standard_normal(out[name].shape)
        drawn = base * np.exp(spread * noise) if base else spread * noise
        out[name] = __import__('jax').numpy.asarray(drawn.astype(out[name].dtype))
    for name, factor in factors.items():
        out[name] = (out[name] * factor).astype(out[name].dtype)
    return out
```

```python
from contextlib import ExitStack
import math

import concourse.bass as bass
from concourse import mybir

ALU = mybir.AluOpType
ACT = mybir.ActivationFunctionType
AX = mybir.AxisListType
F32 = mybir.dt.float32
BF16 = mybir.dt.bfloat16
I32 = mybir.dt.int32
U32 = mybir.dt.uint32

D = 1024
KD = D // 128
TP, NB, NT = 256, 8, 4
TS = NB * NT
T = TP + TS
TILES = [(0, 128), (128, 128), (256, 32)]
G5, P5, C5 = 16, 64, 16
J5 = G5 * P5 // 128
RC = 8.0
H, DK = 4, 128
NE, TOPK, FF = 32, 4, 1024
NPAIR = NE // 2
SLOTS = 64
SWEEPS = -(-T // SLOTS)
EPS = 1e-5
CH = 4096

U0, XR0, GR0, Q0, K0, V0, O0, GI0 = 0, 256, 512, 768, 1280, 1792, 2304, 2816
VEC = {}
_row = 0
for _name, _n in (("norm1_g", 8), ("s5_d", 2), ("s5_glu_b", 2), ("rg_conv_w", 8), ("rg_conv_b", 2), ("rg_ba", 2),
                  ("rg_bx", 2), ("rg_lambda", 2), ("ml_norm_g", 4), ("s5_lambda_re", 8), ("s5_lambda_im", 8)):
    VEC[_name] = (_row, _n)
    _row += _n
NVEC = _row

ORDER = (["vec"] + [f"hT{i}" for i in range(6)] + ["gates", "u0", "u1", "xr0", "xr1", "par", "bt", "ct",
         "gr0", "gr1", "q0", "q1", "bu0r", "bu0i", "bu1r", "bu1i", "q2", "q3", "k0", "k1", "r0", "r1", "i0", "i1",
         "k2", "k3", "va0", "va1", "va2", "bu2r", "bu2i", "bu3r", "bu3i",
         "vb0", "vb1", "vb2", "oa0", "oa1", "oa2", "bu4r", "bu4i", "bu5r", "bu5i",
         "ob0", "ob1", "ob2", "bu6r", "bu6i", "bu7r", "bu7i", "rows", "kt0", "kt1", "kt2"]
         + [f"{n}{h}" for h in range(H) for n in ("mb", "st")] + ["dec"] + [f"sc{h}" for h in range(H)]
         + ["nu20", "nu21", "nu00", "nu01", "nu10", "nu11", "glu0", "glu1"]
         + [f"cu{h}{g}" for h in range(H) for g in range(3)] + ["cp0", "cp1", "nT", "rgT", "s5T"]
         + [f"yT{h}" for h in range(H)]
         + [f"wo{i}{n}" for i in range(3) for n in range(2)] + [f"h2T{i}" for i in range(6)] + ["lg", "cum"])
FILLS = {}
for _i, _n in enumerate(ORDER):
    FILLS[_n] = (_i % 6, _i // 6)
FILLS["ys0"] = (6, 0)
FILLS["ys1"] = (7, 0)
SAID = {
    "dve_said": [("nst_set", 1), ("var_ready", 1), ("xn_ready", 3), ("angle_reduced", 1), ("bb_ready", 4),
        ("cb_ready", 2), ("gate_abs", 1), ("rg_decay", 1), ("m_rows", 1), ("gate_rows", 1), ("xc_ready", 2),
        ("scm_ready", 8), ("s5_scanned", 4), ("rg_ratio", 1), ("rgfin_ready", 1), ("gate_poly", 1),
        ("s5_scanned", 4), ("mix_ready", 1), ("ones_ready", 1), ("e_arg", 4), ("wsm_ready", 1), ("kw_ready", 1),
        ("qm_ready", 1), ("dec_ready", 1), ("den_read", 1), ("nvar_ready", 1), ("den_read", 1), ("nvar_ready", 1),
        ("den_read", 1), ("nvar_ready", 1), ("y3_ready", 1), ("s5_poly", 1), ("s5_gelu", 1), ("rg_used", 1),
        ("c_new", 4), ("x1_added", 6), ("var2_ready", 1), ("x2_ready", 3), ("top_diff", 1), ("mask_ready", 1),
        ("count_ready", 1)],
    "act_said": [("ms_ready", 3), ("root_ready", 1), ("step_ready", 1), ("mag_ready", 1), ("act_rg", 2),
        ("angle_ready", 2), ("gate_exp", 1), ("xp_ready", 2), ("wc_ready", 1), ("gate_rows_exp", 3), ("rg_tanh", 2),
        ("rg_a", 2), ("rg_root", 1), ("gate_tanh", 1), ("rtok_ready", 1), ("e_exp", 4), ("nsq_ready", 4),
        ("nroot_ready", 1), ("nsq_ready", 4), ("nroot_ready", 1), ("nsq_ready", 4), ("nroot_ready", 1),
        ("s5_tanh", 1), ("c_prompt", 2), ("n_staged", 1), ("rg_staged", 2), ("s5_staged", 2), ("ms2_ready", 3),
        ("root2_ready", 1), ("top_exp", 1)],
    "pool_said": [("ident_ready", 1), ("weights_zero", 1), ("bb_zero", 1), ("seg_ready", 1), ("causal_ready", 1),
        ("sel4_ready", 1), ("ind_ready", 1), ("rows_zero", 1), ("table_ready", 1), ("e_zero", 1), ("s5_turned", 8),
        ("vw_ready", 2), ("c_decayed", 4), ("vw_ready", 2), ("bias_ready", 1), ("acc_zero", 1)],
    "pe_said": [("xn_used", 1), ("w_in_used", 2), ("cb_used", 1), ("w_in_used", 2), ("s5_used", 2), ("w_in_used", 1),
        ("s5_used", 2), ("w_in_used", 1), ("s5_used", 4), ("v_ready", 1), ("c0_used", 1), ("vw_used", 4),
        ("y_turned", 1), ("w_out_used", 1), ("mixer_done", 1)],
}
SAID_BY, VALUES = {}, {}
for _line, _said in SAID.items():
    _at = 0
    for _name, _times in _said:
        for _ in range(_times):
            _at += 1
            SAID_BY[_name] = _line
            VALUES.setdefault(_name, []).append(_at)
CB = [(0, 3), (3, 6), (6, 8)]


def spread(v, axis, n):
    shape = list(v.shape)
    shape[axis] = n
    return v.broadcast_to(shape)


def build_program(nc, a, o):
    ctx = ExitStack()
    with ctx:
        def sb(name, shape, dt=F32):
            return ctx.enter_context(nc.sbuf_tensor(name, shape, dt))

        ring = sb("ring", [128, 6, CH])
        xn = sb("xn", [128, 3, D])
        acc = sb("acc", [128, 3, D])
        x1 = sb("x1", [128, 3, D])
        bsplit = sb("bsplit", [128, 3 * D], BF16)
        ident = sb("ident", [128, 128])
        upper = sb("upper", [128, 128], BF16)
        ones_bf = sb("ones_bf", [128, 128], BF16)
        iota_e = sb("iota_e", [128, NE])
        iota_s = sb("iota_s", [128, SLOTS])
        half = sb("half", [128, 2, SLOTS])
        selid = sb("selid", [128, NPAIR + 1])
        cnt = sb("cnt", [128, 1], I32)
        st2 = sb("st2", [128, 16])
        psum = ctx.enter_context(nc.psum_tensor("psum", [128, 8, 512], F32))

        def carve(base, shape):
            region, at = base
            n = math.prod(shape[1:])
            v = region[0:shape[0], at:at + n]
            if len(shape) == 3:
                v = v.rearrange("p (x y) -> p x y", x=shape[1])
            if len(shape) == 4:
                v = v.rearrange("p (x y z) -> p x y z", x=shape[1], y=shape[2])
            base[1] += n
            assert base[1] <= region.shape[1], (shape, base[1])
            return v

        mx = ExitStack()

        def ms(name, shape, dt=F32):
            return mx.enter_context(nc.sbuf_tensor(name, shape, dt))

        hT = ms("hT", [128, KD, T])
        uT = ms("uT", [128, 2, T])
        xpP = ms("xpP", [128, 2, 3 + TP])
        qT = ms("qT", [128, H, T])
        kT = ms("kT", [128, H, T])
        tabc = ms("tabc", [128, 2, J5, T])
        tab_r, tab_i = tabc[:, 0], tabc[:, 1]
        c0 = tabc[:].rearrange("p x j t -> p (x j t)")[:, 0:H * NB * 129].rearrange("p (h b v) -> p h b v", h=H, b=NB)
        t_dve, t_pool = ms("t_dve", [128, T]), ms("t_pool", [128, T])
        fin5 = ms("fin5", [128, 2, 1 + NB, J5])
        wC = ms("wC", [128, 4, 128])
        causal = ms("causal", [128, 416])
        seg = ms("seg", [128, T])
        vecs, parT = ms("vecs", [128, 128]), ms("parT", [128, 256])
        sm = ms("sm", [128, 26, J5])
        rsm = ms("rsm", [128, 64])
        gsm = ms("gsm", [128, 8, T])
        sel4 = ms("sel4", [H, H, 128])
        scm = ms("scm", [H, NB, TS])
        gb = ms("gb", [H, 2])
        m0 = ms("m0", [H, NB])
        dec = ms("dec", [128, H, NB])
        wsm = ms("wsm", [TS, H, NB])
        nbuf = ms("nbuf", [128, 36])
        rgfin = ms("rgfin", [128, 2, 9])
        cvfin = ms("cvfin", [128, 2, 27])
        nst = ms("nst", [128, 16])
        glw = ms("glw", [128, 2, 256])
        ra = [ring[:, 4:6, :].rearrange("p s n -> p (s n)"), 0]
        v_tok = carve(ra, [128, 3, H, 129])
        E = carve(ra, [128, H, 416])
        qm = carve(ra, [128, H, NB, TS])
        kw = carve(ra, [128, 2, H, 128])
        vw = carve(ra, [TS, 2, NB, 129])
        cP = carve(ra, [128, H, 129])
        rb = [ra[0], H * 129 * 3]
        pt1, pt2 = carve(rb, [128, J5, 128]), carve(rb, [128, J5, 128])
        rb[1] = H * 129 * 3 + H * 416 + H * NB * TS
        b_in = carve(rb, [128, 2, J5, C5])
        b_t = carve(rb, [128, 2, J5, C5])
        BB = carve(rb, [128, 2 * J5, 2, C5])
        c_in = carve(rb, [128, 4, P5])
        CBk = carve(rb, [128, 4, 2 * P5])
        vrow, srow, prow = carve(rb, [128, 128]), carve(rb, [128, 128]), carve(rb, [128, 128])
        rb = [ring[:, 3, :], 0]
        w_r, w_i, s_r, s_i = (carve(rb, [128, 2, T]) for _ in range(4))
        wB, wax = carve(rb, [128, 4, 128]), carve(rb, [128, 2, 2, 128])
        d0s, xpS, wgate = carve(rb, [128, J5, TS]), carve(rb, [128, 2, NB, 3 + NT]), carve(rb, [128, KD, 36])
        rb = [x1[:].rearrange("p i n -> p (i n)"), 0]
        k_tok, o_tok = carve(rb, [128, 3, 512]), carve(rb, [128, 3, 512])
        rb = [acc[:].rearrange("p i n -> p (i n)"), 0]
        xc, rr, ri, rt, gate = (carve(rb, [128, 2, T]) for _ in range(5))
        rb = [xn[:].rearrange("p i n -> p (i n)"), 0]
        bias_in = carve(rb, [128, 3 * D // 2])
        rows, rtok, stage = carve(rb, [128, T]), carve(rb, [128, 3, 128]), carve(rb, [128, 6, 128])
        mx.close()

        h2T = sb("h2T", [128, KD, T])
        g2b, gfb = sb("g2b", [128, D]), sb("gfb", [128, D])
        rw = sb("rw", [128, KD, NE])
        rbias = sb("rbias", [128, NE])
        lg = sb("lg", [128, 3, NE])
        top = sb("top", [128, 3, 8])
        topi = sb("topi", [128, 3, 8], U32)
        topf = sb("topf", [128, 3, 8])
        gk = sb("gk", [128, 3, 8])
        msk, gts, tmp3 = sb("msk", [128, 3, NE]), sb("gts", [128, 3, NE]), sb("tmp3", [128, 3, NE])
        mskb = sb("mskb", [128, 3, NE], BF16)
        slot = sb("slot", [128, NPAIR + 1, 3, 2])
        sgate = sb("sgate", [128, NPAIR + 1, 3, 2])
        S = sb("S", [128, 3, 2, SLOTS])
        SG = sb("SG", [128, 3, 2, SLOTS])
        sgt = sb("sgt", [128, T])
        selb = sb("selb", [128, 2, SLOTS], BF16)
        xg = sb("xg", [128, KD, 128])
        aT = sb("aT", [128, 8, 128])
        gact, sg1, uact = sb("gact", [128, 2, 512]), sb("sg1", [128, 2, 512]), sb("uact", [128, 2, 512])
        yb = sb("yb", [128, 2, 512])

        sems = {}

        def sem(name):
            if name not in sems:
                sems[name] = ctx.enter_context(nc.semaphore(name))
            return sems[name]

        counted = {}

        def at(name, n):
            return (sem(SAID_BY.get(name)), VALUES[name][n - 1]) if name in VALUES else (sem(name), n)

        def says_now(name):
            if name not in VALUES:
                return sem(name)
            line = SAID_BY[name]
            for k in (name, line):
                counted[k] = counted.get(k, 0) + 1
            assert counted[line] == VALUES[name][counted[name] - 1], (line, name)
            return sem(line)

        filled = [sem(f"filled{b}") for b in range(8)]
        drained = [sem(f"drained{b}") for b in range(8)]

        def bank(name):
            return psum[:, FILLS[name][0], :]

        def await_fill(eng, name):
            eng.wait_ge(filled[FILLS[name][0]], FILLS[name][1] + 1)

        def await_bank(pe, name):
            if FILLS[name][1]:
                pe.wait_ge(drained[FILLS[name][0]], FILLS[name][1])

        def ends_fill(ins, name):
            ins.then_inc(filled[FILLS[name][0]], 1)

        def vec(name, k=None):
            r, n = VEC[name]
            return vecs[:, r:r + n] if k is None else vecs[:, r + k:r + k + 1]

        ctx.enter_context(nc.allow_non_contiguous_dma(reason="a few rows of single values"))
        block = ctx.enter_context(nc.Block())

        def w_in_cols(c0_, n):
            return a["w_in"][0][:, c0_:c0_ + n].rearrange("(k p) n -> p k n", p=128)

        def slot_view(s, n):
            return ring[:, s, 0:KD * n].rearrange("p (k n) -> p k n", k=KD)

        WCH = [(U0, 512), (GR0, 512), (1024, 512), (1536, 512), (2048, 512), (2560, 256)]
        BLOCKS = 6

        @block.sync
        def _(sp):
            def load_block(m, pair, which, static_free):
                for x in range(2):
                    s = 2 * (which % 3) + x
                    if which < 4:
                        n0 = [0, FF, 512, FF + 512][which]
                        dst = ring[:, s, :].rearrange("p (k n) -> p k n", k=KD)
                        src = a["exp_w1"][0][pair * 2 + x].rearrange("(k p) n -> p k n", p=128)[:, :, n0:n0 + 512]
                    else:
                        f0 = (which - 4) * 4
                        dst = ring[:, s, :].rearrange("p (k n) -> p k n", k=4)
                        src = a["exp_w2"][0][pair * 2 + x].rearrange("(k p) n -> p k n", p=128)[:, f0:f0 + 4, :]
                    sp.dma_start(dst, src).then_inc(sem(f"expert_chunk{s}"), 16)

            sp.dma_start(xn[:, 0:2, :], a["x_prompt"][0].rearrange("(i p) n -> p i n", p=128)).then_inc(sem("x_loaded"), 16)
            sp.dma_start(xn[0:TS, 2, :], a["x_sample"].rearrange("b t n -> (b t) n")).then_inc(sem("x_loaded"), 16)
            for c in range(6):
                if c == 1:
                    sp.wait_ge(*at("weights_zero", 1))
                    for x in range(2):
                        sp.dma_start(wgate[:, :, 32 * x:32 * x + H], w_in_cols(GI0 + H * x, H)).then_inc(sem("wgate_loaded"), 16)
                if c == 3:
                    for x, name in enumerate(("rg_wa", "rg_wx")):
                        for n in range(8):
                            q = slice(32 * (n % 4), 32 * (n % 4) + 32)
                            sp.dma_start(wax[q, x, n // 4, q], a[name][0, n]).then_inc(sem("wax_loaded"), 16)
                if c >= 3:
                    sp.wait_ge(*at("w_in_used", c - 2))
                sp.dma_start(slot_view(c % 3, WCH[c][1]), w_in_cols(*WCH[c])).then_inc(sem(f"w_in{c}"), 16)
            sp.wait_ge(*at("w_in_used", 6))
            for n in range(2):
                if n == 1:
                    sp.wait_ge(*at("s5_used", J5))
                sp.dma_start(slot_view(2 + n, 512), a["w_out"][0][:, n * 512:(n + 1) * 512].rearrange(
                    "(k p) n -> p k n", p=128)).then_inc(sem(f"w_out{n}"), 16)
            load_block(0, 0, 0, None)
            sp.wait_ge(*at("s5_turned", J5))
            for h in range(H):
                sp.dma_start(c0[:, h, :, 0:128], a["state_ml_c"][0, :, h].rearrange("b k v -> k b v")).then_inc(sem("c0_loaded"), 16)
            sp.wait_ge(*at("m_rows", 1))
            sp.dma_start(o[8].rearrange("l b h -> (l h) b"), gsm[0:H, 7, TP - 1:TP]).then_inc(sem("stored"), 16)
            sp.dma_start(o[15][0].rearrange("b h -> h b"), gsm[0:H, 7, TP + NT - 1:T:NT]).then_inc(sem("stored"), 16)
            for h in range(H):
                sp.wait_ge(*at("c_new", h + 1))
                sp.dma_start(o[13][0, :, h].rearrange("b k v -> k b v"), c0[:, h, :, 0:128]).then_inc(sem("stored"), 16)
            sp.wait_ge(*at("c_prompt", 2))
            sp.dma_start(o[6][0, 0].rearrange("h k v -> k h v"), cP[:, :, 0:128]).then_inc(sem("stored"), 16)
            sp.wait_ge(*at("n_staged", 1))
            sp.dma_start(o[14][0].rearrange("b h k -> (b h) k"), stage[0:32, 0, :]).then_inc(sem("stored"), 16)
            sp.dma_start(o[7][0, 0], stage[32:36, 0, :]).then_inc(sem("stored"), 16)
            sp.wait_ge(*at("rg_staged", 1))
            sp.dma_start(o[4][0, 0].rearrange("(a x n) -> a x n", a=1, x=2), stage[0:1, 1:3, :]).then_inc(sem("stored"), 16)
            sp.dma_start(o[11][0].rearrange("b (x n) -> b x n", x=2), stage[1:9, 1:3, :]).then_inc(sem("stored"), 16)
            sp.wait_ge(*at("rg_staged", 2))
            sp.dma_start(o[5][0, 0].rearrange("t (x n) -> t x n", x=2), stage[0:3, 3:5, :]).then_inc(sem("stored"), 16)
            sp.dma_start(o[12][0].rearrange("b t (x n) -> (b t) x n", x=2), stage[3:27, 3:5, :]).then_inc(sem("stored"), 16)
            for x in range(2):
                sp.wait_ge(*at("s5_staged", x + 1))
                src = stage[:, 5, :] if x == 0 else t_dve[:, 0:128]
                sp.dma_start(o[2 + x][0, 0].rearrange("(j g) p -> j (g p)", g=2), src[0:J5, :]).then_inc(sem("stored"), 16)
                sp.dma_start(o[9 + x][0].rearrange("b (j g) p -> (b j) (g p)", g=2), src[J5:9 * J5, :]).then_inc(sem("stored"), 16)
            sp.wait_ge(*at("y_turned", 1))
            sp.dma_start(x1[:, 0:2, :], a["x_prompt"][0].rearrange("(i p) n -> p i n", p=128)).then_inc(sem("x1_loaded"), 16)
            sp.dma_start(x1[0:TS, 2, :], a["x_sample"].rearrange("b t n -> (b t) n")).then_inc(sem("x1_loaded"), 16)
            stored = 16 * 17
            sp.wait_ge(sem("stored"), stored)
            sp.wait_ge(*at("mixer_done", 1))
            sp.dma_start(g2b[:], spread(a["norm2_g"][0:1, :], 0, 128)).then_inc(sem("router_loaded"), 16)
            sp.dma_start(rw[:], a["router_w"][0].rearrange("(k p) e -> p k e", p=128)).then_inc(sem("router_loaded"), 16)
            sp.dma_start(rbias[:], spread(a["router_b"][0:1, :], 0, 128)).then_inc(sem("router_loaded"), 16)
            load_block(2, 0, 2, None)
            sp.wait_ge(*at("w_out_used", 1))
            load_block(1, 0, 1, None)
            sp.dma_start(gfb[:], spread(a["final_norm_g"].rearrange("(a n) -> a n", a=1), 0, 128)).then_inc(sem("gf_loaded"), 16)
            for w in range(3, BLOCKS):
                sp.wait_ge(sem("block_done"), w - 2)
                load_block(w, 0, w, None)
            with sp.Fori(1, NPAIR) as p:
                for w in range(BLOCKS):
                    sp.wait_ge(sem("block_done"), p * BLOCKS + (w - 2))
                    load_block(None, p, w, None)
            sp.wait_ge(*at("count_ready", 1))
            most = sp.value_load(cnt[0:1, 0:1], min_val=0, max_val=T)
            with sp.Fori(1, SWEEPS) as r:
                with sp.If(most > r * SLOTS):
                    with sp.Fori(0, NPAIR) as p:
                        for w in range(BLOCKS):
                            sp.wait_ge(sem("block_done"), r * (NPAIR * BLOCKS) + p * BLOCKS + (w - 2))
                            load_block(None, p, w, None)
            sp.wait_ge(sem("y_final"), 3)
            sp.dma_start(o[0][0].rearrange("(i p) n -> p i n", p=128), x1[:, 0:2, :]).then_inc(sem("stored"), 16)
            sp.dma_start(o[1].rearrange("b t n -> (b t) n"), x1[0:TS, 2, :]).then_inc(sem("stored"), 16)
            sp.wait_ge(sem("stored"), stored + 32)

        @block.gpsimd
        def _(pool):
            n_self = [0]

            def po(ins, name=None):
                if name is None:
                    n_self[0] += 1
                    ins.then_inc(sem("pool_self"), 1)
                    pool.wait_ge(sem("pool_self"), n_self[0])
                else:
                    ins.then_inc(says_now(name), 1)

            g = nc.gpsimd
            po(g.memset(ident[:], 0.0))
            po(g.affine_select(out=ident[:], in_=ident[:], compare_op=ALU.not_equal, fill=1.0, base=0,
                               pattern=[[-1, 128]], channel_multiplier=1), "ident_ready")
            po(g.memset(wgate[:], 0.0))
            po(g.memset(wax[:], 0.0), "weights_zero")
            g.memset(BB[:], 0.0).then_inc(says_now("bb_zero"), 1)
            po(g.memset(seg[:], 1.0))
            po(g.memset(seg[:, 0:1], 0.0))
            po(g.memset(seg[:, TP:T:NT], 0.0), "seg_ready")
            po(g.memset(causal[:], 1.0))
            for c in (0, 256):
                po(g.affine_select(out=causal[:, c:c + 128], in_=causal[:, c:c + 128], compare_op=ALU.is_ge, fill=0.0,
                                   base=0, pattern=[[1, 128]], channel_multiplier=-1))
            po(g.affine_select(out=causal[:, 384:416], in_=causal[:, 384:416], compare_op=ALU.is_ge, fill=0.0,
                               base=0, pattern=[[1, TS]], channel_multiplier=-1))
            cs = causal[:, 384:416].rearrange("p (b t) -> p b t", b=NB)
            po(g.affine_select(out=cs, in_=cs, compare_op=ALU.is_ge, fill=0.0, base=0, pattern=[[-NT, NB], [0, NT]],
                               channel_multiplier=1), "causal_ready")
            po(g.memset(sel4[:], 0.0))
            po(g.affine_select(out=sel4[:], in_=sel4[:], compare_op=ALU.not_equal, fill=1.0, base=0,
                               pattern=[[-1, H], [0, 128]], channel_multiplier=1), "sel4_ready")
            po(g.memset(scm[:], 0.0))
            po(g.memset(wsm[:], 1.0))
            po(g.affine_select(out=wsm[:], in_=wsm[:], compare_op=ALU.is_ge, fill=0.0, base=0,
                               pattern=[[0, H], [-NT, NB]], channel_multiplier=1))
            po(g.affine_select(out=wsm[:], in_=wsm[:], compare_op=ALU.is_ge, fill=0.0, base=NT - 1,
                               pattern=[[0, H], [NT, NB]], channel_multiplier=-1), "ind_ready")
            pool.wait_ge(*at("xn_used", 1))
            po(g.memset(rows[:], 0.0), "rows_zero")
            pool.wait_ge(*at("angle_ready", 2))
            po(g.memset(tab_r[:, :, 0:1], 1.0))
            po(g.memset(tab_i[:, :, 0:1], 0.0))
            po(g.tensor_copy(tab_r[:, :, 1:2], sm[:, 6, :].unsqueeze(2)))
            po(g.tensor_copy(tab_i[:, :, 1:2], sm[:, 7, :].unsqueeze(2)))
            pr, pi, q1, q2, q3 = sm[:, 20, :], sm[:, 21, :], sm[:, 22, :], sm[:, 23, :], sm[:, 24, :]
            po(g.tensor_copy(pr, sm[:, 6, :]))
            po(g.tensor_copy(pi, sm[:, 7, :]))
            n = 2
            while n < TP:
                po(g.tensor_tensor(q1, pr, pr, ALU.mult))
                po(g.tensor_tensor(q2, pi, pi, ALU.mult))
                po(g.tensor_tensor(q3, pr, pi, ALU.mult))
                po(g.tensor_tensor(pr, q1, q2, ALU.subtract))
                po(g.tensor_tensor(pi, q3, q3, ALU.add))
                prb, pib = (spread(v.unsqueeze(2), 2, n) for v in (pr, pi))
                po(g.tensor_tensor(pt1[:, :, 0:n], tab_r[:, :, 0:n], prb, ALU.mult))
                po(g.tensor_tensor(pt2[:, :, 0:n], tab_i[:, :, 0:n], pib, ALU.mult))
                po(g.tensor_tensor(tab_r[:, :, n:2 * n], pt1[:, :, 0:n], pt2[:, :, 0:n], ALU.subtract))
                po(g.tensor_tensor(pt1[:, :, 0:n], tab_r[:, :, 0:n], pib, ALU.mult))
                po(g.tensor_tensor(pt2[:, :, 0:n], tab_i[:, :, 0:n], prb, ALU.mult))
                po(g.tensor_tensor(tab_i[:, :, n:2 * n], pt1[:, :, 0:n], pt2[:, :, 0:n], ALU.add))
                n *= 2
            for k, tb in enumerate((tab_r, tab_i)):
                for j in range(J5):
                    ins = g.tensor_copy(tb[:, j, TP:T].rearrange("p (b t) -> p b t", b=NB),
                                        spread(tb[:, j, 0:NT].unsqueeze(1), 1, NB))
            po(ins, "table_ready")
            pool.wait_ge(*at("table_ready", 1))
            po(g.memset(E[:], 0.0), "e_zero")
            for j in range(J5):
                pool.wait_ge(*at("s5_scanned", j + 1))
                if j >= 2:
                    pool.wait_ge(*at("s5_used", j - 1))
                b = j % 2
                po(g.tensor_tensor(s_r[:, b, :], tab_r[:, j, :], w_r[:, b, :], ALU.mult))
                po(g.tensor_tensor(t_pool[:], tab_i[:, j, :], w_i[:, b, :], ALU.mult))
                po(g.tensor_tensor(s_r[:, b, :], s_r[:, b, :], t_pool[:], ALU.subtract))
                po(g.tensor_tensor(s_i[:, b, :], tab_i[:, j, :], w_r[:, b, :], ALU.mult))
                po(g.tensor_tensor(t_pool[:], tab_r[:, j, :], w_i[:, b, :], ALU.mult))
                po(g.tensor_tensor(s_i[:, b, :], s_i[:, b, :], t_pool[:], ALU.add))
                for x, s in enumerate((s_r, s_i)):
                    g.tensor_copy(fin5[:, x, 0, j:j + 1], s[:, b, TP - 1:TP])
                    ins = g.tensor_copy(fin5[:, x, 1:, j:j + 1], s[:, b, TP + NT - 1:T:NT].unsqueeze(2))
                po(ins, "s5_turned")
            pool.wait_ge(*at("wsm_ready", 1))
            pool.wait_ge(*at("v_ready", 1))
            pool.wait_ge(*at("s5_turned", J5))
            for h in range(H):
                if h >= 2:
                    pool.wait_ge(*at("vw_used", h - 1))
                po(g.tensor_tensor(vw[:, h % 2], spread(v_tok[0:TS, 2, h, :].unsqueeze(1), 1, NB),
                                   spread(wsm[:, h, :].unsqueeze(2), 2, 129), ALU.mult), "vw_ready")
                if h == 1:
                    pool.wait_ge(*at("c0_used", 1))
                    pool.wait_ge(*at("dec_ready", 1))
                    for hh in range(H):
                        g.tensor_tensor(c0[:, hh], c0[:, hh], spread(dec[:, hh, :].unsqueeze(2), 2, 129),
                                        ALU.mult).then_inc(says_now("c_decayed"), 1)
            bias_cols = [[("exp_b1", 0, 1536, 0)], [("exp_b1", 1536, 512, 0), ("exp_b2", 0, 1024, 512)]]

            def load_bias(part):
                for x in range(3):
                    for name, c_, n_, at_ in bias_cols[part]:
                        pool.dma_start(bias_in[32 * x:32 * x + 32, at_:at_ + n_], a[name][0][:, c_:c_ + n_]).then_inc(sem("bias_loaded"), 16)

            load_bias(0)
            po(g.iota(iota_e[:], pattern=[[1, NE]], base=0, channel_multiplier=0, allow_small_or_imprecise_dtypes=True))
            po(g.iota(iota_s[:], pattern=[[1, SLOTS]], base=0, channel_multiplier=0, allow_small_or_imprecise_dtypes=True))
            po(g.iota(half[:], pattern=[[1, 2], [0, SLOTS]], base=0, channel_multiplier=0, allow_small_or_imprecise_dtypes=True))
            for x in range(3):
                po(g.iota(selid[32 * x:32 * x + 32, :], pattern=[[-2, NPAIR + 1]], base=0, channel_multiplier=1,
                          allow_small_or_imprecise_dtypes=True))
            po(g.memset(ones_bf[:], 1.0))
            po(g.affine_select(out=upper[:], in_=ones_bf[:], compare_op=ALU.is_ge, fill=0.0, base=0,
                               pattern=[[1, 128]], channel_multiplier=-1))
            for part in range(2):
                bs = bsplit[:, 1536 * part:1536 * part + 1536]
                if part:
                    load_bias(1)
                pool.wait_ge(sem("bias_loaded"), 48 + 96 * part)
                po(g.tensor_copy(bs[0:96], bias_in[0:96]))
                po(g.tensor_tensor(bias_in[0:96], bias_in[0:96], bs[0:96], ALU.subtract))
                po(g.tensor_copy(bs[32:64], bias_in[32:64]))
                po(g.tensor_copy(bs[64:96], bias_in[64:96]))
                po(g.tensor_tensor(bias_in[64:96], bias_in[64:96], bs[64:96], ALU.subtract))
                ins = g.tensor_copy(bs[64:96], bias_in[64:96])
                po(ins) if part == 0 else po(ins, "bias_ready")
            pool.wait_ge(*at("rg_used", 1))
            pool.wait_ge(*at("bias_ready", 1))
            g.memset(acc[:], 0.0).then_inc(says_now("acc_zero"), 1)

        @block.scalar
        def _(act):
            A = nc.scalar.activation

            def copy_out(name, out, view, scale=1.0, signal=None):
                await_fill(act, name)
                nc.scalar.activation(out, view, ACT.Copy, scale=scale).then_inc(drained[FILLS[name][0]], 1)

            for name, src in (("norm1_g", a["norm1_g"]), ("s5_d", a["s5_d"]), ("s5_glu_b", a["s5_glu_b"]),
                              ("rg_conv_b", a["rg_conv_b"]), ("rg_ba", a["rg_ba"]), ("rg_bx", a["rg_bx"]),
                              ("rg_lambda", a["rg_lambda"]), ("ml_norm_g", a["ml_norm_g"])):
                r, n = VEC[name]
                act.dma_start(vrow[r:r + n, :], src[0].rearrange("(k p) -> k p", p=128)).then_inc(sem("vec_loaded"), 16)
            r, n = VEC["rg_conv_w"]
            act.dma_start(vrow[r:r + n, :], a["rg_conv_w"][0].rearrange("t (k p) -> (t k) p", p=128)).then_inc(sem("vec_loaded"), 16)
            for name in ("s5_lambda_re", "s5_lambda_im"):
                r, n = VEC[name]
                act.dma_start(vrow[r:r + n, :], a[name][0].rearrange("(j g) p -> j (g p)", g=2)).then_inc(sem("vec_loaded"), 16)
            for x, name in enumerate(("s5_b_re", "s5_b_im")):
                for gg in range(2):
                    act.dma_start(b_in[64 * gg:64 * gg + 64, x], a[name][0].rearrange("(j g) p c -> g p j c", g=2)[gg]).then_inc(sem("b_loaded"), 16)
            for gg in range(2):
                act.dma_start(sm[64 * gg:64 * gg + 64, 0, :], spread(a["s5_log_step"][0:1].rearrange("l (j g) -> l g j", g=2)[:, gg, :], 0, 64)).then_inc(sem("step_loaded"), 16)
            for x, name in enumerate(("s5_c_re", "s5_c_im")):
                for tt in range(2):
                    act.dma_start(c_in[:, 2 * x + tt, :], a[name][0, 8 * tt:8 * tt + 8].rearrange("g c p -> (g c) p")).then_inc(sem("c_loaded"), 16)
            for x, name in enumerate(("state_s5_re", "state_s5_im")):
                act.dma_start(srow[64 * x:64 * x + 64, :], a[name][0].rearrange("b (j g) p -> (b j) (g p)", g=2)).then_inc(sem("par_loaded"), 16)
            act.dma_start(prow[0:32, :], a["state_ml_n"][0].rearrange("b h k -> (b h) k")).then_inc(sem("par_loaded"), 16)
            act.dma_start(prow[32:48, :], a["state_rg_h"][0].rearrange("b (x n) -> (b x) n", x=2)).then_inc(sem("par_loaded"), 16)
            act.dma_start(prow[48:96, :], a["state_rg_conv"][0].rearrange("b t (x n) -> (b t x) n", x=2)).then_inc(sem("par_loaded"), 16)
            act.dma_start(gb[:], a["ml_gate_bias"][0].rearrange("(x h) -> h x", x=2)).then_inc(sem("gb_loaded"), 16)
            act.dma_start(m0[:], a["state_ml_m"][0].rearrange("b h -> h b")).then_inc(sem("gb_loaded"), 16)
            act.dma_start(glw[:], a["s5_glu_w"][0].rearrange("(k p) n -> p k n", p=128)).then_inc(sem("glw_loaded"), 16)
            act.wait_ge(sem("x_loaded"), 32)
            act.wait_ge(*at("nst_set", 1))
            for i, (t0, n) in enumerate(TILES):
                A(x1[0:n, i, :], xn[0:n, i, :], ACT.Square, accum_out=nst[0:n, i:i + 1]).then_inc(says_now("ms_ready"), 1)
            act.wait_ge(*at("var_ready", 1))
            A(nst[:, 4:7], nst[:, 4:7], ACT.Sqrt).then_inc(says_now("root_ready"), 1)
            await_fill(act, "vec")
            A(vecs[:, 0:NVEC], bank("vec")[:, 0:NVEC], ACT.Copy).then_inc(drained[FILLS["vec"][0]], 1)
            act.wait_ge(drained[FILLS["vec"][0]], 1)
            act.wait_ge(sem("step_loaded"), 32)
            A(sm[:, 1, :], sm[:, 0, :], ACT.Exp).then_inc(says_now("step_ready"), 1)
            act.wait_ge(*at("angle_reduced", 1))
            A(sm[:, 5, :], sm[:, 2, :], ACT.Exp).then_inc(says_now("mag_ready"), 1)
            A(rsm[:, 0:2], vec("rg_lambda"), ACT.Abs).then_inc(says_now("act_rg"), 1)
            act.wait_ge(*at("act_rg", 1))
            A(rsm[:, 0:2], rsm[:, 0:2], ACT.Exp, scale=-1.0).then_inc(says_now("act_rg"), 1)
            A(sm[:, 6, :], sm[:, 9, :], ACT.Sin).then_inc(says_now("angle_ready"), 1)
            A(sm[:, 7, :], sm[:, 8, :], ACT.Sin).then_inc(says_now("angle_ready"), 1)
            for x in range(2):
                copy_out(f"u{x}", uT[:, x, :], bank(f"u{x}")[:, 0:T])
            act.wait_ge(*at("gate_abs", 1))
            A(gsm[0:H, 2, :], gsm[0:H, 2, :], ACT.Exp, scale=-1.0).then_inc(says_now("gate_exp"), 1)
            for x in range(2):
                await_fill(act, f"xr{x}")
                A(xpP[:, x, 3:], bank(f"xr{x}")[:, 0:TP], ACT.Copy).then_inc(says_now("xp_ready"), 1)
                A(xpS[:, x, :, 3:], bank(f"xr{x}")[:, TP:T].rearrange("p (b t) -> p b t", b=NB), ACT.Copy).then_inc(drained[FILLS[f"xr{x}"][0]], 1)
            copy_out("par", parT[:, 0:224], bank("par")[:, 0:224])
            copy_out("bt", wB[:], bank("bt").rearrange("p (x n) -> p x n", x=4))
            await_fill(act, "ct")
            A(wC[:, 0:2, :], bank("ct")[:, 0:256].rearrange("p (x n) -> p x n", x=2), ACT.Copy).then_inc(says_now("wc_ready"), 1)
            A(wC[:, 2:4, :], bank("ct")[:, 256:512].rearrange("p (x n) -> p x n", x=2), ACT.Copy, scale=-1.0).then_inc(drained[FILLS["ct"][0]], 1)
            for x in range(2):
                copy_out(f"gr{x}", gate[:, x, :], bank(f"gr{x}")[:, 0:T])
            for h in range(2):
                copy_out(f"q{h}", qT[:, h, :], bank(f"q{h}")[:, 0:T])
            act.wait_ge(*at("gate_rows", 1))
            act.wait_ge(*at("rows_zero", 1))
            A(rows[32:32 + H, :], gsm[0:H, 7, :], ACT.Exp, scale=-1.0).then_inc(says_now("gate_rows_exp"), 1)
            A(rows[64:64 + H, :], gsm[0:H, 5, :], ACT.Exp).then_inc(says_now("gate_rows_exp"), 1)
            A(gsm[0:H, 6, 0:TS + NB], gsm[0:H, 6, 0:TS + NB], ACT.Exp).then_inc(says_now("gate_rows_exp"), 1)
            for h in range(2, H):
                copy_out(f"q{h}", qT[:, h, :], bank(f"q{h}")[:, 0:T])
            for h in range(2):
                copy_out(f"k{h}", kT[:, h, :], bank(f"k{h}")[:, 0:T], scale=DK ** -0.5)
            for x in range(2):
                await_fill(act, f"r{x}")
                A(rr[:, x, :], bank(f"r{x}")[:, 0:T], ACT.Sigmoid, bias=vec("rg_ba", x)).then_inc(drained[FILLS[f"r{x}"][0]], 1)
            for x in range(2):
                await_fill(act, f"i{x}")
                A(ri[:, x, :], bank(f"i{x}")[:, 0:T], ACT.Sigmoid, bias=vec("rg_bx", x)).then_inc(drained[FILLS[f"i{x}"][0]], 1)
            for h in range(2, H):
                copy_out(f"k{h}", kT[:, h, :], bank(f"k{h}")[:, 0:T], scale=DK ** -0.5)

            def v_out(name, i, n, c):
                await_fill(act, name)
                A(v_tok[0:n, i, 2 * c:2 * c + 2, 0:128], bank(name)[0:n, 0:256].rearrange("p (h v) -> p h v", h=2), ACT.Copy).then_inc(
                    drained[FILLS[name][0]], 1)

            def o_out(name, i, n, c):
                await_fill(act, name)
                A(o_tok[0:n, i, 256 * c:256 * c + 256], bank(name)[0:n, 0:256], ACT.Sigmoid).then_inc(drained[FILLS[name][0]], 1)

            for i, (t0, n) in enumerate(TILES):
                v_out(f"va{i}", i, n, 0)
            act.wait_ge(*at("rg_decay", 1))
            for x in range(2):
                act.wait_ge(drained[FILLS["r1"][0]], FILLS["r1"][1] + 1)
                act.wait_ge(drained[FILLS["r0"][0]], FILLS["r0"][1] + 1)
                A(rt[:, x, :], rr[:, x, :], ACT.Tanh, scale=rsm[:, 4 + x:5 + x]).then_inc(says_now("rg_tanh"), 1)
            act.wait_ge(*at("rg_tanh", 2))
            for x in range(2):
                A(rr[:, x, :], rr[:, x, :], ACT.Exp, scale=rsm[:, 6 + x:7 + x]).then_inc(says_now("rg_a"), 1)
            for i, (t0, n) in enumerate(TILES):
                v_out(f"vb{i}", i, n, 1)
            act.wait_ge(*at("rg_ratio", 1))
            A(rt[:], rt[:], ACT.Sqrt).then_inc(says_now("rg_root"), 1)
            for i, (t0, n) in enumerate(TILES):
                o_out(f"oa{i}", i, n, 0)
            act.wait_ge(*at("gate_poly", 1))
            A(rt[:], rt[:], ACT.Tanh, scale=math.sqrt(2.0 / math.pi)).then_inc(says_now("gate_tanh"), 1)
            for i, (t0, n) in enumerate(TILES):
                o_out(f"ob{i}", i, n, 1)
            act.wait_ge(*at("ones_ready", 1))
            await_fill(act, "rows")
            A(rtok[:, 0:2, :], bank("rows")[:, 0:256].rearrange("p (i n) -> p i n", i=2), ACT.Copy).then_inc(says_now("rtok_ready"), 1)
            A(rtok[0:TS, 2, :], bank("rows")[0:TS, 256:384], ACT.Copy).then_inc(drained[FILLS["rows"][0]], 1)
            for i, (t0, n) in enumerate(TILES):
                copy_out(f"kt{i}", k_tok[0:n, i, :], bank(f"kt{i}")[0:n, :])
            for h in range(H):
                act.wait_ge(*at("e_arg", h + 1))
                A(E[:, h, :], E[:, h, :], ACT.Exp, scale=-1.0).then_inc(says_now("e_exp"), 1)
            copy_out("dec", dec[:], bank("dec")[:, 0:H * NB].rearrange("p (h b) -> p h b", h=H))
            for k, i in enumerate((2, 0, 1)):
                n = TILES[i][1]
                act.wait_ge(*at("den_read", k + 1))
                for hh in range(2):
                    await_fill(act, f"nu{i}{hh}")
                    if hh:
                        act.wait_ge(*at("nsq_ready", 4 * k + 2))
                    for x in range(2):
                        A(t_dve[0:n, 128 * x:128 * x + 128], bank(f"nu{i}{hh}")[0:n, 129 * x:129 * x + 128], ACT.Square,
                          accum_out=rsm[0:n, 16 + 4 * i + 2 * hh + x:17 + 4 * i + 2 * hh + x]).then_inc(says_now("nsq_ready"), 1)
                act.wait_ge(*at("nvar_ready", k + 1))
                A(rsm[0:n, 32 + 4 * i:36 + 4 * i], rsm[0:n, 32 + 4 * i:36 + 4 * i], ACT.Sqrt).then_inc(says_now("nroot_ready"), 1)
            act.wait_ge(*at("s5_poly", 1))
            A(rt[:], rt[:], ACT.Tanh, scale=math.sqrt(2.0 / math.pi)).then_inc(says_now("s5_tanh"), 1)
            for x in range(2):
                await_fill(act, f"glu{x}")
                A(ri[:, x, :], bank(f"glu{x}")[:, 0:T], ACT.Sigmoid, bias=vec("s5_glu_b", x)).then_inc(drained[FILLS[f"glu{x}"][0]], 1)
            for hh in range(2):
                await_fill(act, f"cp{hh}")
                A(cP[:, 2 * hh:2 * hh + 2, :], bank(f"cp{hh}")[:, 0:258].rearrange("p (h v) -> p h v", h=2), ACT.Copy).then_inc(drained[FILLS[f"cp{hh}"][0]], 1)
            act.wait_ge(drained[FILLS["cp0"][0]], FILLS["cp0"][1] + 1)
            act.wait_ge(drained[FILLS["cp1"][0]], FILLS["cp1"][1] + 1)
            for hh in range(2):
                A(nbuf[:, 32 + 2 * hh:34 + 2 * hh], cP[:, 2 * hh:2 * hh + 2, 128], ACT.Copy).then_inc(says_now("c_prompt"), 1)
            await_fill(act, "nT")
            A(stage[0:36, 0, :], bank("nT")[0:36, 0:128], ACT.Copy).then_inc(says_now("n_staged"), 1)
            act.wait_ge(*at("n_staged", 1))
            act.sem_inc(drained[FILLS["nT"][0]], 1)
            await_fill(act, "rgT")
            A(stage[0:9, 1:3, :], bank("rgT")[0:9, 0:256].rearrange("p (x n) -> p x n", x=2), ACT.Copy).then_inc(says_now("rg_staged"), 1)
            A(stage[0:27, 3:5, :], bank("rgT")[0:27, 256:512].rearrange("p (x n) -> p x n", x=2), ACT.Copy).then_inc(says_now("rg_staged"), 1)
            act.wait_ge(*at("rg_staged", 2))
            act.sem_inc(drained[FILLS["rgT"][0]], 1)
            await_fill(act, "s5T")
            A(stage[0:72, 5, :], bank("s5T")[0:72, 0:128], ACT.Copy).then_inc(says_now("s5_staged"), 1)
            A(t_dve[0:72, 0:128], bank("s5T")[0:72, 128:256], ACT.Copy).then_inc(says_now("s5_staged"), 1)
            act.wait_ge(*at("s5_staged", 2))
            act.sem_inc(drained[FILLS["s5T"][0]], 1)
            for h in range(H):
                await_fill(act, f"yT{h}")
                A(hT[:, 4 + h, :], bank(f"yT{h}")[:, 0:T], ACT.Copy, scale=vec("ml_norm_g", h)).then_inc(drained[FILLS[f"yT{h}"][0]], 1)
            for i, (t0, n) in enumerate(TILES):
                act.wait_ge(*at("x1_added", 2 * i + 2))
                if i == 0:
                    act.wait_ge(*at("bias_ready", 1))
                A(xn[0:n, i, :], x1[0:n, i, :], ACT.Square, accum_out=st2[0:n, i:i + 1]).then_inc(says_now("ms2_ready"), 1)
            act.wait_ge(*at("var2_ready", 1))
            A(st2[:, 4:7], st2[:, 4:7], ACT.Sqrt).then_inc(says_now("root2_ready"), 1)
            for k in range(6):
                i, hf = k // 2, k % 2
                t0, n = TILES[i]
                copy_out(f"h2T{k}", h2T[:, 4 * hf:4 * hf + 4, t0:t0 + n],
                         bank(f"h2T{k}")[:, 0:4 * 128].rearrange("p (k n) -> p k n", k=4)[:, :, 0:n])
            act.wait_ge(*at("top_diff", 1))
            A(gk[:, :, 0:TOPK], gk[:, :, 0:TOPK], ACT.Exp).then_inc(says_now("top_exp"), 1)

            def gathered(g1):
                for x in range(2):
                    act.wait_ge(sem("gather_ready"), g1 * 2 - 1 + x)
                    A(xg[:, 4 * x:4 * x + 4, :], psum[:, 6 + x, :].rearrange("p (k n) -> p k n", k=4), ACT.Copy).then_inc(sem("xg_copied"), 1)

            def sweep(base):
                with act.Fori(0, NPAIR) as p:
                    gp = base + p
                    for x in range(2):
                        act.wait_ge(sem("g_clipped"), gp * 2 + 1 + x)
                        A(sg1[:, x, :], gact[:, x, :], ACT.Sigmoid, scale=1.702).then_inc(sem("sig_ready"), 1)
                    gathered_at = gp * 2 + 2
                    for x in range(2):
                        act.wait_ge(sem("gather_ready"), gathered_at + 1 + x)
                        A(xg[:, 4 * x:4 * x + 4, :], psum[:, 6 + x, :].rearrange("p (k n) -> p k n", k=4), ACT.Copy).then_inc(sem("xg_copied"), 1)
                    for x in range(2):
                        act.wait_ge(sem("aT_ready"), gp * 2 + 1 + x)
                        A(aT[:, 4 * x:4 * x + 4, :], psum[:, x, :].rearrange("p (k n) -> p k n", k=4), ACT.Copy).then_inc(sem("aT_copied"), 1)
                    act.wait_ge(sem("sgt_ready"), gp + 1)
                    A(sgt[:], psum[:, 6, 0:T], ACT.Copy).then_inc(sem("sgt_copied"), 1)
                    act.wait_ge(sem("block_done"), gp * BLOCKS + 6)
                    for x in range(2):
                        A(yb[:, x, :], psum[:, 4 + x, :], ACT.Copy).then_inc(sem("y_copied"), 1)

            gathered(1)
            sweep(0)
            act.wait_ge(*at("count_ready", 1))
            most = act.value_load(cnt[0:1, 0:1], min_val=0, max_val=T)
            with act.Fori(1, SWEEPS) as r:
                with act.If(most > r * SLOTS):
                    g1 = r * (NPAIR + 1)
                    for x in range(2):
                        act.wait_ge(sem("regather_ready"), r * 2 - 1 + x)
                        A(xg[:, 4 * x:4 * x + 4, :], psum[:, 6 + x, :].rearrange("p (k n) -> p k n", k=4), ACT.Copy).then_inc(sem("xg_recopied"), 1)
                    sweep(r * NPAIR)
            act.wait_ge(sem("x2_added"), 1)
            for i, (t0, n) in enumerate(TILES):
                A(xn[0:n, i, :], x1[0:n, i, :], ACT.Square, accum_out=st2[0:n, i:i + 1]).then_inc(sem("ms3_ready"), 1)
            act.wait_ge(sem("var3_ready"), 1)
            A(st2[:, 4:7], st2[:, 4:7], ACT.Sqrt).then_inc(sem("root3_ready"), 1)

        @block.vector
        def _(dve):
            n_self = [0]
            V = nc.vector

            def dv(ins, s=None, value=None):
                if s is None:
                    n_self[0] += 1
                    ins.then_inc(sem("dve_self"), 1)
                    dve.wait_ge(sem("dve_self"), n_self[0])
                else:
                    ins.then_inc(s, 1)

            def drains(ins, name):
                b, n = FILLS[name]
                ins.then_inc(drained[b], 1)
                dve.wait_ge(drained[b], n + 1)

            def says(ins, name, n):
                ins.then_inc(says_now(name), 1)
                dve.wait_ge(*at(name, n))

            TT, TSC, STT = V.tensor_tensor, V.tensor_scalar, V.scalar_tensor_tensor

            def log1p(out, y, tmp1, tmp2):
                dv(TSC(tmp1, y, 2.0, None, ALU.add))
                dv(V.reciprocal(tmp1, tmp1))
                dv(TT(tmp1, tmp1, y, ALU.mult))
                dv(TT(tmp2, tmp1, tmp1, ALU.mult))
                dv(TSC(out, tmp2, 1.0 / 19.0, None, ALU.mult))
                for k in range(8, 0, -1):
                    dv(STT(out=out, in0=out, scalar=1.0 / (2 * k + 1), in1=tmp2, op0=ALU.add, op1=ALU.mult))
                dv(STT(out=out, in0=out, scalar=1.0, in1=tmp1, op0=ALU.add, op1=ALU.mult))
                dv(TSC(out, out, 2.0, None, ALU.mult))

            dv(V.memset(st2[:], 1.0))
            says(V.memset(nst[:], 1.0), "nst_set", 1)
            dve.wait_ge(*at("ms_ready", 3))
            says(TSC(nst[:, 4:7], nst[:, 0:3], 1.0 / D, EPS, ALU.mult, ALU.add), "var_ready", 1)
            dve.wait_ge(*at("root_ready", 1))
            dv(V.reciprocal(nst[:, 4:7], nst[:, 4:7]))
            for i, (t0, n) in enumerate(TILES):
                says(TSC(xn[0:n, i, :], xn[0:n, i, :], nst[0:n, 4 + i:5 + i], None, ALU.mult), "xn_ready", i + 1)
            dve.wait_ge(drained[FILLS["vec"][0]], 1)
            for k in range(6):
                i, hf = k // 2, k % 2
                t0, n = TILES[i]
                await_fill(dve, f"hT{k}")
                drains(TT(hT[:, 4 * hf:4 * hf + 4, t0:t0 + n], bank(f"hT{k}").rearrange("p (k n) -> p k n", k=4)[:, :, 0:n],
                          spread(vec("norm1_g")[:, 4 * hf:4 * hf + 4].unsqueeze(2), 2, n), ALU.mult), f"hT{k}")
            lr, li = vec("s5_lambda_re"), vec("s5_lambda_im")
            dve.wait_ge(*at("step_ready", 1))
            dv(TT(sm[:, 2, :], lr, sm[:, 1, :], ALU.mult))
            dv(TT(sm[:, 3, :], li, sm[:, 1, :], ALU.mult))
            magic = 12582912.0
            dv(TSC(sm[:, 4, :], sm[:, 3, :], 1.0 / (2 * math.pi), None, ALU.mult))
            dv(TSC(sm[:, 4, :], sm[:, 4, :], magic, None, ALU.add))
            dv(TSC(sm[:, 4, :], sm[:, 4, :], magic, None, ALU.subtract))
            p1, p2 = 6.28125, 0.0019350051879882812
            p3 = 2 * math.pi - p1 - p2
            dv(STT(out=sm[:, 8, :], in0=sm[:, 4, :], scalar=-p1, in1=sm[:, 3, :], op0=ALU.mult, op1=ALU.add))
            dv(STT(out=sm[:, 8, :], in0=sm[:, 4, :], scalar=-p2, in1=sm[:, 8, :], op0=ALU.mult, op1=ALU.add))
            dv(STT(out=sm[:, 8, :], in0=sm[:, 4, :], scalar=-p3, in1=sm[:, 8, :], op0=ALU.mult, op1=ALU.add))
            dv(TSC(sm[:, 8, :], sm[:, 8, :], 3.1415925, -3.1415925, ALU.min, ALU.max))
            dv(STT(out=sm[:, 9, :], in0=sm[:, 8, :], scalar=-1.0, in1=sm[:, 8, :], op0=ALU.mult, op1=ALU.min))
            says(TSC(sm[:, 9, :], sm[:, 9, :], math.pi / 2, None, ALU.add), "angle_reduced", 1)
            dve.wait_ge(*at("mag_ready", 1))
            dve.wait_ge(*at("angle_ready", 2))
            mag = sm[:, 5, :]
            dv(TT(sm[:, 10, :], mag, sm[:, 6, :], ALU.mult))
            dv(TT(sm[:, 11, :], mag, sm[:, 7, :], ALU.mult))
            dv(TT(sm[:, 14, :], lr, lr, ALU.mult))
            dv(TT(sm[:, 15, :], li, li, ALU.mult))
            dv(TT(sm[:, 14, :], sm[:, 14, :], sm[:, 15, :], ALU.add))
            dv(V.reciprocal(sm[:, 14, :], sm[:, 14, :]))
            dv(TSC(sm[:, 15, :], sm[:, 10, :], -1.0, None, ALU.add))
            dv(TT(sm[:, 16, :], sm[:, 15, :], lr, ALU.mult))
            dv(TT(sm[:, 17, :], sm[:, 11, :], li, ALU.mult))
            dv(TT(sm[:, 12, :], sm[:, 16, :], sm[:, 17, :], ALU.add))
            dv(TT(sm[:, 12, :], sm[:, 12, :], sm[:, 14, :], ALU.mult))
            dv(TT(sm[:, 16, :], sm[:, 11, :], lr, ALU.mult))
            dv(TT(sm[:, 17, :], sm[:, 15, :], li, ALU.mult))
            dv(TT(sm[:, 13, :], sm[:, 16, :], sm[:, 17, :], ALU.subtract))
            dv(TT(sm[:, 13, :], sm[:, 13, :], sm[:, 14, :], ALU.mult))
            dve.wait_ge(sem("b_loaded"), 64)
            dve.wait_ge(*at("bb_zero", 1))
            zr, zi = (spread(sm[:, k, :].unsqueeze(2), 2, C5) for k in (12, 13))
            for x, (za, zb, op) in enumerate(((zr, zi, ALU.subtract), (zi, zr, ALU.add))):
                dv(TT(b_t[:, 0], b_in[:, 0], za, ALU.mult))
                dv(TT(b_t[:, 1], b_in[:, 1], zb, ALU.mult))
                for gg in range(2):
                    q = slice(64 * gg, 64 * gg + 64)
                    says(TT(BB[q, x * J5:(x + 1) * J5, gg, :], b_t[q, 0], b_t[q, 1], op), "bb_ready", 2 * x + gg + 1)
            dve.wait_ge(sem("c_loaded"), 64)
            par_i = cvfin[:, 0, 0:2].bitcast(I32)
            dv(V.tensor_reduce(cvfin[:, 1, 0:1], ident[:], AX.X, ALU.add))
            for gg in range(2):
                dv(V.tensor_reduce(rsm[:, 10 + gg:11 + gg],
                                   ident[:].rearrange("p (j g c) -> p g j c", g=2, c=C5)[:, gg], AX.XY, ALU.add))
            for gg in range(2):
                says(TSC(CBk[:, :, 64 * gg:64 * gg + 64], c_in[:], rsm[:, 10 + gg:11 + gg], None, ALU.mult), "cb_ready", gg + 1)
            ig, fg, ge, s3, s4, wd, sd, mt = (gsm[0:H, k, :] for k in range(8))
            dve.wait_ge(sem("gb_loaded"), 32)
            await_fill(dve, "gates")
            dv(TSC(ig, bank("gates")[0:H, 0:T], gb[:, 0:1], None, ALU.add))
            drains(V.tensor_copy(fg, bank("gates")[32:32 + H, 0:T]), "gates")
            dv(TSC(fg, fg, gb[:, 1:2], None, ALU.add))
            says(STT(out=ge, in0=fg, scalar=-1.0, in1=fg, op0=ALU.mult, op1=ALU.max), "gate_abs", 1)
            dve.wait_ge(*at("act_rg", 2))
            log1p(rsm[:, 2:4], rsm[:, 0:2], rsm[:, 8:10], rsm[:, 12:14])
            dv(TSC(rsm[:, 8:10], vec("rg_lambda"), -1.0, 0.0, ALU.mult, ALU.max))
            dv(TT(rsm[:, 2:4], rsm[:, 2:4], rsm[:, 8:10], ALU.add))
            dv(TSC(rsm[:, 4:6], rsm[:, 2:4], RC, None, ALU.mult))
            says(TSC(rsm[:, 6:8], rsm[:, 2:4], -RC, None, ALU.mult), "rg_decay", 1)
            dve.wait_ge(*at("gate_exp", 1))
            log1p(s3, ge, s4, wd)
            dv(TSC(fg, fg, 0.0, None, ALU.min))
            dv(TT(fg, fg, s3, ALU.subtract))
            dve.wait_ge(*at("seg_ready", 1))
            dve.wait_ge(*at("rows_zero", 1))
            bb, aa, mm = s3, rows[0:H, :], s4
            dv(V.tensor_tensor_scan(bb, seg[0:H, :], fg, 0.0, ALU.mult, ALU.add))
            dv(TT(aa, ig, bb, ALU.subtract))
            dv(V.tensor_tensor_scan(mm[:, 0:TP], aa[:, 0:TP], aa[:, 0:TP], 0.0, ALU.max, ALU.max))
            dv(TT(mm[:, TP:T:NT], aa[:, TP:T:NT], m0[:], ALU.max))
            for t in range(1, NT):
                dv(TT(mm[:, TP + t:T:NT], aa[:, TP + t:T:NT], mm[:, TP + t - 1:T:NT], ALU.max))
            says(TT(mt, bb, mm, ALU.add), "m_rows", 1)
            dv(TSC(wd[:, 0:TP], aa[:, 0:TP], mm[:, TP - 1:TP], None, ALU.subtract))
            mlast = mm[:, TP + NT - 1:T:NT]
            by_b = lambda v: v.rearrange("p (b t) -> p b t", b=NB)
            dv(TT(by_b(wd[:, TP:T]), by_b(aa[:, TP:T]), spread(mlast.unsqueeze(2), 2, NT), ALU.subtract))
            dv(TT(by_b(sd[:, 0:TS]), spread(m0[:].unsqueeze(2), 2, NT), by_b(mm[:, TP:T]), ALU.subtract))
            says(TT(sd[:, TS:TS + NB], m0[:], mlast, ALU.subtract), "gate_rows", 1)
            ip = FILLS["par"]
            dve.wait_ge(drained[ip[0]], ip[1] + 1)
            dv(V.memset(xpP[:, :, 0:3], 0.0))
            for x in range(2):
                dv(V.tensor_copy(xpS[:, x, :, 0:3], parT[:, 128 + 48:128 + 96].rearrange("p (b t x) -> p x b t", t=3, x=2)[:, x]))
            s0 = [parT[:, 64 * x:64 * x + 64].rearrange("p (b j) -> p b j", b=NB) for x in range(2)]
            ar, ai = (spread(sm[:, k, :].unsqueeze(1), 1, NB) for k in (10, 11))
            as5 = [stage[:, x, 0:64].rearrange("p (b j) -> p b j", b=NB) for x in range(4)]
            dv(TT(as5[0], s0[0], ar, ALU.mult))
            dv(TT(as5[1], s0[1], ai, ALU.mult))
            dv(TT(as5[2], as5[0], as5[1], ALU.subtract))
            dv(TT(as5[0], s0[1], ar, ALU.mult))
            dv(TT(as5[1], s0[0], ai, ALU.mult))
            dv(TT(as5[3], as5[0], as5[1], ALU.add))
            dv(TT(d0s[:], spread(seg[:, TP:T].unsqueeze(1), 1, J5), spread(mag.unsqueeze(2), 2, TS), ALU.mult))
            for x in range(2):
                fx = FILLS[f"xr{x}"]
                dve.wait_ge(*at("xp_ready", x + 1))
                dve.wait_ge(drained[fx[0]], fx[1] + 1)
                cw = lambda t: vec("rg_conv_w", 2 * t + x)
                outs = (xc[:, x, 0:TP], by_b(xc[:, x, TP:T]))
                ins = (lambda t: xpP[:, x, t:t + TP], lambda t: xpS[:, x, :, t:t + NT])
                for k in range(2):
                    dv(TSC(outs[k], ins[k](0), cw(0), vec("rg_conv_b", x), ALU.mult, ALU.add))
                for t in range(1, 4):
                    for k in range(2):
                        ins_ = STT(out=outs[k], in0=ins[k](t), scalar=cw(t), in1=outs[k], op0=ALU.mult, op1=ALU.add)
                        if t == 3 and k == 1:
                            says(ins_, "xc_ready", x + 1)
                        else:
                            dv(ins_)
            for x in range(2):
                dv(V.tensor_copy(cvfin[:, x, 0:3], xpP[:, x, TP:TP + 3]))
                dv(V.tensor_copy(cvfin[:, x, 3:27].rearrange("p (b t) -> p b t", b=NB), xpS[:, x, :, NT:NT + 3]))
            dve.wait_ge(*at("gate_rows_exp", 3))
            dve.wait_ge(*at("ind_ready", 1))
            for b in range(NB):
                V.tensor_copy(scm[:, b, NT * b:NT * b + NT], sd[:, NT * b:NT * b + NT]).then_inc(says_now("scm_ready"), 1)
            def s5_scan(j):
                b = j % 2
                if j == 0:
                    dve.wait_ge(*at("table_ready", 1))
                if j >= 2:
                    dve.wait_ge(*at("s5_turned", j - 1))
                for n in (f"bu{j}r", f"bu{j}i"):
                    await_fill(dve, n)
                br, bi = bank(f"bu{j}r")[:, 0:T], bank(f"bu{j}i")[:, 0:T]
                dv(TT(w_r[:, b, :], br, tab_r[:, j, :], ALU.mult))
                dv(TT(t_dve[:], bi, tab_i[:, j, :], ALU.mult))
                dv(TT(w_r[:, b, :], w_r[:, b, :], t_dve[:], ALU.add))
                drains(TT(w_i[:, b, :], bi, tab_r[:, j, :], ALU.mult), f"bu{j}i")
                drains(TT(t_dve[:], br, tab_i[:, j, :], ALU.mult), f"bu{j}r")
                dv(TT(w_i[:, b, :], w_i[:, b, :], t_dve[:], ALU.subtract))
                for x, w in enumerate((w_r, w_i)):
                    dv(TT(w[:, b, TP:T:NT], w[:, b, TP:T:NT], as5[2 + x][:, :, j], ALU.add))
                for x, w in enumerate((w_r, w_i)):
                    dv(V.tensor_tensor_scan(w[:, b, 0:TP], spread(mag[:, j:j + 1], 1, TP), w[:, b, 0:TP], 0.0, ALU.mult, ALU.add))
                    ins_ = V.tensor_tensor_scan(w[:, b, TP:T], d0s[:, j, :], w[:, b, TP:T], 0.0, ALU.mult, ALU.add)
                    if x == 0:
                        dv(ins_)
                    else:
                        says(ins_, "s5_scanned", j + 1)

            s5_scan(0)
            s5_scan(1)
            for x in range(2):
                f1 = FILLS[f"i{x}"]
                dve.wait_ge(drained[f1[0]], f1[1] + 1)
            dv(TT(xc[:], xc[:], ri[:], ALU.mult))
            s5_scan(2)
            s5_scan(3)
            dve.wait_ge(*at("rg_tanh", 2))
            dv(TSC(ri[:], rt[:], 1.0, None, ALU.add))
            dv(V.reciprocal(ri[:], ri[:]))
            says(STT(out=rt[:], in0=rt[:], scalar=2.0, in1=ri[:], op0=ALU.mult, op1=ALU.mult), "rg_ratio", 1)
            dve.wait_ge(*at("rg_a", 2))
            dve.wait_ge(*at("rg_root", 1))
            dv(TT(xc[:], xc[:], rt[:], ALU.mult))
            h0 = parT[:, 128 + 32:128 + 48].rearrange("p (b x) -> p x b", x=2)
            dv(TT(rsm[:, 48:64].rearrange("p (x b) -> p x b", x=2), rr[:, :, TP:T:NT], h0, ALU.mult))
            dv(TT(xc[:, :, TP:T:NT], xc[:, :, TP:T:NT], rsm[:, 48:64].rearrange("p (x b) -> p x b", x=2), ALU.add))
            dv(TT(rr[:], rr[:], spread(seg[:].unsqueeze(1), 1, 2), ALU.mult))
            for x in range(2):
                dv(V.tensor_tensor_scan(ri[:, x, :], rr[:, x, :], xc[:, x, :], 0.0, ALU.mult, ALU.add))
            dv(V.tensor_copy(rgfin[:, :, 0:1], ri[:, :, TP - 1:TP]))
            says(V.tensor_copy(rgfin[:, :, 1:9], ri[:, :, TP + NT - 1:T:NT]), "rgfin_ready", 1)

            def gelu_arg(y, tmp, name):
                dv(TT(tmp, y, y, ALU.mult))
                dv(TSC(tmp, tmp, 0.044715, 1.0, ALU.mult, ALU.add))
                says(TT(tmp, tmp, y, ALU.mult), name, 1)

            gelu_arg(gate[:], rt[:], "gate_poly")
            s5_scan(4)
            s5_scan(5)
            dve.wait_ge(*at("gate_tanh", 1))
            dv(STT(out=gate[:], in0=rt[:], scalar=1.0, in1=gate[:], op0=ALU.add, op1=ALU.mult))
            s5_scan(6)
            s5_scan(7)
            dve.wait_ge(*at("w_in_used", 6))
            says(STT(out=hT[:, 2:4, :], in0=gate[:], scalar=0.5, in1=ri[:], op0=ALU.mult, op1=ALU.mult), "mix_ready", 1)
            dve.wait_ge(sem("stored"), 0) if False else None
            says(V.memset(v_tok[:, :, :, 128:129], 1.0), "ones_ready", 1)
            dve.wait_ge(*at("e_zero", 1))
            dve.wait_ge(*at("causal_ready", 1))
            fr = FILLS["rows"]
            dve.wait_ge(drained[fr[0]], fr[1] + 1)
            dve.wait_ge(*at("rtok_ready", 1))

            def e_arg(h):
                await_fill(dve, f"mb{h}")
                mb = bank(f"mb{h}")
                dv(TSC(E[:, h, 0:256], mb[:, 0:256], rtok[:, 0, h:h + 1], 0.0, ALU.subtract, ALU.max))
                dv(TSC(E[:, h, 256:384], mb[:, 128:256], rtok[:, 1, h:h + 1], 0.0, ALU.subtract, ALU.max))
                drains(TSC(E[0:TS, h, 384:416], mb[0:TS, 256:288], rtok[0:TS, 2, h:h + 1], 0.0, ALU.subtract, ALU.max), f"mb{h}")
                dve.sem_inc(says_now("e_arg"), 1)

            def e_prob(h):
                dve.wait_ge(*at("e_exp", h + 1))
                dv(TT(E[:, h, :], E[:, h, :], causal[:], ALU.mult))
                await_fill(dve, f"st{h}")
                dv(TT(E[:, h, 0:384], bank(f"st{h}")[:, 0:384], E[:, h, 0:384], ALU.mult))
                drains(TT(E[0:TS, h, 384:416], bank(f"st{h}")[0:TS, 384:416], E[0:TS, h, 384:416], ALU.mult), f"st{h}")

            for h in range(H):
                e_arg(h)
                e_prob(h)
            dv(TT(wsm[:], wsm[:], spread(rtok[0:TS, 2, 64:64 + H].unsqueeze(2), 2, NB), ALU.mult), says_now("wsm_ready"))
            for i in range(3):
                fk = FILLS[f"kt{i}"]
                dve.wait_ge(drained[fk[0]], fk[1] + 1)
            dve.wait_ge(*at("cb_used", 1))
            says(TT(kw[:], k_tok[:, 0:2, :].rearrange("p i (h k) -> p i h k", h=H),
                    spread(rtok[:, 0:2, 64:64 + H].unsqueeze(3), 3, DK), ALU.mult), "kw_ready", 1)
            dve.wait_ge(sem("c0_loaded"), 64)
            dv(V.tensor_copy(c0[:, :, :, 128], parT[:, 128:160].rearrange("p (b h) -> p h b", h=H)))
            for h in range(H):
                await_fill(dve, f"sc{h}")
                drains(TT(qm[:, h], bank(f"sc{h}")[:, 0:NB * TS].rearrange("p (b t) -> p b t", b=NB),
                          spread(qT[:, h, TP:T].unsqueeze(1), 1, NB), ALU.mult), f"sc{h}")
            dve.sem_inc(says_now("qm_ready"), 1)
            dfl = FILLS["dec"]
            dve.wait_ge(drained[dfl[0]], dfl[1] + 1)
            dve.sem_inc(says_now("dec_ready"), 1)
            for k, i in enumerate((2, 0, 1)):
                n = TILES[i][1]
                rc, rv = rsm[0:n, 0:4], rsm[0:n, 32 + 4 * i:36 + 4 * i]
                for hh in range(2):
                    await_fill(dve, f"nu{i}{hh}")
                    den, out = bank(f"nu{i}{hh}")[0:n, 128:258:129], rc[:, 2 * hh:2 * hh + 2]
                    dv(V.tensor_copy(out, den))
                    dv(STT(out=out, in0=den, scalar=-1.0, in1=out, op0=ALU.mult, op1=ALU.max))
                    ins_ = TT(out, out, rtok[0:n, i, 32 + 2 * hh:34 + 2 * hh], ALU.max)
                    says(ins_, "den_read", k + 1) if hh else dv(ins_)
                dv(V.reciprocal(rc, rc))
                dve.wait_ge(*at("nsq_ready", 4 * k + 4))
                dv(TT(rv, rc, rc, ALU.mult))
                dv(TT(rv, rv, rsm[0:n, 16 + 4 * i:20 + 4 * i], ALU.mult))
                says(TSC(rv, rv, 1.0 / DK, EPS, ALU.mult, ALU.add), "nvar_ready", k + 1)
                dve.wait_ge(*at("nroot_ready", k + 1))
                dv(V.reciprocal(rv, rv))
                dv(TT(rv, rv, rc, ALU.mult))
                for h in range(H):
                    name = f"nu{i}{h // 2}"
                    ot = o_tok[0:n, i, 128 * h:128 * h + 128]
                    ins_ = STT(out=ot, in0=bank(name)[0:n, 129 * (h % 2):129 * (h % 2) + 128], scalar=rv[:, h:h + 1],
                               in1=ot, op0=ALU.mult, op1=ALU.mult)
                    if h % 2:
                        drains(ins_, name)
                    else:
                        dv(ins_)
            dve.sem_inc(says_now("y3_ready"), 1)
            for x in range(2):
                await_fill(dve, f"ys{x}")
                drains(STT(out=xc[:, x, :], in0=uT[:, x, :], scalar=vec("s5_d", x), in1=bank(f"ys{x}")[:, 0:T],
                           op0=ALU.mult, op1=ALU.add), f"ys{x}")
            gelu_arg(xc[:], rt[:], "s5_poly")
            dve.wait_ge(*at("s5_tanh", 1))
            dv(STT(out=rt[:], in0=rt[:], scalar=1.0, in1=xc[:], op0=ALU.add, op1=ALU.mult))
            says(TSC(rt[:], rt[:], 0.5, None, ALU.mult), "s5_gelu", 1)
            for x in range(2):
                fgl = FILLS[f"glu{x}"]
                dve.wait_ge(drained[fgl[0]], fgl[1] + 1)
            says(TT(hT[:, 0:2, :], rt[:], ri[:], ALU.mult), "rg_used", 1)
            for h in range(H):
                dve.wait_ge(*at("c_decayed", h + 1))
                for gidx, (b0, b1) in enumerate(CB):
                    name = f"cu{h}{gidx}"
                    await_fill(dve, name)
                    drains(TT(c0[:, h, b0:b1, :], c0[:, h, b0:b1, :],
                              bank(name)[:, 0:(b1 - b0) * 129].rearrange("p (b v) -> p b v", v=129), ALU.add), name)
                says(V.tensor_copy(nbuf[:, 0:32].rearrange("p (b h) -> p h b", h=H)[:, h, :], c0[:, h, :, 128]), "c_new", h + 1)
            dve.wait_ge(sem("x1_loaded"), 32)
            for i, (t0, n) in enumerate(TILES):
                for c in range(2):
                    name = f"wo{i}{c}"
                    await_fill(dve, name)
                    xs = x1[0:n, i, 512 * c:512 * c + 512]
                    b, f = FILLS[name]
                    says(TT(xs, xs, bank(name)[0:n, :], ALU.add), "x1_added", 2 * i + c + 1)
                    dve.sem_inc(drained[b], 1)
            dve.wait_ge(*at("mixer_done", 1))
            dve.wait_ge(*at("ms2_ready", 3))
            says(TSC(st2[:, 4:7], st2[:, 0:3], 1.0 / D, EPS, ALU.mult, ALU.add), "var2_ready", 1)
            dve.wait_ge(*at("root2_ready", 1))
            dv(V.reciprocal(st2[:, 4:7], st2[:, 4:7]))
            dve.wait_ge(sem("router_loaded"), 48)
            for i, (t0, n) in enumerate(TILES):
                says(STT(out=xn[0:n, i, :], in0=x1[0:n, i, :], scalar=st2[0:n, 4 + i:5 + i], in1=g2b[0:n, :],
                         op0=ALU.mult, op1=ALU.mult), "x2_ready", i + 1)
            dv(V.memset(lg[:], 0.0))
            dv(V.memset(slot[:], -1.0))
            dv(V.memset(sgate[:], 0.0))
            dv(V.memset(yb[:], 0.0))
            dv(V.memset(sgt[:], 0.0))
            await_fill(dve, "lg")
            lgp = bank("lg")[:, 0:96].rearrange("p (i e) -> p i e", i=3)
            dv(TT(lg[:, 0:2, :], lgp[:, 0:2, :], spread(rbias[:].unsqueeze(1), 1, 2), ALU.add))
            drains(TT(lg[0:TS, 2, :], lgp[0:TS, 2, :], rbias[0:TS, :], ALU.add), "lg")
            for i in range(3):
                dv(V.max(top[:, i, :], lg[:, i, :]))
                dv(V.max_index(topi[:, i, :], top[:, i, :], lg[:, i, :]))
            dv(V.tensor_copy(topf[:], topi[:]))
            says(TT(gk[:, :, 0:TOPK], top[:, :, 0:TOPK], spread(top[:, :, 0:1], 2, TOPK), ALU.subtract), "top_diff", 1)
            dve.wait_ge(*at("top_exp", 1))
            dv(V.tensor_reduce(gk[:, :, 4:5], gk[:, :, 0:TOPK], AX.X, ALU.add))
            dv(V.reciprocal(gk[:, :, 4:5], gk[:, :, 4:5]))
            dv(TT(gk[:, :, 0:TOPK], gk[:, :, 0:TOPK], spread(gk[:, :, 4:5], 2, TOPK), ALU.mult))
            dve.wait_ge(*at("bias_ready", 1))
            ie = spread(iota_e[:].unsqueeze(1), 1, 3)
            for k in range(TOPK):
                of = lambda v: spread(v[:, :, k:k + 1], 2, NE)
                if k == 0:
                    dv(TT(msk[:], ie, of(topf), ALU.is_equal))
                    dv(TT(gts[:], msk[:], of(gk), ALU.mult))
                else:
                    dv(TT(tmp3[:], ie, of(topf), ALU.is_equal))
                    dv(TT(msk[:], msk[:], tmp3[:], ALU.add))
                    dv(TT(tmp3[:], tmp3[:], of(gk), ALU.mult))
                    dv(TT(gts[:], gts[:], tmp3[:], ALU.add))
            says(V.tensor_copy(mskb[:], msk[:]), "mask_ready", 1)
            await_fill(dve, "cum")
            cp = bank("cum")[:, 0:96].rearrange("p (i e) -> p i e", i=3)
            dv(TT(tmp3[:, 0:2, :], cp[:, 0:2, :], msk[:, 0:2, :], ALU.mult))
            dv(TT(tmp3[0:TS, 2, :], cp[0:TS, 2, :], msk[0:TS, 2, :], ALU.mult))
            dv(V.tensor_reduce(st2[:, 8:9], bank("cum")[:, 96:128], AX.X, ALU.max))
            says(V.tensor_copy(cnt[:], st2[:, 8:9]), "count_ready", 1)
            for i, (t0, n) in enumerate(TILES):
                pairs = lambda v: v[0:n, 0:NPAIR, i, :]
                src = lambda v: v[0:n, i, :].rearrange("p (q x) -> p q x", x=2)
                dv(TSC(pairs(slot), src(tmp3), -1.0, None, ALU.add))
                dv(V.tensor_copy(pairs(sgate), src(gts)))

            def wide(v, p):
                return spread(v[:, bass.ds(p, 1), :, :].rearrange("p a i x -> p (a i) x").unsqueeze(3), 3, SLOTS)

            slots4 = spread(spread(iota_s[:].unsqueeze(1).unsqueeze(1), 1, 3), 2, 2)

            def select(p):
                return TT(S[:], wide(slot, p), slots4, ALU.is_equal)

            def select_bias(p):
                return TSC(selb[0:96], half[0:96], selid[0:96, bass.ds(p, 1)], None, ALU.is_equal)

            def add_combined(c):
                i, nn = c // 2, c % 2
                n = TILES[i][1]
                dst = acc[0:n, i, 512 * nn:512 * nn + 512]
                return TT(dst, dst, psum[0:n, 6 + c % 2, :], ALU.add)

            STEPS = 6

            def sweep(base, extra):
                with dve.Fori(0, NPAIR) as p:
                    gp = base + p
                    k = [0]

                    def dl(ins):
                        k[0] += 1
                        ins.then_inc(sem("dve_loop"), 1)
                        dve.wait_ge(sem("dve_loop"), gp * STEPS + k[0])

                    dve.wait_ge(sem("sgt_ready"), gp)
                    dl(TT(SG[:], S[:], wide(sgate, p), ALU.mult))
                    dve.sem_inc(sem("sg_ready"), 1)
                    dve.wait_ge(sem("gather_ready"), gp * 2 + 2)
                    dl(select(p + 1))
                    dve.sem_inc(sem("s_ready"), 1)
                    for x in range(2):
                        for c in (range(0, 2) if x == 0 else range(4, 6)):
                            dve.wait_ge(sem("combine_ready"), gp * 6 + c + 1 + extra * 6)
                            add_combined(c).then_inc(sem("combine_added"), 1)
                        dve.wait_ge(sem("block_done"), gp * BLOCKS + 2 * x + 1)
                        dve.wait_ge(sem("aT_ready"), gp * 2 - 0) if x == 0 else None
                        TSC(gact[:, x, :], psum[:, 2 * x, :], 7.0, None, ALU.min).then_inc(sem("g_clipped"), 1)
                        if x == 0:
                            for c in range(2, 4):
                                dve.wait_ge(sem("combine_ready"), gp * 6 + c + 1 + extra * 6)
                                add_combined(c).then_inc(sem("combine_added"), 1)
                        dve.wait_ge(sem("block_done"), gp * BLOCKS + 2 * x + 2)
                        dl(TSC(uact[:, x, :], psum[:, 2 * x + 1, :], 7.0, -7.0, ALU.min, ALU.max))
                        dve.wait_ge(sem("g_clipped"), gp * 2 + 1 + x)
                        dl(STT(out=uact[:, x, :], in0=uact[:, x, :], scalar=1.0, in1=gact[:, x, :], op0=ALU.add, op1=ALU.mult))
                        dve.wait_ge(sem("sig_ready"), gp * 2 + 1 + x)
                        TT(gact[:, x, :], uact[:, x, :], sg1[:, x, :], ALU.mult).then_inc(sem("act_ready"), 1)
                    dve.wait_ge(sem("bias_used"), gp + 1)
                    select_bias(p + 1).then_inc(sem("selb_ready"), 1)
                    assert k[0] == STEPS
                for c in range(6):
                    dve.wait_ge(sem("combine_ready"), base * 6 + NPAIR * 6 + extra * 6 + c + 1)
                    add_combined(c).then_inc(sem("combine_added"), 1)
                V.memset(sgt[:], 0.0).then_inc(sem("sgt_cleared"), 1)

            t2 = st2[:, 12:14]
            says(select(0), "s_ready", 1)
            says(select_bias(0), "selb_ready", 1)
            dve.wait_ge(*at("acc_zero", 1))
            sweep(0, 0)
            most = dve.value_load(cnt[0:1, 0:1], min_val=0, max_val=T)
            with dve.Fori(1, SWEEPS) as r:
                with dve.If(most > r * SLOTS):
                    TSC(iota_s[:], iota_s[:], float(SLOTS), None, ALU.add).then_inc(sem("slots_moved"), 1)
                    dve.wait_ge(sem("slots_moved"), r)
                    dve.wait_ge(sem("gather_ready"), r * (2 * NPAIR) + 2)
                    dve.wait_ge(sem("selb_ready"), r * NPAIR + 1)
                    select(0).then_inc(sem("reselected"), 1)
                    select_bias(0).then_inc(sem("reselected"), 1)
                    dve.wait_ge(sem("reselected"), r * 2)
                    dve.wait_ge(sem("regather_ready"), r * 2)
                    dve.sem_inc(sem("sweep_entered"), 1)
                    sweep(r * NPAIR, r)
            V.memset(t2[0:1, 0:1], 0.0).then_inc(sem("sums_done"), 1)
            dve.wait_ge(sem("sums_done"), 1)
            says(TT(x1[:, 0:2, :], x1[:, 0:2, :], acc[:, 0:2, :], ALU.add), "x2_part", 1)
            says(TT(x1[0:TS, 2, :], x1[0:TS, 2, :], acc[0:TS, 2, :], ALU.add), "x2_added", 1)
            dve.wait_ge(sem("ms3_ready"), 3)
            says(TSC(st2[:, 4:7], st2[:, 0:3], 1.0 / D, EPS, ALU.mult, ALU.add), "var3_ready", 1)
            dve.wait_ge(sem("root3_ready"), 1)
            dv(V.reciprocal(st2[:, 4:7], st2[:, 4:7]))
            dve.wait_ge(sem("gf_loaded"), 16)
            for i, (t0, n) in enumerate(TILES):
                STT(out=x1[0:n, i, :], in0=x1[0:n, i, :], scalar=st2[0:n, 4 + i:5 + i], in1=gfb[0:n, :],
                    op0=ALU.mult, op1=ALU.mult).then_inc(sem("y_final"), 1)

        @block.tensor
        def _(pe):
            M, TR = nc.tensor.matmul, nc.tensor.transpose

            pe.wait_ge(*at("ident_ready", 1))
            pe.wait_ge(sem("vec_loaded"), 16 * 11)
            ends_fill(TR(bank("vec")[:, 0:NVEC], vrow[0:NVEC, :], ident[0:NVEC, 0:NVEC]), "vec")
            for k in range(6):
                i, hf = k // 2, k % 2
                t0, n = TILES[i]
                pe.wait_ge(*at("xn_ready", i + 1))
                await_bank(pe, f"hT{k}")
                for c in range(4):
                    m = TR(bank(f"hT{k}")[:, 128 * c:128 * c + n], xn[0:n, i, (4 * hf + c) * 128:(4 * hf + c + 1) * 128], ident[0:n, 0:n])
                ends_fill(m, f"hT{k}")
            pe.wait_ge(filled[FILLS["hT5"][0]], FILLS["hT5"][1] + 1)
            pe.sem_inc(says_now("xn_used"), 1)
            for k in range(6):
                b, f = FILLS[f"hT{k}"]
                pe.wait_ge(drained[b], f + 1)
            pe.wait_ge(sem("wgate_loaded"), 32)
            await_bank(pe, "gates")
            for k in range(KD):
                m = M(bank("gates")[0:36, 0:T], wgate[:, k, :], hT[:, k, :], start=(k == 0), stop=(k == KD - 1))
            ends_fill(m, "gates")

            def channels(name, c, col):
                await_bank(pe, name)
                w = slot_view(c % 3, WCH[c][1])
                for k in range(KD):
                    m = M(bank(name)[:, 0:T], w[:, k, col:col + 128], hT[:, k, :], start=(k == 0), stop=(k == KD - 1))
                ends_fill(m, name)

            def tokens(name, c, col, i):
                await_bank(pe, name)
                t0, n = TILES[i]
                w = slot_view(c % 3, WCH[c][1])
                for k in range(KD):
                    m = M(bank(name)[0:n, 0:256], hT[:, k, t0:t0 + n], w[:, k, col:col + 256], start=(k == 0), stop=(k == KD - 1))
                ends_fill(m, name)

            def used(name, count):
                b, f = FILLS[name]
                pe.wait_ge(filled[b], f + 1)
                pe.sem_inc(says_now("w_in_used"), 1)

            def s5_in(j):
                r0, tt = 32 * (j % 4), j // 4
                for x, name in enumerate((f"bu{j}r", f"bu{j}i")):
                    await_bank(pe, name)
                    ends_fill(M(bank(name)[:, 0:T], wB[r0:r0 + 32, 2 * x + tt, :], uT[r0:r0 + 32, tt, :], start=True, stop=True), name)

            def s5_out(j):
                r0, tt = 32 * (j % 4), j // 4
                pe.wait_ge(*at("s5_turned", j + 1))
                out = bank(f"ys{tt}")[r0:r0 + 32, 0:T]
                M(out, wC[:, tt, r0:r0 + 32], s_r[:, j % 2, :], start=True, stop=False)
                M(out, wC[:, 2 + tt, r0:r0 + 32], s_i[:, j % 2, :], start=False, stop=True).then_inc(says_now("s5_used"), 1)
                if j % 4 == 3:
                    pe.wait_ge(*at("s5_used", j + 1))
                    pe.sem_inc(filled[FILLS[f"ys{tt}"][0]], 1)

            pe.wait_ge(sem("w_in0"), 16)
            for n, name in enumerate(("u0", "u1", "xr0", "xr1")):
                channels(name, 0, 128 * n)
            used("xr1", 1)
            pe.wait_ge(sem("par_loaded"), 16 * 5)
            await_bank(pe, "par")
            TR(bank("par")[:, 0:128], srow[:], ident[:])
            ends_fill(TR(bank("par")[:, 128:224], prow[0:96, :], ident[0:96, 0:96]), "par")
            pe.wait_ge(*at("bb_ready", 4))
            await_bank(pe, "bt")
            for x in range(4):
                m = TR(bank("bt")[:, 128 * x:128 * x + 128], BB[:, 4 * x:4 * x + 4].rearrange("p j g c -> p (j g c)"), ident[:])
            ends_fill(m, "bt")
            pe.wait_ge(*at("cb_ready", 2))
            await_bank(pe, "ct")
            for x in range(4):
                m = TR(bank("ct")[:, 128 * x:128 * x + 128], CBk[:, x, :], ident[:])
            ends_fill(m, "ct")
            pe.wait_ge(sem("w_in1"), 16)
            for n, name in enumerate(("gr0", "gr1", "q0", "q1")):
                channels(name, 1, 128 * n)
            used("q1", 2)
            pe.sem_inc(says_now("cb_used"), 1)
            for n in ("u0", "u1", "bt"):
                pe.wait_ge(drained[FILLS[n][0]], FILLS[n][1] + 1)
            s5_in(0)
            s5_in(1)
            pe.wait_ge(sem("w_in2"), 16)
            for n, name in enumerate(("q2", "q3", "k0", "k1")):
                channels(name, 2, 128 * n)
            used("k1", 3)
            pe.wait_ge(sem("wax_loaded"), 16 * 16)
            pe.wait_ge(*at("xc_ready", 2))
            for x, nm in enumerate(("r", "i")):
                for tt in range(2):
                    await_bank(pe, f"{nm}{tt}")
                    ends_fill(M(bank(f"{nm}{tt}")[:, 0:T], wax[:, x, tt, :], xc[:, tt, :], start=True, stop=True), f"{nm}{tt}")
            pe.wait_ge(sem("w_in3"), 16)
            channels("k2", 3, 0)
            channels("k3", 3, 128)
            for i in range(3):
                tokens(f"va{i}", 3, 256, i)
            used("va2", 4)
            s5_in(2)
            s5_in(3)
            pe.wait_ge(drained[FILLS["ct"][0]], FILLS["ct"][1] + 1)
            s5_out(0)
            s5_out(1)
            pe.wait_ge(sem("w_in4"), 16)
            for i in range(3):
                tokens(f"vb{i}", 4, 0, i)
            for i in range(3):
                tokens(f"oa{i}", 4, 256, i)
            used("oa2", 5)
            s5_in(4)
            s5_in(5)
            s5_out(2)
            s5_out(3)
            pe.wait_ge(sem("w_in5"), 16)
            for i in range(3):
                tokens(f"ob{i}", 5, 0, i)
            used("ob2", 6)
            s5_in(6)
            s5_in(7)
            s5_out(4)
            s5_out(5)
            pe.wait_ge(*at("gate_rows_exp", 3))
            await_bank(pe, "rows")
            for i, (t0, n) in enumerate(TILES):
                m = TR(bank("rows")[0:n, 128 * i:128 * i + 128], rows[:, t0:t0 + n], ident[:])
            ends_fill(m, "rows")
            for h in range(H):
                b, f = FILLS[f"k{h}"]
                pe.wait_ge(drained[b], f + 1)
            for i, (t0, n) in enumerate(TILES):
                await_bank(pe, f"kt{i}")
                for h in range(H):
                    m = TR(bank(f"kt{i}")[0:n, 128 * h:128 * h + 128], kT[:, h, t0:t0 + n], ident[:])
                ends_fill(m, f"kt{i}")
            s5_out(6)
            s5_out(7)
            pe.wait_ge(*at("sel4_ready", 1))
            pe.wait_ge(*at("m_rows", 1))
            for h in range(H):
                await_bank(pe, f"mb{h}")
                ends_fill(M(bank(f"mb{h}")[:, 0:T], sel4[:, h, :], gsm[0:H, 4, :], start=True, stop=True), f"mb{h}")
                await_bank(pe, f"st{h}")
                sb_ = bank(f"st{h}")
                M(sb_[:, 0:256], kT[:, h, 0:128], qT[:, h, 0:256], start=True, stop=True)
                M(sb_[:, 256:384], kT[:, h, 128:256], qT[:, h, 128:256], start=True, stop=True)
                ends_fill(M(sb_[0:TS, 384:416], kT[:, h, TP:T], qT[:, h, TP:T], start=True, stop=True), f"st{h}")
            await_bank(pe, "dec")
            for h in range(H):
                m = M(bank("dec")[:, NB * h:NB * h + NB], sel4[:, h, :], gsm[0:H, 6, TS:TS + NB], start=True, stop=True)
            ends_fill(m, "dec")
            pe.wait_ge(*at("scm_ready", NB))
            for h in range(H):
                await_bank(pe, f"sc{h}")
                ends_fill(M(bank(f"sc{h}")[:, 0:NB * TS], sel4[:, h, :], scm[:].rearrange("h b t -> h (b t)"), start=True, stop=True), f"sc{h}")
            pe.wait_ge(*at("ones_ready", 1))
            for h in range(H):
                b, f = FILLS[f"st{h}"]
                pe.wait_ge(drained[b], f + 1)
            for n in ("vb2", "vb1", "vb0", "va2", "va1", "va0"):
                pe.wait_ge(drained[FILLS[n][0]], FILLS[n][1] + 1)
            pe.sem_inc(says_now("v_ready"), 1)
            pe.wait_ge(*at("qm_ready", 1))
            for i in (2, 0, 1):
                n = TILES[i][1]
                for hh in range(2):
                    name = f"nu{i}{hh}"
                    await_bank(pe, name)
                    for x in range(2):
                        h = 2 * hh + x
                        out = bank(name)[0:n, 129 * x:129 * x + 129]
                        if i == 2:
                            M(out, E[0:TS, h, 384:416], v_tok[0:TS, 2, h, :], start=True, stop=False)
                            for b in range(NB):
                                m = M(out, qm[:, h, b, :], c0[:, h, b, :], start=False, stop=(b == NB - 1))
                        elif i == 0:
                            m = M(out, E[:, h, 0:128], v_tok[:, 0, h, :], start=True, stop=True)
                        else:
                            M(out, E[:, h, 128:256], v_tok[:, 0, h, :], start=True, stop=False)
                            m = M(out, E[:, h, 256:384], v_tok[:, 1, h, :], start=False, stop=True)
                    ends_fill(m, name)
                if i == 2:
                    pe.wait_ge(filled[FILLS["nu21"][0]], FILLS["nu21"][1] + 1)
                    pe.sem_inc(says_now("c0_used"), 1)
            pe.wait_ge(*at("s5_gelu", 1))
            pe.wait_ge(sem("glw_loaded"), 16)
            for x in range(2):
                await_bank(pe, f"glu{x}")
                for k in range(2):
                    m = M(bank(f"glu{x}")[:, 0:T], glw[:, k, 128 * x:128 * x + 128], rt[:, k, :], start=(k == 0), stop=(k == 1))
                ends_fill(m, f"glu{x}")
            for h in range(H):
                pe.wait_ge(*at("vw_ready", h + 1))
                for gidx, (b0, b1) in enumerate(CB):
                    name = f"cu{h}{gidx}"
                    await_bank(pe, name)
                    ends_fill(M(bank(name)[:, 0:(b1 - b0) * 129], k_tok[0:TS, 2, 128 * h:128 * h + 128],
                                vw[:, h % 2, b0:b1, :].rearrange("p b v -> p (b v)"), start=True, stop=True), name)
                b, f = FILLS[f"cu{h}2"]
                pe.wait_ge(filled[b], f + 1)
                pe.sem_inc(says_now("vw_used"), 1)
            pe.wait_ge(*at("kw_ready", 1))
            for hh in range(2):
                await_bank(pe, f"cp{hh}")
                for x in range(2):
                    h = 2 * hh + x
                    for i in range(2):
                        m = M(bank(f"cp{hh}")[:, 129 * x:129 * x + 129], kw[:, i, h, :], v_tok[:, i, h, :], start=(i == 0), stop=(i == 1))
                ends_fill(m, f"cp{hh}")
            pe.wait_ge(*at("c_new", H))
            pe.wait_ge(*at("c_prompt", 2))
            await_bank(pe, "nT")
            ends_fill(TR(bank("nT")[0:36, 0:128], nbuf[:], ident[:]), "nT")
            pe.wait_ge(*at("rgfin_ready", 1))
            await_bank(pe, "rgT")
            for x in range(2):
                TR(bank("rgT")[0:9, 128 * x:128 * x + 128], rgfin[:, x, :], ident[:])
            for x in range(2):
                m = TR(bank("rgT")[0:27, 256 + 128 * x:384 + 128 * x], cvfin[:, x, :], ident[:])
            ends_fill(m, "rgT")
            await_bank(pe, "s5T")
            for x in range(2):
                m = TR(bank("s5T")[0:72, 128 * x:128 * x + 128], fin5[:, x].rearrange("p s j -> p (s j)"), ident[:])
            ends_fill(m, "s5T")
            pe.wait_ge(*at("y3_ready", 1))
            for h in range(H):
                await_bank(pe, f"yT{h}")
                for i, (t0, n) in enumerate(TILES):
                    m = TR(bank(f"yT{h}")[:, t0:t0 + n], o_tok[0:n, i, 128 * h:128 * h + 128], ident[0:n, 0:n])
                ends_fill(m, f"yT{h}")
            b, f = FILLS["yT3"]
            pe.wait_ge(filled[b], f + 1)
            pe.sem_inc(says_now("y_turned"), 1)
            pe.wait_ge(*at("rg_used", 1))
            pe.wait_ge(*at("mix_ready", 1))
            for h in range(H):
                b, f = FILLS[f"yT{h}"]
                pe.wait_ge(drained[b], f + 1)
            for n in range(2):
                pe.wait_ge(sem(f"w_out{n}"), 16)
            for i, (t0, n) in enumerate(TILES):
                for c in range(2):
                    name = f"wo{i}{c}"
                    await_bank(pe, name)
                    w = slot_view(2 + c, 512)
                    for k in range(KD):
                        m = M(bank(name)[0:n, :], hT[:, k, t0:t0 + n], w[:, k, :], start=(k == 0), stop=(k == KD - 1))
                    ends_fill(m, name)
            for i in range(6):
                b, f = FILLS[f"wo{i // 2}{i % 2}"]
                pe.wait_ge(filled[b], f + 1)
            pe.sem_inc(says_now("w_out_used"), 1)
            pe.wait_ge(sem("stored"), 16 * 17)
            pe.wait_ge(*at("x1_added", 6))
            pe.sem_inc(says_now("mixer_done"), 1)
            for k in range(6):
                i, hf = k // 2, k % 2
                t0, n = TILES[i]
                pe.wait_ge(*at("x2_ready", i + 1))
                await_bank(pe, f"h2T{k}")
                for c in range(4):
                    m = TR(bank(f"h2T{k}")[:, 128 * c:128 * c + n], xn[0:n, i, (4 * hf + c) * 128:(4 * hf + c + 1) * 128], ident[0:n, 0:n])
                ends_fill(m, f"h2T{k}")
            for k in range(6):
                b, f = FILLS[f"h2T{k}"]
                pe.wait_ge(drained[b], f + 1)
            pe.wait_ge(sem("router_loaded"), 48)
            await_bank(pe, "lg")
            for i, (t0, n) in enumerate(TILES):
                for k in range(KD):
                    m = M(bank("lg")[0:n, NE * i:NE * i + NE], h2T[:, k, t0:t0 + n], rw[:, k, :], start=(k == 0), stop=(k == KD - 1))
            ends_fill(m, "lg")
            pe.wait_ge(*at("mask_ready", 1))
            await_bank(pe, "cum")
            for i, (t0, n) in enumerate(TILES):
                for j in range(i + 1):
                    nj = TILES[j][1]
                    lhs = upper[0:nj, 0:n] if j == i else ones_bf[0:nj, 0:n]
                    M(bank("cum")[0:n, NE * i:NE * i + NE], lhs, mskb[0:nj, j, :], start=(j == 0), stop=(j == i))
            for i, (t0, n) in enumerate(TILES):
                m = M(bank("cum")[:, 96:128], ones_bf[0:n, :], mskb[0:n, i, :], start=(i == 0), stop=(i == 2))
            ends_fill(m, "cum")

            W1COL = [0, 2, 1, 3]

            def gather(name, inc_count):
                for c in range(KD):
                    for i, (t0, n) in enumerate(TILES):
                        m = M(psum[:, 6 + c // 4, 128 * (c % 4):128 * (c % 4) + 128], xn[0:n, i, 128 * c:128 * c + 128],
                              S[0:n, i].rearrange("p x s -> p (x s)"), start=(i == 0), stop=(i == 2))
                    if c % 4 == 3:
                        m.then_inc(sem(name), 1)

            def combine(c):
                i, nn = c // 2, c % 2
                t0, n = TILES[i]
                M(psum[0:n, 6 + c % 2, :], sgt[:, t0:t0 + n], yb[:, nn, :], start=True, stop=True).then_inc(sem("combine_ready"), 1)

            def bias(bk, col):
                return M(psum[:, bk, :], selb[0:96].rearrange("p x s -> p (x s)"), bsplit[0:96, col:col + 512], start=True, stop=False)

            def sweep(base, extra, chunk_base):
                with pe.Fori(0, NPAIR) as p:
                    gp = base + p

                    def await_chunks(w):
                        for x in range(2):
                            pe.wait_ge(sem(f"expert_chunk{2 * (w % 3) + x}"), gp * 32 + 16 * (w // 3) + 16)

                    pe.wait_ge(sem("selb_ready"), gp + 1)
                    pe.wait_ge(sem("xg_copied"), gp * 2 + 2)
                    for w in range(4):
                        if w < 2:
                            pe.wait_ge(sem("aT_copied"), gp * 2 + 0)
                        bias(w, [0, FF, 512, FF + 512][w])
                        await_chunks(w)
                        for k in range(KD):
                            for x in range(2):
                                m = M(psum[64 * x:64 * x + 64, w, :], xg[:, k, 64 * x:64 * x + 64],
                                      ring[:, 2 * (w % 3) + x, 512 * k:512 * k + 512], start=False, stop=(k == KD - 1))
                        m.then_inc(sem("block_done"), 1)
                        if w < 3:
                            for c in (2 * w, 2 * w + 1):
                                if c < 2:
                                    if c == 0:
                                        pe.wait_ge(sem("y_copied"), gp * 2)
                                        pe.wait_ge(sem("sgt_copied"), gp)
                                else:
                                    pe.wait_ge(sem("combine_added"), gp * 6 + c - 1 + extra * 6)
                                combine(c)
                    pe.wait_ge(sem("combine_added"), gp * 6 + 6 + extra * 6)
                    pe.wait_ge(sem("s_ready"), gp + 2)
                    gather("gather_ready", None)
                    for x in range(2):
                        pe.wait_ge(sem("act_ready"), gp * 2 + 1 + x)
                        for c in range(4):
                            m = TR(psum[:, x, 128 * c:128 * c + 128], gact[:, x, 128 * c:128 * c + 128], ident[:])
                        m.then_inc(sem("aT_ready"), 1)
                    pe.wait_ge(sem("sg_ready"), gp + 1)
                    pe.wait_ge(sem("xg_copied"), gp * 2 + 3)
                    for i, (t0, n) in enumerate(TILES):
                        m = TR(psum[:, 6, t0:t0 + n], SG[0:n, i].rearrange("p x s -> p (x s)"), ident[0:n, 0:n])
                    m.then_inc(sem("sgt_ready"), 1)
                    for nn in range(2):
                        m = bias(4 + nn, 2 * FF + 512 * nn)
                    m.then_inc(sem("bias_used"), 1)
                    for hf in range(2):
                        await_chunks(4 + hf)
                        pe.wait_ge(sem("aT_copied"), gp * 2 + 1 + hf)
                        for k in range(4):
                            for nn in range(2):
                                for x in range(2):
                                    m = M(psum[64 * x:64 * x + 64, 4 + nn, :], aT[:, 4 * hf + k, 64 * x:64 * x + 64],
                                          ring[:, 2 * ((4 + hf) % 3) + x, 1024 * k + 512 * nn:1024 * k + 512 * nn + 512],
                                          start=False, stop=(hf == 1 and k == 3))
                        m.then_inc(sem("block_done"), 1)
                pe.wait_ge(sem("y_copied"), base * 2 + NPAIR * 2)
                pe.wait_ge(sem("sgt_copied"), base + NPAIR)
                pe.wait_ge(sem("xg_copied"), base * 2 + NPAIR * 2 + 2)
                for c in range(6):
                    if c >= 2:
                        pe.wait_ge(sem("combine_added"), base * 6 + NPAIR * 6 + extra * 6 + c - 1)
                    combine(c)

            pe.wait_ge(sem("s_ready"), 1)
            pe.wait_ge(*at("bias_ready", 1))
            gather("gather_ready", None)
            sweep(0, 0, 0)
            pe.wait_ge(*at("count_ready", 1))
            most = pe.value_load(cnt[0:1, 0:1], min_val=0, max_val=T)
            with pe.Fori(1, SWEEPS) as r:
                with pe.If(most > r * SLOTS):
                    pe.wait_ge(sem("sgt_cleared"), r)
                    pe.wait_ge(sem("reselected"), r * 2)
                    gather("regather_ready", None)
                    pe.wait_ge(sem("xg_recopied"), r * 2)
                    pe.sem_inc(sem("sweep_entered"), 1)
                    sweep(r * NPAIR, r, 0)


_INS = ["x_prompt", "x_sample", "state_s5_re", "state_s5_im", "state_rg_h", "state_rg_conv", "state_ml_c",
        "state_ml_n", "state_ml_m", "norm1_g", "w_in", "s5_lambda_re", "s5_lambda_im", "s5_log_step", "s5_b_re",
        "s5_b_im", "s5_c_re", "s5_c_im", "s5_d", "s5_glu_w", "s5_glu_b", "rg_conv_w", "rg_conv_b", "rg_wa", "rg_ba",
        "rg_wx", "rg_bx", "rg_lambda", "ml_gate_bias", "ml_norm_g", "w_out", "norm2_g", "router_w", "router_b",
        "exp_w1", "exp_b1", "exp_w2", "exp_b2", "final_norm_g"]
_STATES = lambda b: [(1, b, G5, P5), (1, b, G5, P5), (1, b, 256), (1, b, 3, 256), (1, b, H, DK, DK), (1, b, H, DK), (1, b, H)]
_OUTS = [(1, TP, D), (NB, NT, D)] + _STATES(1) + _STATES(NB)


def kernel(**inputs):
    import numpy as _np
    import concourse.bacc as _bacc
    from concourse.bass_utils import run_bass_kernel_spmd as _run

    nc = _bacc.Bacc("TRN2", target_bir_lowering=False, num_devices=1)
    arrays, args = {}, {}
    for name in _INS:
        v = _np.ascontiguousarray(inputs[name])
        arrays[f"in_{name}_dram"] = v
        args[name] = nc.dram_tensor(f"in_{name}_dram", v.shape, mybir.dt.from_np(v.dtype), kind="ExternalInput").ap()
    outs = [nc.dram_tensor(f"out_{i}_dram", shape, F32, kind="ExternalOutput").ap() for i, shape in enumerate(_OUTS)]
    build_program(nc, args, outs)
    r = _run(nc, [arrays], core_ids=[0])
    return tuple(r.results[0][f"out_{i}_dram"] for i in range(len(_OUTS)))
```

```python
from contextlib import ExitStack
import math

import concourse.bass as bass
from concourse import mybir

ALU = mybir.AluOpType
ACT = mybir.ActivationFunctionType
AX = mybir.AxisListType
F32 = mybir.dt.float32
BF16 = mybir.dt.bfloat16
I32 = mybir.dt.int32
U32 = mybir.dt.uint32

D = 1024
KD = D // 128
TP, NB, NT = 256, 8, 4
TS = NB * NT
T = TP + TS
TILES = [(0, 128), (128, 128), (256, 32)]
G5, P5, C5 = 16, 64, 16
J5 = G5 * P5 // 128
RC = 8.0
H, DK = 4, 128
NE, TOPK, FF = 32, 4, 1024
NPAIR = NE // 2
SLOTS = 64
SWEEPS = -(-T // SLOTS)
EPS = 1e-5
CH = 4096

U0, XR0, GR0, Q0, K0, V0, O0, GI0 = 0, 256, 512, 768, 1280, 1792, 2304, 2816
VEC = {}
_row = 0
for _name, _n in (("norm1_g", 8), ("s5_d", 2), ("s5_glu_b", 2), ("rg_conv_w", 8), ("rg_conv_b", 2), ("rg_ba", 2),
                  ("rg_bx", 2), ("rg_lambda", 2), ("ml_norm_g", 4), ("s5_lambda_re", 8), ("s5_lambda_im", 8)):
    VEC[_name] = (_row, _n)
    _row += _n
NVEC = _row

ORDER = (["vec"] + [f"hT{i}" for i in range(6)] + ["u0", "u1", "xr0", "xr1", "gates", "par", "bt", "ct",
         "gr0", "gr1", "q0", "q1", "bu0r", "bu0i", "bu1r", "bu1i", "q2", "q3", "k0", "k1", "r0", "r1", "i0", "i1",
         "k2", "k3", "va0", "va1", "va2", "bu2r", "bu2i", "bu3r", "bu3i",
         "vb0", "vb1", "vb2", "oa0", "oa1", "oa2", "bu4r", "bu4i", "bu5r", "bu5i",
         "ob0", "ob1", "ob2", "bu6r", "bu6i", "bu7r", "bu7i", "rows", "mb0", "st0", "mb1", "st1", "mb2", "st2",
         "kt0", "kt1", "kt2", "mb3", "st3", "dec"] + [f"sc{h}" for h in range(H)] + ["rgT", "s5T", "cp0", "cp1",
         "nu00", "nu01", "nu10", "nu11", "nu20", "nu21", "wo00", "nT", "wo01", "wo2", "wo10", "wo11", "h2T0", "h2T1",
         "h2T4", "h2T5", "lg", "h2T2", "h2T3", "cum"])
FILLS = {}
for _i, _n in enumerate(ORDER):
    FILLS[_n] = (_i % 6, _i // 6)
CB = [(0, 3), (3, 6), (6, 8)]
for _i, _n in enumerate(["ys0", "ys1", "glu0", "glu1"] + [f"cu{h}{g}" for h in range(H) for g in range(len(CB))]
                        + [f"yT{h}" for h in range(H)]):
    FILLS[_n] = (6 + _i % 2, _i // 2)
SAID = {
    "dve_said": [("nst_set", 1), ("xn_ready", 3), ("angle_reduced", 1), ("bb_ready", 4), ("cb_ready", 2),
        ("gate_abs", 1), ("rg_decay", 1), ("m_rows", 1), ("gate_rows", 1), ("xc_ready", 2), ("scm_ready", 8),
        ("s5_scanned", 4), ("rg_ratio", 1), ("rgfin_ready", 1), ("gate_poly", 1), ("s5_scanned", 4),
        ("mix_ready", 1), ("ones_ready", 1), ("wsm_ready", 1), ("e_arg", 4), ("s5_poly", 1), ("qm_ready", 1),
        ("s5_gelu", 1), ("den_read", 3), ("nvar_ready", 1), ("y3_ready", 4), ("rg_used", 1), ("c_new", 4),
        ("x1_added", 1), ("x2_ready", 1), ("x1_added", 1), ("x2_ready", 1), ("x1_added", 1), ("x2_ready", 1),
        ("top_diff", 1), ("mask_ready", 1), ("count_ready", 1)],
    "act_said": [("ms_ready", 1), ("root_ready", 1), ("ms_ready", 1), ("root_ready", 1), ("ms_ready", 1),
        ("root_ready", 1), ("step_ready", 1), ("mag_ready", 1), ("act_rg", 2), ("angle_ready", 2), ("gate_exp", 1),
        ("xp_ready", 2), ("wc_ready", 1), ("bias_rounded", 1), ("gate_rows_exp", 3), ("bias_rounded", 1),
        ("v_half", 2), ("rg_tanh", 2), ("rg_a", 2), ("v_half", 2), ("bias_rounded", 1), ("rg_root", 1),
        ("o_half", 2), ("bias_rounded", 1), ("gate_tanh", 1), ("o_half", 2), ("rtok_ready", 1), ("bias_rounded", 1),
        ("e_exp", 4), ("s5_tanh", 1), ("rg_staged", 2), ("s5_staged", 1), ("nsq_ready", 12), ("nroot_ready", 1),
        ("c_prompt", 2), ("bias_ready", 1), ("n_staged", 1), ("ms2_ready", 1), ("root2_ready", 1), ("ms2_ready", 1),
        ("root2_ready", 1), ("ms2_ready", 1), ("root2_ready", 1), ("top_exp", 1)],
    "pool_said": [("ident_ready", 1), ("weights_zero", 1), ("bb_zero", 1), ("seg_ready", 1), ("causal_ready", 1),
        ("sel4_ready", 1), ("ind_ready", 1), ("rows_zero", 1), ("table_ready", 1), ("e_zero", 1), ("s5_turned", 2),
        ("bias_rest", 1), ("s5_turned", 1), ("bias_rest", 1), ("s5_turned", 3), ("bias_rest", 1), ("s5_turned", 2),
        ("kw_ready", 1), ("vw_ready", 4), ("bias_rest", 1), ("c_decayed", 4)],
    "pe_said": [("xn_used", 1), ("w_in_used", 2), ("cb_used", 1), ("w_in_used", 2), ("s5_used", 2), ("w_in_used", 1),
        ("s5_used", 2), ("w_in_used", 1), ("s5_used", 4), ("c0_used", 1), ("y_turned", 1), ("mlstm_done", 1),
        ("w_out_used", 1)],
}
SAID_BY, VALUES = {}, {}
for _line, _said in SAID.items():
    _at = 0
    for _name, _times in _said:
        for _ in range(_times):
            _at += 1
            SAID_BY[_name] = _line
            VALUES.setdefault(_name, []).append(_at)


def spread(v, axis, n):
    shape = list(v.shape)
    shape[axis] = n
    return v.broadcast_to(shape)


def build_program(nc, a, o):
    ctx = ExitStack()
    with ctx:
        def sb(name, shape, dt=F32):
            return ctx.enter_context(nc.sbuf_tensor(name, shape, dt))

        ring = sb("ring", [128, 6, CH])
        xn = sb("xn", [128, 3, D])
        x1 = sb("x1", [128, 3, D])
        bsplit = sb("bsplit", [128, 3 * D], BF16)
        ident = sb("ident", [128, 128])
        upper = sb("upper", [128, 128], BF16)
        ones_bf = sb("ones_bf", [128, 128], BF16)
        iota_e = sb("iota_e", [128, NE])
        iota_s = sb("iota_s", [128, SLOTS])
        half = sb("half", [128, 2, SLOTS])
        selid = sb("selid", [128, NPAIR + 1])
        cnt = sb("cnt", [128, 1], I32)
        st2 = sb("st2", [128, 16])
        psum = ctx.enter_context(nc.psum_tensor("psum", [128, 8, 512], F32))

        def carve(base, shape):
            region, at = base
            n = math.prod(shape[1:])
            v = region[0:shape[0], at:at + n]
            if len(shape) == 3:
                v = v.rearrange("p (x y) -> p x y", x=shape[1])
            if len(shape) == 4:
                v = v.rearrange("p (x y z) -> p x y z", x=shape[1], y=shape[2])
            base[1] += n
            assert base[1] <= region.shape[1], (shape, base[1])
            return v

        mx = ExitStack()

        def ms(name, shape, dt=F32):
            return mx.enter_context(nc.sbuf_tensor(name, shape, dt))

        tabc = ms("tabc", [128, 2, J5, T])
        tab_r, tab_i = tabc[:, 0], tabc[:, 1]
        uT = ms("uT", [128, 2, T])
        xpP = ms("xpP", [128, 2, 3 + TP])
        qT = ms("qT", [128, H, T])
        kT = ms("kT", [128, H, T])
        rgb = ms("rgb", [128, 5 * 2 * T])
        rb = [rgb[:], 0]
        xc, rr, ri, rt, gate = (carve(rb, [128, 2, T]) for _ in range(5))
        gsm = ms("gsm", [128, 8, T])
        causal = ms("causal", [128, 416])
        seg = ms("seg", [128, T])
        t_pool = ms("t_pool", [128, T])
        wC = ms("wC", [128, 4, 128])
        parT = ms("parT", [128, 256])
        sm = ms("sm", [128, 26, J5])
        sel4 = ms("sel4", [H, H, 128])
        scm = ms("scm", [H, NB, TS])
        gb = ms("gb", [H, 2])
        m0 = ms("m0", [H, NB])
        wsm = ms("wsm", [TS, H, NB])
        glw = ms("glw", [128, 2, 256])
        hT = ms("hT", [128, KD, T])
        t_dve = ms("t_dve", [128, T])
        vecs = ms("vecs", [128, 128])
        fin5 = ms("fin5", [128, 2, 1 + NB, J5])
        rsm = ms("rsm", [128, 64])
        dec = ms("dec", [128, H, NB])
        nbuf = ms("nbuf", [128, 36])
        rgfin = ms("rgfin", [128, 2, 9])
        cvfin = ms("cvfin", [128, 2, 27])
        nst = ms("nst", [128, 16])
        ra = [ring[:, 4:6, :].rearrange("p s n -> p (s n)"), 0]
        v_tok = carve(ra, [128, 3, H, 129])
        E = carve(ra, [128, H, 416])
        vw = carve(ra, [TS, H, NB, 129])
        rb = [ra[0], H * 129 * 3]
        pt1, pt2 = carve(rb, [128, J5, 128]), carve(rb, [128, J5, 128])
        b_in = carve(rb, [128, 2, J5, C5])
        b_t = carve(rb, [128, 2, J5, C5])
        BB = carve(rb, [128, 2 * J5, 2, C5])
        c_in = carve(rb, [128, 4, P5])
        CBk = carve(rb, [128, 4, 2 * P5])
        vrow, srow, prow = carve(rb, [128, 128]), carve(rb, [128, 128]), carve(rb, [128, 128])
        rb = [tabc[:].rearrange("p x j t -> p (x j t)"), 0]
        k_tok, kw, qm = carve(rb, [128, 3, 512]), carve(rb, [128, 2, H, 128]), carve(rb, [128, H, NB, TS])
        cP = carve(rb, [128, H, 129])
        rb = [ring[:, 0:2, :].rearrange("p s n -> p (s n)"), 0]
        c0 = carve(rb, [128, H * NB, 129]).rearrange("p (h b) v -> p h b v", h=H)
        rb = [ring[:, 3, :], 0]
        w_r, w_i, s_r, s_i = (carve(rb, [128, 2, T]) for _ in range(4))
        wB, wax = carve(rb, [128, 4, 128]), carve(rb, [128, 2, 2, 128])
        d0s, xpS, wgate = carve(rb, [128, J5, TS]), carve(rb, [128, 2, NB, 3 + NT]), carve(rb, [128, KD, 36])
        rb = [x1[:].rearrange("p i n -> p (i n)"), 0]
        bias_in = carve(rb, [128, 3 * D // 2])
        o_tok = carve(rb, [128, 3, 512])
        rb = [xn[:].rearrange("p i n -> p (i n)"), 3 * D - (T + 10 * 128)]
        rows, rtok, stage = carve(rb, [128, T]), carve(rb, [128, 3, 128]), carve(rb, [128, 7, 128])
        mx.close()

        ring_b = sb("ring_b", [128, 2, CH])
        acts = sb("acts", [128, 3 * 1024])
        rb = [acts[:], 0]
        h2T, rw, rbias = carve(rb, [128, KD, T]), carve(rb, [128, KD, NE]), carve(rb, [128, NE])
        rb = [acts[:], 0]
        gact, sg1, uact = (carve(rb, [128, 2, 512]) for _ in range(3))
        g2b, gfb = sb("g2b", [128, D]), sb("gfb", [128, D])
        lg = sb("lg", [128, 3, NE])
        top = sb("top", [128, 3, 8])
        topi = sb("topi", [128, 3, 8], U32)
        topf = sb("topf", [128, 3, 8])
        gk = sb("gk", [128, 3, 8])
        msk, gts, tmp3 = sb("msk", [128, 3, NE]), sb("gts", [128, 3, NE]), sb("tmp3", [128, 3, NE])
        mskb = sb("mskb", [128, 3, NE], BF16)
        slot = sb("slot", [128, NPAIR + 1, 3, 2])
        sgate = sb("sgate", [128, NPAIR + 1, 3, 2])
        selb = sb("selb", [128, 2, SLOTS], BF16)
        xg = sb("xg", [128, KD, 128])
        aT = sb("aT", [128, 8, 128])
        sgt = sb("sgt", [128, T])
        S = sb("S", [128, 3, 2, SLOTS])
        SG = sb("SG", [128, 3, 2, SLOTS])
        yb = sb("yb", [128, 2, 512])

        sems = {}

        def sem(name):
            if name not in sems:
                sems[name] = ctx.enter_context(nc.semaphore(name))
            return sems[name]

        counted = {}

        def at(name, n):
            return (sem(SAID_BY.get(name)), VALUES[name][n - 1]) if name in VALUES else (sem(name), n)

        def says_now(name):
            if name not in VALUES:
                return sem(name)
            line = SAID_BY[name]
            for k in (name, line):
                counted[k] = counted.get(k, 0) + 1
            assert counted[line] == VALUES[name][counted[name] - 1], (line, name)
            return sem(line)

        filled = [sem(f"filled{b}") for b in range(8)]
        drained = [sem(f"drained{b}") for b in range(8)]

        def bank(name):
            return psum[:, FILLS[name][0], :]

        def await_fill(eng, name):
            eng.wait_ge(filled[FILLS[name][0]], FILLS[name][1] + 1)

        def await_bank(pe, name):
            if FILLS[name][1]:
                pe.wait_ge(drained[FILLS[name][0]], FILLS[name][1])

        def ends_fill(ins, name):
            ins.then_inc(filled[FILLS[name][0]], 1)

        def vec(name, k=None):
            r, n = VEC[name]
            return vecs[:, r:r + n] if k is None else vecs[:, r + k:r + k + 1]

        ctx.enter_context(nc.allow_non_contiguous_dma(reason="a few rows of single values"))
        block = ctx.enter_context(nc.Block())

        def w_in_cols(c0_, n):
            return a["w_in"][0][:, c0_:c0_ + n].rearrange("(k p) n -> p k n", p=128)

        def slot_view(s, n):
            return ring[:, s, 0:KD * n].rearrange("p (k n) -> p k n", k=KD)

        WCH = [(U0, 512), (GR0, 512), (1024, 512), (1536, 512), (2048, 512), (2560, 256)]
        BLOCKS = 6
        DEPTH = 4

        def ring_slot(b, x):
            s = 2 * (b % DEPTH) + x
            return s, (ring[:, s, :] if s < 6 else ring_b[:, s - 6, :])

        VECTORS = [(name, a[name][0].rearrange("(k p) -> k p", p=128)) for name in
                   ("norm1_g", "s5_d", "s5_glu_b", "rg_conv_b", "rg_ba", "rg_bx", "rg_lambda", "ml_norm_g")]
        VECTORS += [("rg_conv_w", a["rg_conv_w"][0].rearrange("t (k p) -> (t k) p", p=128))]
        VECTORS += [(name, a[name][0].rearrange("(j g) p -> j (g p)", g=2)) for name in ("s5_lambda_re", "s5_lambda_im")]

        def load_vector(eng, name, src):
            r, n = VEC[name]
            eng.dma_start(vrow[r:r + n, :], src).then_inc(sem("vec_loaded"), 16)

        @block.sync
        def _(sp):
            def load_block(pair, b):
                which = b % BLOCKS
                late = []
                for x in range(2):
                    s, place = ring_slot(b, x)
                    if which < 4:
                        n0 = [0, FF, 512, FF + 512][which]
                        dst = place.rearrange("p (k n) -> p k n", k=KD)
                        src = a["exp_w1"][0][pair * 2 + x].rearrange("(k p) n -> p k n", p=128)[:, :, n0:n0 + 512]
                    else:
                        f0 = (which - 4) * 4
                        dst = place.rearrange("p (k n) -> p k n", k=4)
                        src = a["exp_w2"][0][pair * 2 + x].rearrange("(k p) n -> p k n", p=128)[:, f0:f0 + 4, :]
                    if which == 5:
                        late.append((dst[:, 2:4], src[:, 2:4]))
                        dst, src = dst[:, 0:2], src[:, 0:2]
                    sp.dma_start(dst, src).then_inc(sem(f"expert_chunk{s}"), 16)
                for dst, src in late:
                    sp.dma_start(dst, src).then_inc(sem("last_half"), 16)

            for i in range(2):
                sp.dma_start(xn[:, i, :], a["x_prompt"][0, 128 * i:128 * i + 128, :]).then_inc(sem(f"x_loaded{i}"), 16)
            sp.dma_start(xn[0:TS, 2, :], a["x_sample"].rearrange("b t n -> (b t) n")).then_inc(sem("x_loaded2"), 16)
            for name, src in VECTORS[4:]:
                load_vector(sp, name, src)
            for c in range(6):
                if c == 1:
                    for x, name in enumerate(("s5_b_re", "s5_b_im")):
                        for gg in range(2):
                            sp.dma_start(b_in[64 * gg:64 * gg + 64, x], a[name][0].rearrange("(j g) p c -> g p j c", g=2)[gg]).then_inc(sem("b_loaded"), 16)
                    for gg in range(2):
                        sp.dma_start(sm[64 * gg:64 * gg + 64, 0, :], spread(a["s5_log_step"][0:1].rearrange("l (j g) -> l g j", g=2)[:, gg, :], 0, 64)).then_inc(sem("step_loaded"), 16)
                    for x, name in enumerate(("s5_c_re", "s5_c_im")):
                        for tt in range(2):
                            sp.dma_start(c_in[:, 2 * x + tt, :], a[name][0, 8 * tt:8 * tt + 8].rearrange("g c p -> (g c) p")).then_inc(sem("c_loaded"), 16)
                    for x, name in enumerate(("state_s5_re", "state_s5_im")):
                        sp.dma_start(srow[64 * x:64 * x + 64, :], a[name][0].rearrange("b (j g) p -> (b j) (g p)", g=2)).then_inc(sem("par_loaded"), 16)
                    sp.dma_start(prow[0:32, :], a["state_ml_n"][0].rearrange("b h k -> (b h) k")).then_inc(sem("par_loaded"), 16)
                    sp.dma_start(prow[32:48, :], a["state_rg_h"][0].rearrange("b (x n) -> (b x) n", x=2)).then_inc(sem("par_loaded"), 16)
                    sp.dma_start(prow[48:96, :], a["state_rg_conv"][0].rearrange("b t (x n) -> (b t x) n", x=2)).then_inc(sem("par_loaded"), 16)
                    sp.dma_start(gb[:], a["ml_gate_bias"][0].rearrange("(x h) -> h x", x=2)).then_inc(sem("gb_loaded"), 16)
                    sp.dma_start(m0[:], a["state_ml_m"][0].rearrange("b h -> h b")).then_inc(sem("gb_loaded"), 16)
                    sp.dma_start(glw[:], a["s5_glu_w"][0].rearrange("(k p) n -> p k n", p=128)).then_inc(sem("glw_loaded"), 16)
                    sp.wait_ge(*at("weights_zero", 1))
                    for x in range(2):
                        sp.dma_start(wgate[:, :, 32 * x:32 * x + H], w_in_cols(GI0 + H * x, H)).then_inc(sem("wgate_loaded"), 16)
                if c == 3:
                    for x, name in enumerate(("rg_wa", "rg_wx")):
                        for n in range(8):
                            q = slice(32 * (n % 4), 32 * (n % 4) + 32)
                            sp.dma_start(wax[q, x, n // 4, q], a[name][0, n]).then_inc(sem("wax_loaded"), 16)
                if c >= 3:
                    sp.wait_ge(*at("w_in_used", c - 2))
                sp.dma_start(slot_view(c % 3, WCH[c][1]), w_in_cols(*WCH[c])).then_inc(sem(f"w_in{c}"), 16)
            sp.wait_ge(*at("w_in_used", 5))
            for h in range(H):
                sp.dma_start(c0[:, h, :, 0:128], a["state_ml_c"][0, :, h].rearrange("b k v -> k b v")).then_inc(sem("c0_loaded"), 16)
            sp.dma_start(o[8].rearrange("l b h -> (l h) b"), gsm[0:H, 7, TP - 1:TP]).then_inc(sem("m_stored"), 16)
            sp.dma_start(o[15][0].rearrange("b h -> h b"), gsm[0:H, 7, TP + NT - 1:T:NT]).then_inc(sem("m_stored"), 16)
            sp.wait_ge(*at("w_in_used", 6))
            for n in range(2):
                if n == 1:
                    sp.wait_ge(*at("s5_used", J5))
                sp.dma_start(slot_view(2 + n, 512), a["w_out"][0][:, n * 512:(n + 1) * 512].rearrange(
                    "(k p) n -> p k n", p=128)).then_inc(sem(f"w_out{n}"), 16)
            sp.wait_ge(*at("rg_staged", 2))
            sp.dma_start(o[4][0, 0].rearrange("(a x n) -> a x n", a=1, x=2), stage[0:1, 1:3, :]).then_inc(sem("stored"), 16)
            sp.dma_start(o[11][0].rearrange("b (x n) -> b x n", x=2), stage[1:9, 1:3, :]).then_inc(sem("stored"), 16)
            sp.dma_start(o[5][0, 0].rearrange("t (x n) -> t x n", x=2), stage[0:3, 3:5, :]).then_inc(sem("stored"), 16)
            sp.dma_start(o[12][0].rearrange("b t (x n) -> (b t) x n", x=2), stage[3:27, 3:5, :]).then_inc(sem("stored"), 16)
            sp.wait_ge(*at("s5_staged", 1))
            for x in range(2):
                src = stage[:, 5 + x, :]
                sp.dma_start(o[2 + x][0, 0].rearrange("(j g) p -> j (g p)", g=2), src[0:J5, :]).then_inc(sem("stored"), 16)
                sp.dma_start(o[9 + x][0].rearrange("b (j g) p -> (b j) (g p)", g=2), src[J5:9 * J5, :]).then_inc(sem("stored"), 16)
            sp.wait_ge(*at("c_prompt", 2))
            sp.dma_start(o[6][0, 0].rearrange("h k v -> k h v"), cP[:, :, 0:128]).then_inc(sem("cp_stored"), 16)
            sp.wait_ge(*at("y_turned", 1))
            sp.wait_ge(*at("bias_ready", 1))
            sp.dma_start(x1[:, 0:2, :], a["x_prompt"][0].rearrange("(i p) n -> p i n", p=128)).then_inc(sem("x1_loaded"), 16)
            sp.dma_start(x1[0:TS, 2, :], a["x_sample"].rearrange("b t n -> (b t) n")).then_inc(sem("x1_loaded"), 16)
            for h in range(H):
                sp.wait_ge(*at("c_new", h + 1))
                sp.dma_start(o[13][0, :, h].rearrange("b k v -> k b v"), c0[:, h, :, 0:128]).then_inc(sem("c_stored"), 16)
            sp.wait_ge(*at("mlstm_done", 1))
            sp.wait_ge(sem("m_stored"), 32)
            sp.dma_start(g2b[:], spread(a["norm2_g"][0:1, :], 0, 128)).then_inc(sem("router_loaded"), 16)
            sp.dma_start(rw[:], a["router_w"][0].rearrange("(k p) e -> p k e", p=128)).then_inc(sem("router_loaded"), 16)
            sp.dma_start(rbias[:], spread(a["router_b"][0:1, :], 0, 128)).then_inc(sem("router_loaded"), 16)
            load_block(0, 2)
            sp.wait_ge(sem("cp_stored"), 16)
            sp.wait_ge(*at("rg_used", 1))
            load_block(0, 3)
            sp.wait_ge(*at("n_staged", 1))
            sp.dma_start(o[14][0].rearrange("b h k -> (b h) k"), stage[0:32, 0, :]).then_inc(sem("stored"), 16)
            sp.dma_start(o[7][0, 0], stage[32:36, 0, :]).then_inc(sem("stored"), 16)
            sp.wait_ge(sem("c_stored"), 64)
            load_block(0, 0)
            stored = 16 * 10
            sp.wait_ge(*at("w_out_used", 1))
            load_block(0, 1)
            sp.wait_ge(sem("stored"), stored)
            sp.dma_start(gfb[:], spread(a["final_norm_g"].rearrange("(a n) -> a n", a=1), 0, 128)).then_inc(sem("gf_loaded"), 16)
            for b in range(DEPTH, 2 * BLOCKS):
                sp.wait_ge(sem("block_done"), b + 1 - DEPTH)
                load_block(b // BLOCKS, b)
            with sp.Fori(1, NPAIR // 2) as q:
                for b in range(2 * BLOCKS):
                    sp.wait_ge(sem("block_done"), q * (2 * BLOCKS) + (b + 1 - DEPTH))
                    load_block(q * 2 + b // BLOCKS, b)
            sp.wait_ge(*at("count_ready", 1))
            most = sp.value_load(cnt[0:1, 0:1], min_val=0, max_val=T)
            with sp.If(most > SLOTS):
                with sp.Fori(1, SWEEPS) as r:
                    with sp.If(most > r * SLOTS):
                        with sp.Fori(0, NPAIR // 2) as q:
                            for b in range(2 * BLOCKS):
                                sp.wait_ge(sem("block_done"), r * (NPAIR * BLOCKS) + q * (2 * BLOCKS) + (b + 1 - DEPTH))
                                load_block(q * 2 + b // BLOCKS, b)
            for i in range(2):
                sp.wait_ge(sem("y_final"), i + 1)
                sp.dma_start(o[0][0, 128 * i:128 * i + 128, :], x1[:, i, :]).then_inc(sem("stored"), 16)
            sp.wait_ge(sem("y_final"), 3)
            sp.dma_start(o[1].rearrange("b t n -> (b t) n"), x1[0:TS, 2, :]).then_inc(sem("stored"), 16)
            sp.wait_ge(sem("stored"), stored + 48)

        @block.gpsimd
        def _(pool):
            n_self = [0]

            def po(ins, name=None):
                if name is None:
                    n_self[0] += 1
                    ins.then_inc(sem("pool_self"), 1)
                    pool.wait_ge(sem("pool_self"), n_self[0])
                else:
                    ins.then_inc(says_now(name), 1)

            g = nc.gpsimd
            po(g.memset(ident[:], 0.0))
            po(g.affine_select(out=ident[:], in_=ident[:], compare_op=ALU.not_equal, fill=1.0, base=0,
                               pattern=[[-1, 128]], channel_multiplier=1), "ident_ready")
            po(g.memset(wgate[:], 0.0))
            po(g.memset(wax[:], 0.0), "weights_zero")
            g.memset(BB[:], 0.0).then_inc(says_now("bb_zero"), 1)
            po(g.memset(seg[:], 1.0))
            po(g.memset(seg[:, 0:1], 0.0))
            po(g.memset(seg[:, TP:T:NT], 0.0), "seg_ready")
            po(g.memset(causal[:], 1.0))
            for c in (0, 256):
                po(g.affine_select(out=causal[:, c:c + 128], in_=causal[:, c:c + 128], compare_op=ALU.is_ge, fill=0.0,
                                   base=0, pattern=[[1, 128]], channel_multiplier=-1))
            po(g.affine_select(out=causal[:, 384:416], in_=causal[:, 384:416], compare_op=ALU.is_ge, fill=0.0,
                               base=0, pattern=[[1, TS]], channel_multiplier=-1))
            cs = causal[:, 384:416].rearrange("p (b t) -> p b t", b=NB)
            po(g.affine_select(out=cs, in_=cs, compare_op=ALU.is_ge, fill=0.0, base=0, pattern=[[-NT, NB], [0, NT]],
                               channel_multiplier=1), "causal_ready")
            po(g.memset(sel4[:], 0.0))
            po(g.affine_select(out=sel4[:], in_=sel4[:], compare_op=ALU.not_equal, fill=1.0, base=0,
                               pattern=[[-1, H], [0, 128]], channel_multiplier=1), "sel4_ready")
            po(g.memset(scm[:], 0.0))
            po(g.memset(wsm[:], 1.0))
            po(g.affine_select(out=wsm[:], in_=wsm[:], compare_op=ALU.is_ge, fill=0.0, base=0,
                               pattern=[[0, H], [-NT, NB]], channel_multiplier=1))
            po(g.affine_select(out=wsm[:], in_=wsm[:], compare_op=ALU.is_ge, fill=0.0, base=NT - 1,
                               pattern=[[0, H], [NT, NB]], channel_multiplier=-1), "ind_ready")
            po(g.iota(iota_e[:], pattern=[[1, NE]], base=0, channel_multiplier=0, allow_small_or_imprecise_dtypes=True))
            po(g.iota(iota_s[:], pattern=[[1, SLOTS]], base=0, channel_multiplier=0, allow_small_or_imprecise_dtypes=True))
            po(g.iota(half[:], pattern=[[1, 2], [0, SLOTS]], base=0, channel_multiplier=0, allow_small_or_imprecise_dtypes=True))
            for x in range(3):
                po(g.iota(selid[32 * x:32 * x + 32, :], pattern=[[-2, NPAIR + 1]], base=0, channel_multiplier=1,
                          allow_small_or_imprecise_dtypes=True))
            po(g.memset(ones_bf[:], 1.0))
            po(g.affine_select(out=upper[:], in_=ones_bf[:], compare_op=ALU.is_ge, fill=0.0, base=0,
                               pattern=[[1, 128]], channel_multiplier=-1))
            bias_cols = [[("exp_b1", 0, 1536, 0)], [("exp_b1", 1536, 512, 0), ("exp_b2", 0, 1024, 512)]]

            def load_bias(part):
                for x in range(3):
                    for name, c_, n_, at_ in bias_cols[part]:
                        pool.dma_start(bias_in[32 * x:32 * x + 32, at_:at_ + n_], a[name][0][:, c_:c_ + n_]).then_inc(sem("bias_loaded"), 16)

            def bias_rest(part, step):
                pool.wait_ge(*at("bias_rounded", 3 * part + step + 1))
                r = slice(0, 96 if step == 0 else 32)
                po(g.tensor_tensor(bias_in[r], bias_in[r], bsplit[r, 1536 * part:1536 * part + 1536], ALU.subtract), "bias_rest")

            pool.wait_ge(*at("ms_ready", 3))
            load_bias(0)
            pool.wait_ge(*at("xn_used", 1))
            po(g.memset(rows[:], 0.0), "rows_zero")
            pool.wait_ge(*at("angle_ready", 2))
            po(g.memset(tab_r[:, :, 0:1], 1.0))
            po(g.memset(tab_i[:, :, 0:1], 0.0))
            po(g.tensor_copy(tab_r[:, :, 1:2], sm[:, 6, :].unsqueeze(2)))
            po(g.tensor_copy(tab_i[:, :, 1:2], sm[:, 7, :].unsqueeze(2)))
            pr, pi, q1, q2, q3 = sm[:, 20, :], sm[:, 21, :], sm[:, 22, :], sm[:, 23, :], sm[:, 24, :]
            po(g.tensor_copy(pr, sm[:, 6, :]))
            po(g.tensor_copy(pi, sm[:, 7, :]))
            n = 2
            while n < TP:
                po(g.tensor_tensor(q1, pr, pr, ALU.mult))
                po(g.tensor_tensor(q2, pi, pi, ALU.mult))
                po(g.tensor_tensor(q3, pr, pi, ALU.mult))
                po(g.tensor_tensor(pr, q1, q2, ALU.subtract))
                po(g.tensor_tensor(pi, q3, q3, ALU.add))
                prb, pib = (spread(v.unsqueeze(2), 2, n) for v in (pr, pi))
                po(g.tensor_tensor(pt1[:, :, 0:n], tab_r[:, :, 0:n], prb, ALU.mult))
                po(g.tensor_tensor(pt2[:, :, 0:n], tab_i[:, :, 0:n], pib, ALU.mult))
                po(g.tensor_tensor(tab_r[:, :, n:2 * n], pt1[:, :, 0:n], pt2[:, :, 0:n], ALU.subtract))
                po(g.tensor_tensor(pt1[:, :, 0:n], tab_r[:, :, 0:n], pib, ALU.mult))
                po(g.tensor_tensor(pt2[:, :, 0:n], tab_i[:, :, 0:n], prb, ALU.mult))
                po(g.tensor_tensor(tab_i[:, :, n:2 * n], pt1[:, :, 0:n], pt2[:, :, 0:n], ALU.add))
                n *= 2
            for k, tb in enumerate((tab_r, tab_i)):
                for j in range(J5):
                    ins = g.tensor_copy(tb[:, j, TP:T].rearrange("p (b t) -> p b t", b=NB),
                                        spread(tb[:, j, 0:NT].unsqueeze(1), 1, NB))
            po(ins, "table_ready")
            pool.wait_ge(*at("table_ready", 1))
            po(g.memset(E[:], 0.0), "e_zero")
            for j in range(J5):
                pool.wait_ge(*at("s5_scanned", j + 1))
                if j >= 2:
                    pool.wait_ge(*at("s5_used", j - 1))
                b = j % 2
                po(g.tensor_tensor(s_r[:, b, :], tab_r[:, j, :], w_r[:, b, :], ALU.mult))
                po(g.tensor_tensor(t_pool[:], tab_i[:, j, :], w_i[:, b, :], ALU.mult))
                po(g.tensor_tensor(s_r[:, b, :], s_r[:, b, :], t_pool[:], ALU.subtract))
                po(g.tensor_tensor(s_i[:, b, :], tab_i[:, j, :], w_r[:, b, :], ALU.mult))
                po(g.tensor_tensor(t_pool[:], tab_r[:, j, :], w_i[:, b, :], ALU.mult))
                po(g.tensor_tensor(s_i[:, b, :], s_i[:, b, :], t_pool[:], ALU.add))
                for x, s in enumerate((s_r, s_i)):
                    g.tensor_copy(fin5[:, x, 0, j:j + 1], s[:, b, TP - 1:TP])
                    ins = g.tensor_copy(fin5[:, x, 1:, j:j + 1], s[:, b, TP + NT - 1:T:NT].unsqueeze(2))
                po(ins, "s5_turned")
                if j == 1:
                    bias_rest(0, 0)
                if j == 2:
                    bias_rest(0, 1)
                if j == 3:
                    pool.wait_ge(*at("bias_rounded", 3))
                    load_bias(1)
                if j == 5:
                    bias_rest(1, 0)
            for i in range(3):
                b, f = FILLS[f"kt{i}"]
                pool.wait_ge(drained[b], f + 1)
            pool.wait_ge(*at("rtok_ready", 1))
            pool.wait_ge(drained[FILLS["rows"][0]], FILLS["rows"][1] + 1)
            pool.wait_ge(*at("s5_turned", J5))
            po(g.tensor_tensor(kw[:], k_tok[:, 0:2, :].rearrange("p i (h k) -> p i h k", h=H),
                               spread(rtok[:, 0:2, 64:64 + H].unsqueeze(3), 3, DK), ALU.mult), "kw_ready")
            pool.wait_ge(*at("wsm_ready", 1))
            pool.wait_ge(*at("cb_used", 1))
            for n in ("va2", "vb2"):
                b, f = FILLS[n]
                pool.wait_ge(drained[b], f + 1)
            pool.wait_ge(*at("ones_ready", 1))
            for h in range(H):
                po(g.tensor_tensor(vw[:, h], spread(v_tok[0:TS, 2, h, :].unsqueeze(1), 1, NB),
                                   spread(wsm[:, h, :].unsqueeze(2), 2, 129), ALU.mult), "vw_ready")
            bias_rest(1, 1)
            pool.wait_ge(*at("c0_used", 1))
            b, f = FILLS["dec"]
            pool.wait_ge(drained[b], f + 1)
            for h in range(H):
                g.tensor_tensor(c0[:, h], c0[:, h], spread(dec[:, h, :].unsqueeze(2), 2, 129),
                                ALU.mult).then_inc(says_now("c_decayed"), 1)

        @block.scalar
        def _(act):
            A = nc.scalar.activation

            def copy_out(name, out, view, scale=1.0, signal=None):
                await_fill(act, name)
                nc.scalar.activation(out, view, ACT.Copy, scale=scale).then_inc(drained[FILLS[name][0]], 1)

            for name, src in VECTORS[:4]:
                load_vector(act, name, src)
            act.wait_ge(*at("nst_set", 1))
            for i, (t0, n) in enumerate(TILES):
                act.wait_ge(sem(f"x_loaded{i}"), 16)
                A(x1[0:n, i, :], xn[0:n, i, :], ACT.Square, accum_out=nst[0:n, i:i + 1]).then_inc(says_now("ms_ready"), 1)
                act.wait_ge(*at("ms_ready", i + 1))
                A(nst[:, 4 + i:5 + i], nst[:, i:i + 1], ACT.Sqrt, scale=1.0 / D, bias=nst[:, 8:9]).then_inc(says_now("root_ready"), 1)
            await_fill(act, "vec")
            A(vecs[:, 0:NVEC], bank("vec")[:, 0:NVEC], ACT.Copy).then_inc(drained[FILLS["vec"][0]], 1)
            act.wait_ge(drained[FILLS["vec"][0]], 1)
            act.wait_ge(sem("step_loaded"), 32)
            A(sm[:, 1, :], sm[:, 0, :], ACT.Exp).then_inc(says_now("step_ready"), 1)
            act.wait_ge(*at("angle_reduced", 1))
            A(sm[:, 5, :], sm[:, 2, :], ACT.Exp).then_inc(says_now("mag_ready"), 1)
            A(rsm[:, 0:2], vec("rg_lambda"), ACT.Abs).then_inc(says_now("act_rg"), 1)
            act.wait_ge(*at("act_rg", 1))
            A(rsm[:, 0:2], rsm[:, 0:2], ACT.Exp, scale=-1.0).then_inc(says_now("act_rg"), 1)
            A(sm[:, 6, :], sm[:, 9, :], ACT.Sin).then_inc(says_now("angle_ready"), 1)
            A(sm[:, 7, :], sm[:, 8, :], ACT.Sin).then_inc(says_now("angle_ready"), 1)
            for x in range(2):
                copy_out(f"u{x}", uT[:, x, :], bank(f"u{x}")[:, 0:T])
            act.wait_ge(*at("gate_abs", 1))
            A(gsm[0:H, 2, :], gsm[0:H, 2, :], ACT.Exp, scale=-1.0).then_inc(says_now("gate_exp"), 1)
            for x in range(2):
                await_fill(act, f"xr{x}")
                A(xpP[:, x, 3:], bank(f"xr{x}")[:, 0:TP], ACT.Copy).then_inc(says_now("xp_ready"), 1)
                A(xpS[:, x, :, 3:], bank(f"xr{x}")[:, TP:T].rearrange("p (b t) -> p b t", b=NB), ACT.Copy).then_inc(drained[FILLS[f"xr{x}"][0]], 1)
            copy_out("par", parT[:, 0:224], bank("par")[:, 0:224])
            def bias_round(part, step):
                if step == 0:
                    act.wait_ge(sem("bias_loaded"), 48 + 96 * part)
                else:
                    act.wait_ge(*at("bias_rest", 2 * part + step))
                r = slice(0, (96, 64, 32)[step])
                last = part == 1 and step == 2
                A(bsplit[r, 1536 * part:1536 * part + 1536], bias_in[r], ACT.Copy).then_inc(
                    says_now("bias_ready" if last else "bias_rounded"), 1)

            copy_out("bt", wB[:], bank("bt").rearrange("p (x n) -> p x n", x=4))
            await_fill(act, "ct")
            A(wC[:, 0:2, :], bank("ct")[:, 0:256].rearrange("p (x n) -> p x n", x=2), ACT.Copy).then_inc(says_now("wc_ready"), 1)
            A(wC[:, 2:4, :], bank("ct")[:, 256:512].rearrange("p (x n) -> p x n", x=2), ACT.Copy, scale=-1.0).then_inc(drained[FILLS["ct"][0]], 1)
            for x in range(2):
                copy_out(f"gr{x}", gate[:, x, :], bank(f"gr{x}")[:, 0:T])
            for h in range(2):
                copy_out(f"q{h}", qT[:, h, :], bank(f"q{h}")[:, 0:T])
            bias_round(0, 0)
            act.wait_ge(*at("gate_rows", 1))
            act.wait_ge(*at("rows_zero", 1))
            A(rows[32:32 + H, :], gsm[0:H, 7, :], ACT.Exp, scale=-1.0).then_inc(says_now("gate_rows_exp"), 1)
            A(rows[64:64 + H, :], gsm[0:H, 5, :], ACT.Exp).then_inc(says_now("gate_rows_exp"), 1)
            A(gsm[0:H, 6, 0:TS + NB], gsm[0:H, 6, 0:TS + NB], ACT.Exp).then_inc(says_now("gate_rows_exp"), 1)
            for h in range(2, H):
                copy_out(f"q{h}", qT[:, h, :], bank(f"q{h}")[:, 0:T])
            for h in range(2):
                copy_out(f"k{h}", kT[:, h, :], bank(f"k{h}")[:, 0:T], scale=DK ** -0.5)
            for x in range(2):
                await_fill(act, f"r{x}")
                A(rr[:, x, :], bank(f"r{x}")[:, 0:T], ACT.Sigmoid, bias=vec("rg_ba", x)).then_inc(drained[FILLS[f"r{x}"][0]], 1)
            for x in range(2):
                await_fill(act, f"i{x}")
                A(ri[:, x, :], bank(f"i{x}")[:, 0:T], ACT.Sigmoid, bias=vec("rg_bx", x)).then_inc(drained[FILLS[f"i{x}"][0]], 1)
            for h in range(2, H):
                copy_out(f"k{h}", kT[:, h, :], bank(f"k{h}")[:, 0:T], scale=DK ** -0.5)

            def v_out(name, i, n, c):
                await_fill(act, name)
                if i < 2:
                    A(v_tok[0:n, i, 2 * c:2 * c + 2, 0:128], bank(name)[0:n, 0:256].rearrange("p (h v) -> p h v", h=2), ACT.Copy).then_inc(
                        drained[FILLS[name][0]], 1)
                else:
                    A(v_tok[0:n, i, 2 * c, 0:128], bank(name)[0:n, 0:128], ACT.Copy).then_inc(says_now("v_half"), 1)
                    A(v_tok[0:n, i, 2 * c + 1, 0:128], bank(name)[n:2 * n, 0:128], ACT.Copy).then_inc(says_now("v_half"), 1)
                    act.wait_ge(*at("v_half", 2 * c + 2))
                    act.sem_inc(drained[FILLS[name][0]], 1)

            def o_out(name, i, n, c):
                await_fill(act, name)
                if i < 2:
                    A(o_tok[0:n, i, 256 * c:256 * c + 256], bank(name)[0:n, 0:256], ACT.Sigmoid).then_inc(drained[FILLS[name][0]], 1)
                else:
                    for x in range(2):
                        A(o_tok[0:n, i, 256 * c + 128 * x:256 * c + 128 * x + 128], bank(name)[n * x:n * x + n, 0:128],
                          ACT.Sigmoid).then_inc(says_now("o_half"), 1)
                    act.wait_ge(*at("o_half", 2 * c + 2))
                    act.sem_inc(drained[FILLS[name][0]], 1)

            bias_round(0, 1)
            for i, (t0, n) in enumerate(TILES):
                v_out(f"va{i}", i, n, 0)
            act.wait_ge(*at("rg_decay", 1))
            for x in range(2):
                act.wait_ge(drained[FILLS["r1"][0]], FILLS["r1"][1] + 1)
                act.wait_ge(drained[FILLS["r0"][0]], FILLS["r0"][1] + 1)
                A(rt[:, x, :], rr[:, x, :], ACT.Tanh, scale=rsm[:, 4 + x:5 + x]).then_inc(says_now("rg_tanh"), 1)
            act.wait_ge(*at("rg_tanh", 2))
            for x in range(2):
                A(rr[:, x, :], rr[:, x, :], ACT.Exp, scale=rsm[:, 6 + x:7 + x]).then_inc(says_now("rg_a"), 1)
            for i, (t0, n) in enumerate(TILES):
                v_out(f"vb{i}", i, n, 1)
            bias_round(0, 2)
            act.wait_ge(*at("rg_ratio", 1))
            A(rt[:], rt[:], ACT.Sqrt).then_inc(says_now("rg_root"), 1)
            for i, (t0, n) in enumerate(TILES):
                o_out(f"oa{i}", i, n, 0)
            bias_round(1, 0)
            act.wait_ge(*at("gate_poly", 1))
            A(rt[:], rt[:], ACT.Tanh, scale=math.sqrt(2.0 / math.pi)).then_inc(says_now("gate_tanh"), 1)
            for i, (t0, n) in enumerate(TILES):
                o_out(f"ob{i}", i, n, 1)
            act.wait_ge(*at("ones_ready", 1))
            await_fill(act, "rows")
            A(rtok[:, 0:2, :], bank("rows")[:, 0:256].rearrange("p (i n) -> p i n", i=2), ACT.Copy).then_inc(says_now("rtok_ready"), 1)
            A(rtok[0:TS, 2, :], bank("rows")[0:TS, 256:384], ACT.Copy).then_inc(drained[FILLS["rows"][0]], 1)
            bias_round(1, 1)
            for h in range(H):
                if h == 3:
                    act.wait_ge(*at("s5_turned", J5))
                    for i, (t0, n) in enumerate(TILES):
                        copy_out(f"kt{i}", k_tok[0:n, i, :], bank(f"kt{i}")[0:n, :])
                act.wait_ge(*at("e_arg", h + 1))
                A(E[:, h, :], E[:, h, :], ACT.Exp, scale=-1.0).then_inc(says_now("e_exp"), 1)
            copy_out("dec", dec[:], bank("dec")[:, 0:H * NB].rearrange("p (h b) -> p h b", h=H))
            act.wait_ge(*at("s5_poly", 1))
            A(rt[:], rt[:], ACT.Tanh, scale=math.sqrt(2.0 / math.pi)).then_inc(says_now("s5_tanh"), 1)
            await_fill(act, "rgT")
            A(stage[0:9, 1:3, :], bank("rgT")[0:9, 0:256].rearrange("p (x n) -> p x n", x=2), ACT.Copy).then_inc(says_now("rg_staged"), 1)
            A(stage[0:27, 3:5, :], bank("rgT")[0:27, 256:512].rearrange("p (x n) -> p x n", x=2), ACT.Copy).then_inc(says_now("rg_staged"), 1)
            act.wait_ge(*at("rg_staged", 2))
            act.sem_inc(drained[FILLS["rgT"][0]], 1)
            await_fill(act, "s5T")
            A(stage[0:72, 5:7, :], bank("s5T")[0:72, 0:256].rearrange("p (x n) -> p x n", x=2), ACT.Copy).then_inc(says_now("s5_staged"), 1)
            act.wait_ge(*at("s5_staged", 1))
            act.sem_inc(drained[FILLS["s5T"][0]], 1)
            for hh in range(2):
                await_fill(act, f"cp{hh}")
                A(cP[:, 2 * hh:2 * hh + 2, :], bank(f"cp{hh}")[:, 0:258].rearrange("p (h v) -> p h v", h=2), ACT.Copy).then_inc(drained[FILLS[f"cp{hh}"][0]], 1)
            for i, (t0, n) in enumerate(TILES):
                act.wait_ge(*at("den_read", i + 1))
                for hh in range(2):
                    await_fill(act, f"nu{i}{hh}")
                    if hh or i:
                        act.wait_ge(*at("nsq_ready", 4 * i + 2 * hh))
                    for x in range(2):
                        A(t_dve[0:n, 128 * x:128 * x + 128], bank(f"nu{i}{hh}")[0:n, 129 * x:129 * x + 128], ACT.Square,
                          accum_out=rsm[0:n, 16 + 4 * i + 2 * hh + x:17 + 4 * i + 2 * hh + x]).then_inc(says_now("nsq_ready"), 1)
            act.wait_ge(*at("nvar_ready", 1))
            A(rsm[:, 32:44], rsm[:, 32:44], ACT.Sqrt).then_inc(says_now("nroot_ready"), 1)
            for x in range(2):
                await_fill(act, f"glu{x}")
                A(ri[:, x, :], bank(f"glu{x}")[:, 0:T], ACT.Sigmoid, bias=vec("s5_glu_b", x)).then_inc(drained[FILLS[f"glu{x}"][0]], 1)
            for hh in range(2):
                b, f = FILLS[f"cp{hh}"]
                act.wait_ge(drained[b], f + 1)
            for hh in range(2):
                A(nbuf[:, 32 + 2 * hh:34 + 2 * hh], cP[:, 2 * hh:2 * hh + 2, 128], ACT.Copy).then_inc(says_now("c_prompt"), 1)
            bias_round(1, 2)
            for h in range(H):
                await_fill(act, f"yT{h}")
                A(hT[:, 4 + h, :], bank(f"yT{h}")[:, 0:T], ACT.Copy, scale=vec("ml_norm_g", h)).then_inc(drained[FILLS[f"yT{h}"][0]], 1)
            await_fill(act, "nT")
            A(stage[0:36, 0, :], bank("nT")[0:36, 0:128], ACT.Copy).then_inc(says_now("n_staged"), 1)
            act.wait_ge(*at("n_staged", 1))
            act.sem_inc(drained[FILLS["nT"][0]], 1)
            for m, i in enumerate((0, 2, 1)):
                t0, n = TILES[i]
                act.wait_ge(*at("x1_added", m + 1))
                if i == 2:
                    act.wait_ge(sem("stored"), 16 * 10)
                A(xn[0:n, i, :], x1[0:n, i, :], ACT.Square, accum_out=st2[0:n, i:i + 1]).then_inc(says_now("ms2_ready"), 1)
                act.wait_ge(*at("ms2_ready", m + 1))
                A(st2[0:n, 4 + i:5 + i], st2[0:n, i:i + 1], ACT.Sqrt, scale=1.0 / D, bias=st2[0:n, 12:13]).then_inc(says_now("root2_ready"), 1)
                for hf in range(2):
                    name = f"h2T{2 * i + hf}"
                    copy_out(name, h2T[:, 4 * hf:4 * hf + 4, t0:t0 + n],
                             bank(name)[:, 0:4 * 128].rearrange("p (k n) -> p k n", k=4)[:, :, 0:n])
            act.wait_ge(*at("top_diff", 1))
            A(gk[:, :, 0:TOPK], gk[:, :, 0:TOPK], ACT.Exp).then_inc(says_now("top_exp"), 1)

            def gathered(g1):
                for x in range(2):
                    act.wait_ge(sem("gather_ready"), g1 * 2 - 1 + x)
                    A(xg[:, 4 * x:4 * x + 4, :], psum[:, 6 + x, :].rearrange("p (k n) -> p k n", k=4), ACT.Copy).then_inc(sem("xg_copied"), 1)

            def pair_steps(gp):
                for x in range(2):
                    act.wait_ge(sem("g_clipped"), gp * 2 + 1 + x)
                    A(sg1[:, x, :], gact[:, x, :], ACT.Sigmoid, scale=1.702).then_inc(sem("sig_ready"), 1)
                gathered_at = gp * 2 + 2
                for x in range(2):
                    act.wait_ge(sem("gather_ready"), gathered_at + 1 + x)
                    A(xg[:, 4 * x:4 * x + 4, :], psum[:, 6 + x, :].rearrange("p (k n) -> p k n", k=4), ACT.Copy).then_inc(sem("xg_copied"), 1)
                for x in range(2):
                    act.wait_ge(sem("aT_ready"), gp * 2 + 1 + x)
                    A(aT[:, 4 * x:4 * x + 4, :], psum[:, x, :].rearrange("p (k n) -> p k n", k=4), ACT.Copy).then_inc(sem("aT_copied"), 1)
                act.wait_ge(sem("sgt_ready"), gp + 1)
                A(sgt[:], psum[:, 6, 0:T], ACT.Copy).then_inc(sem("sgt_copied"), 1)
                act.wait_ge(sem("block_done"), gp * BLOCKS + 6)
                for x in range(2):
                    A(yb[:, x, :], psum[:, 4 + x, :], ACT.Copy).then_inc(sem("y_copied"), 1)

            def sweep(base):
                with act.Fori(0, NPAIR // 2) as q:
                    for u in range(2):
                        pair_steps(base + q * 2 + u)

            gathered(1)
            sweep(0)
            act.wait_ge(*at("count_ready", 1))
            most = act.value_load(cnt[0:1, 0:1], min_val=0, max_val=T)
            with act.If(most > SLOTS):
                with act.Fori(1, SWEEPS) as r:
                    with act.If(most > r * SLOTS):
                        g1 = r * (NPAIR + 1)
                        for x in range(2):
                            act.wait_ge(sem("regather_ready"), r * 2 - 1 + x)
                            A(xg[:, 4 * x:4 * x + 4, :], psum[:, 6 + x, :].rearrange("p (k n) -> p k n", k=4), ACT.Copy).then_inc(sem("xg_recopied"), 1)
                        sweep(r * NPAIR)
            act.wait_ge(sem("sums_done"), 1)
            for i, (t0, n) in enumerate(TILES):
                A(xn[0:n, i, :], x1[0:n, i, :], ACT.Square, accum_out=st2[0:n, i:i + 1]).then_inc(sem("ms3_ready"), 1)
                act.wait_ge(sem("ms3_ready"), i + 1)
                A(st2[0:n, 4 + i:5 + i], st2[0:n, i:i + 1], ACT.Sqrt, scale=1.0 / D, bias=st2[0:n, 12:13]).then_inc(sem("root3_ready"), 1)

        @block.vector
        def _(dve):
            n_self = [0]
            V = nc.vector

            def dv(ins, s=None, value=None):
                if s is None:
                    n_self[0] += 1
                    ins.then_inc(sem("dve_self"), 1)
                    dve.wait_ge(sem("dve_self"), n_self[0])
                else:
                    ins.then_inc(s, 1)

            def drains(ins, name):
                b, n = FILLS[name]
                ins.then_inc(drained[b], 1)
                dve.wait_ge(drained[b], n + 1)

            def says(ins, name, n):
                ins.then_inc(says_now(name), 1)
                dve.wait_ge(*at(name, n))

            TT, TSC, STT = V.tensor_tensor, V.tensor_scalar, V.scalar_tensor_tensor

            def log1p(out, y, tmp1, tmp2):
                dv(TSC(tmp1, y, 2.0, None, ALU.add))
                dv(V.reciprocal(tmp1, tmp1))
                dv(TT(tmp1, tmp1, y, ALU.mult))
                dv(TT(tmp2, tmp1, tmp1, ALU.mult))
                dv(TSC(out, tmp2, 1.0 / 19.0, None, ALU.mult))
                for k in range(8, 0, -1):
                    dv(STT(out=out, in0=out, scalar=1.0 / (2 * k + 1), in1=tmp2, op0=ALU.add, op1=ALU.mult))
                dv(STT(out=out, in0=out, scalar=1.0, in1=tmp1, op0=ALU.add, op1=ALU.mult))
                dv(TSC(out, out, 2.0, None, ALU.mult))

            dv(V.memset(st2[:], 1.0))
            dv(V.memset(st2[:, 12:13], EPS))
            dv(V.memset(nst[:], 1.0))
            says(V.memset(nst[:, 8:9], EPS), "nst_set", 1)
            for i, (t0, n) in enumerate(TILES):
                dve.wait_ge(*at("root_ready", i + 1))
                dv(V.reciprocal(nst[:, 4 + i:5 + i], nst[:, 4 + i:5 + i]))
                says(TSC(xn[0:n, i, :], xn[0:n, i, :], nst[0:n, 4 + i:5 + i], None, ALU.mult), "xn_ready", i + 1)
            dve.wait_ge(drained[FILLS["vec"][0]], 1)
            for k in range(6):
                i, hf = k // 2, k % 2
                t0, n = TILES[i]
                await_fill(dve, f"hT{k}")
                drains(TT(hT[:, 4 * hf:4 * hf + 4, t0:t0 + n], bank(f"hT{k}").rearrange("p (k n) -> p k n", k=4)[:, :, 0:n],
                          spread(vec("norm1_g")[:, 4 * hf:4 * hf + 4].unsqueeze(2), 2, n), ALU.mult), f"hT{k}")
            lr, li = vec("s5_lambda_re"), vec("s5_lambda_im")
            dve.wait_ge(*at("step_ready", 1))
            dv(TT(sm[:, 2, :], lr, sm[:, 1, :], ALU.mult))
            dv(TT(sm[:, 3, :], li, sm[:, 1, :], ALU.mult))
            magic = 12582912.0
            dv(TSC(sm[:, 4, :], sm[:, 3, :], 1.0 / (2 * math.pi), None, ALU.mult))
            dv(TSC(sm[:, 4, :], sm[:, 4, :], magic, None, ALU.add))
            dv(TSC(sm[:, 4, :], sm[:, 4, :], magic, None, ALU.subtract))
            p1, p2 = 6.28125, 0.0019350051879882812
            p3 = 2 * math.pi - p1 - p2
            dv(STT(out=sm[:, 8, :], in0=sm[:, 4, :], scalar=-p1, in1=sm[:, 3, :], op0=ALU.mult, op1=ALU.add))
            dv(STT(out=sm[:, 8, :], in0=sm[:, 4, :], scalar=-p2, in1=sm[:, 8, :], op0=ALU.mult, op1=ALU.add))
            dv(STT(out=sm[:, 8, :], in0=sm[:, 4, :], scalar=-p3, in1=sm[:, 8, :], op0=ALU.mult, op1=ALU.add))
            dv(TSC(sm[:, 8, :], sm[:, 8, :], 3.1415925, -3.1415925, ALU.min, ALU.max))
            dv(STT(out=sm[:, 9, :], in0=sm[:, 8, :], scalar=-1.0, in1=sm[:, 8, :], op0=ALU.mult, op1=ALU.min))
            says(TSC(sm[:, 9, :], sm[:, 9, :], math.pi / 2, None, ALU.add), "angle_reduced", 1)
            dve.wait_ge(*at("mag_ready", 1))
            dve.wait_ge(*at("angle_ready", 2))
            mag = sm[:, 5, :]
            dv(TT(sm[:, 10, :], mag, sm[:, 6, :], ALU.mult))
            dv(TT(sm[:, 11, :], mag, sm[:, 7, :], ALU.mult))
            dv(TT(sm[:, 14, :], lr, lr, ALU.mult))
            dv(TT(sm[:, 15, :], li, li, ALU.mult))
            dv(TT(sm[:, 14, :], sm[:, 14, :], sm[:, 15, :], ALU.add))
            dv(V.reciprocal(sm[:, 14, :], sm[:, 14, :]))
            dv(TSC(sm[:, 15, :], sm[:, 10, :], -1.0, None, ALU.add))
            dv(TT(sm[:, 16, :], sm[:, 15, :], lr, ALU.mult))
            dv(TT(sm[:, 17, :], sm[:, 11, :], li, ALU.mult))
            dv(TT(sm[:, 12, :], sm[:, 16, :], sm[:, 17, :], ALU.add))
            dv(TT(sm[:, 12, :], sm[:, 12, :], sm[:, 14, :], ALU.mult))
            dv(TT(sm[:, 16, :], sm[:, 11, :], lr, ALU.mult))
            dv(TT(sm[:, 17, :], sm[:, 15, :], li, ALU.mult))
            dv(TT(sm[:, 13, :], sm[:, 16, :], sm[:, 17, :], ALU.subtract))
            dv(TT(sm[:, 13, :], sm[:, 13, :], sm[:, 14, :], ALU.mult))
            dve.wait_ge(sem("b_loaded"), 64)
            dve.wait_ge(*at("bb_zero", 1))
            zr, zi = (spread(sm[:, k, :].unsqueeze(2), 2, C5) for k in (12, 13))
            for x, (za, zb, op) in enumerate(((zr, zi, ALU.subtract), (zi, zr, ALU.add))):
                dv(TT(b_t[:, 0], b_in[:, 0], za, ALU.mult))
                dv(TT(b_t[:, 1], b_in[:, 1], zb, ALU.mult))
                for gg in range(2):
                    q = slice(64 * gg, 64 * gg + 64)
                    says(TT(BB[q, x * J5:(x + 1) * J5, gg, :], b_t[q, 0], b_t[q, 1], op), "bb_ready", 2 * x + gg + 1)
            dve.wait_ge(sem("c_loaded"), 64)
            par_i = cvfin[:, 0, 0:2].bitcast(I32)
            dv(V.tensor_reduce(cvfin[:, 1, 0:1], ident[:], AX.X, ALU.add))
            for gg in range(2):
                dv(V.tensor_reduce(rsm[:, 10 + gg:11 + gg],
                                   ident[:].rearrange("p (j g c) -> p g j c", g=2, c=C5)[:, gg], AX.XY, ALU.add))
            for gg in range(2):
                says(TSC(CBk[:, :, 64 * gg:64 * gg + 64], c_in[:], rsm[:, 10 + gg:11 + gg], None, ALU.mult), "cb_ready", gg + 1)
            ig, fg, ge, s3, s4, wd, sd, mt = (gsm[0:H, k, :] for k in range(8))
            dve.wait_ge(sem("gb_loaded"), 32)
            await_fill(dve, "gates")
            dv(TSC(ig, bank("gates")[0:H, 0:T], gb[:, 0:1], None, ALU.add))
            drains(V.tensor_copy(fg, bank("gates")[32:32 + H, 0:T]), "gates")
            dv(TSC(fg, fg, gb[:, 1:2], None, ALU.add))
            says(STT(out=ge, in0=fg, scalar=-1.0, in1=fg, op0=ALU.mult, op1=ALU.max), "gate_abs", 1)
            dve.wait_ge(*at("act_rg", 2))
            log1p(rsm[:, 2:4], rsm[:, 0:2], rsm[:, 8:10], rsm[:, 12:14])
            dv(TSC(rsm[:, 8:10], vec("rg_lambda"), -1.0, 0.0, ALU.mult, ALU.max))
            dv(TT(rsm[:, 2:4], rsm[:, 2:4], rsm[:, 8:10], ALU.add))
            dv(TSC(rsm[:, 4:6], rsm[:, 2:4], RC, None, ALU.mult))
            says(TSC(rsm[:, 6:8], rsm[:, 2:4], -RC, None, ALU.mult), "rg_decay", 1)
            dve.wait_ge(*at("gate_exp", 1))
            log1p(s3, ge, s4, wd)
            dv(TSC(fg, fg, 0.0, None, ALU.min))
            dv(TT(fg, fg, s3, ALU.subtract))
            dve.wait_ge(*at("seg_ready", 1))
            dve.wait_ge(*at("rows_zero", 1))
            bb, aa, mm = s3, rows[0:H, :], s4
            dv(V.tensor_tensor_scan(bb, seg[0:H, :], fg, 0.0, ALU.mult, ALU.add))
            dv(TT(aa, ig, bb, ALU.subtract))
            dv(V.tensor_tensor_scan(mm[:, 0:TP], aa[:, 0:TP], aa[:, 0:TP], 0.0, ALU.max, ALU.max))
            dv(TT(mm[:, TP:T:NT], aa[:, TP:T:NT], m0[:], ALU.max))
            for t in range(1, NT):
                dv(TT(mm[:, TP + t:T:NT], aa[:, TP + t:T:NT], mm[:, TP + t - 1:T:NT], ALU.max))
            says(TT(mt, bb, mm, ALU.add), "m_rows", 1)
            dv(TSC(wd[:, 0:TP], aa[:, 0:TP], mm[:, TP - 1:TP], None, ALU.subtract))
            mlast = mm[:, TP + NT - 1:T:NT]
            by_b = lambda v: v.rearrange("p (b t) -> p b t", b=NB)
            dv(TT(by_b(wd[:, TP:T]), by_b(aa[:, TP:T]), spread(mlast.unsqueeze(2), 2, NT), ALU.subtract))
            dv(TT(by_b(sd[:, 0:TS]), spread(m0[:].unsqueeze(2), 2, NT), by_b(mm[:, TP:T]), ALU.subtract))
            says(TT(sd[:, TS:TS + NB], m0[:], mlast, ALU.subtract), "gate_rows", 1)
            ip = FILLS["par"]
            dve.wait_ge(drained[ip[0]], ip[1] + 1)
            dv(V.memset(xpP[:, :, 0:3], 0.0))
            for x in range(2):
                dv(V.tensor_copy(xpS[:, x, :, 0:3], parT[:, 128 + 48:128 + 96].rearrange("p (b t x) -> p x b t", t=3, x=2)[:, x]))
            s0 = [parT[:, 64 * x:64 * x + 64].rearrange("p (b j) -> p b j", b=NB) for x in range(2)]
            ar, ai = (spread(sm[:, k, :].unsqueeze(1), 1, NB) for k in (10, 11))
            as5 = [stage[:, x, 0:64].rearrange("p (b j) -> p b j", b=NB) for x in range(4)]
            dv(TT(as5[0], s0[0], ar, ALU.mult))
            dv(TT(as5[1], s0[1], ai, ALU.mult))
            dv(TT(as5[2], as5[0], as5[1], ALU.subtract))
            dv(TT(as5[0], s0[1], ar, ALU.mult))
            dv(TT(as5[1], s0[0], ai, ALU.mult))
            dv(TT(as5[3], as5[0], as5[1], ALU.add))
            dv(TT(d0s[:], spread(seg[:, TP:T].unsqueeze(1), 1, J5), spread(mag.unsqueeze(2), 2, TS), ALU.mult))
            for x in range(2):
                fx = FILLS[f"xr{x}"]
                dve.wait_ge(*at("xp_ready", x + 1))
                dve.wait_ge(drained[fx[0]], fx[1] + 1)
                cw = lambda t: vec("rg_conv_w", 2 * t + x)
                outs = (xc[:, x, 0:TP], by_b(xc[:, x, TP:T]))
                ins = (lambda t: xpP[:, x, t:t + TP], lambda t: xpS[:, x, :, t:t + NT])
                for k in range(2):
                    dv(TSC(outs[k], ins[k](0), cw(0), vec("rg_conv_b", x), ALU.mult, ALU.add))
                for t in range(1, 4):
                    for k in range(2):
                        ins_ = STT(out=outs[k], in0=ins[k](t), scalar=cw(t), in1=outs[k], op0=ALU.mult, op1=ALU.add)
                        if t == 3 and k == 1:
                            says(ins_, "xc_ready", x + 1)
                        else:
                            dv(ins_)
            for x in range(2):
                dv(V.tensor_copy(cvfin[:, x, 0:3], xpP[:, x, TP:TP + 3]))
                dv(V.tensor_copy(cvfin[:, x, 3:27].rearrange("p (b t) -> p b t", b=NB), xpS[:, x, :, NT:NT + 3]))
            dve.wait_ge(*at("gate_rows_exp", 3))
            dve.wait_ge(*at("ind_ready", 1))
            for b in range(NB):
                V.tensor_copy(scm[:, b, NT * b:NT * b + NT], sd[:, NT * b:NT * b + NT]).then_inc(says_now("scm_ready"), 1)
            def s5_scan(j):
                b = j % 2
                if j == 0:
                    dve.wait_ge(*at("table_ready", 1))
                if j >= 2:
                    dve.wait_ge(*at("s5_turned", j - 1))
                for n in (f"bu{j}r", f"bu{j}i"):
                    await_fill(dve, n)
                br, bi = bank(f"bu{j}r")[:, 0:T], bank(f"bu{j}i")[:, 0:T]
                dv(TT(w_r[:, b, :], br, tab_r[:, j, :], ALU.mult))
                dv(TT(t_dve[:], bi, tab_i[:, j, :], ALU.mult))
                dv(TT(w_r[:, b, :], w_r[:, b, :], t_dve[:], ALU.add))
                drains(TT(w_i[:, b, :], bi, tab_r[:, j, :], ALU.mult), f"bu{j}i")
                drains(TT(t_dve[:], br, tab_i[:, j, :], ALU.mult), f"bu{j}r")
                dv(TT(w_i[:, b, :], w_i[:, b, :], t_dve[:], ALU.subtract))
                for x, w in enumerate((w_r, w_i)):
                    dv(TT(w[:, b, TP:T:NT], w[:, b, TP:T:NT], as5[2 + x][:, :, j], ALU.add))
                for x, w in enumerate((w_r, w_i)):
                    dv(V.tensor_tensor_scan(w[:, b, 0:TP], spread(mag[:, j:j + 1], 1, TP), w[:, b, 0:TP], 0.0, ALU.mult, ALU.add))
                    ins_ = V.tensor_tensor_scan(w[:, b, TP:T], d0s[:, j, :], w[:, b, TP:T], 0.0, ALU.mult, ALU.add)
                    if x == 0:
                        dv(ins_)
                    else:
                        says(ins_, "s5_scanned", j + 1)

            s5_scan(0)
            s5_scan(1)
            for x in range(2):
                f1 = FILLS[f"i{x}"]
                dve.wait_ge(drained[f1[0]], f1[1] + 1)
            dv(TT(xc[:], xc[:], ri[:], ALU.mult))
            s5_scan(2)
            s5_scan(3)
            dve.wait_ge(*at("rg_tanh", 2))
            dv(TSC(ri[:], rt[:], 1.0, None, ALU.add))
            dv(V.reciprocal(ri[:], ri[:]))
            says(STT(out=rt[:], in0=rt[:], scalar=2.0, in1=ri[:], op0=ALU.mult, op1=ALU.mult), "rg_ratio", 1)
            dve.wait_ge(*at("rg_a", 2))
            dve.wait_ge(*at("rg_root", 1))
            dv(TT(xc[:], xc[:], rt[:], ALU.mult))
            h0 = parT[:, 128 + 32:128 + 48].rearrange("p (b x) -> p x b", x=2)
            dv(TT(rsm[:, 48:64].rearrange("p (x b) -> p x b", x=2), rr[:, :, TP:T:NT], h0, ALU.mult))
            dv(TT(xc[:, :, TP:T:NT], xc[:, :, TP:T:NT], rsm[:, 48:64].rearrange("p (x b) -> p x b", x=2), ALU.add))
            dv(TT(rr[:], rr[:], spread(seg[:].unsqueeze(1), 1, 2), ALU.mult))
            for x in range(2):
                dv(V.tensor_tensor_scan(ri[:, x, :], rr[:, x, :], xc[:, x, :], 0.0, ALU.mult, ALU.add))
            dv(V.tensor_copy(rgfin[:, :, 0:1], ri[:, :, TP - 1:TP]))
            says(V.tensor_copy(rgfin[:, :, 1:9], ri[:, :, TP + NT - 1:T:NT]), "rgfin_ready", 1)

            def gelu_arg(y, tmp, name):
                dv(TT(tmp, y, y, ALU.mult))
                dv(TSC(tmp, tmp, 0.044715, 1.0, ALU.mult, ALU.add))
                says(TT(tmp, tmp, y, ALU.mult), name, 1)

            gelu_arg(gate[:], rt[:], "gate_poly")
            s5_scan(4)
            s5_scan(5)
            dve.wait_ge(*at("gate_tanh", 1))
            dv(STT(out=gate[:], in0=rt[:], scalar=1.0, in1=gate[:], op0=ALU.add, op1=ALU.mult))
            s5_scan(6)
            s5_scan(7)
            dve.wait_ge(*at("w_in_used", 6))
            says(STT(out=hT[:, 2:4, :], in0=gate[:], scalar=0.5, in1=ri[:], op0=ALU.mult, op1=ALU.mult), "mix_ready", 1)
            says(V.memset(v_tok[:, :, :, 128:129], 1.0), "ones_ready", 1)
            dve.wait_ge(*at("e_zero", 1))
            dve.wait_ge(*at("causal_ready", 1))
            fr = FILLS["rows"]
            dve.wait_ge(drained[fr[0]], fr[1] + 1)
            dve.wait_ge(*at("rtok_ready", 1))
            dve.wait_ge(*at("ind_ready", 1))
            dv(TT(wsm[:], wsm[:], spread(rtok[0:TS, 2, 64:64 + H].unsqueeze(2), 2, NB), ALU.mult), says_now("wsm_ready"))

            def e_arg(h):
                await_fill(dve, f"mb{h}")
                mb = bank(f"mb{h}")
                dv(TSC(E[:, h, 0:256], mb[:, 0:256], rtok[:, 0, h:h + 1], 0.0, ALU.subtract, ALU.max))
                dv(TSC(E[:, h, 256:384], mb[:, 128:256], rtok[:, 1, h:h + 1], 0.0, ALU.subtract, ALU.max))
                drains(TSC(E[0:TS, h, 384:416], mb[0:TS, 256:288], rtok[0:TS, 2, h:h + 1], 0.0, ALU.subtract, ALU.max), f"mb{h}")
                dve.sem_inc(says_now("e_arg"), 1)

            def e_prob(h):
                dve.wait_ge(*at("e_exp", h + 1))
                dv(TT(E[:, h, :], E[:, h, :], causal[:], ALU.mult))
                await_fill(dve, f"st{h}")
                dv(TT(E[:, h, 0:384], bank(f"st{h}")[:, 0:384], E[:, h, 0:384], ALU.mult))
                drains(TT(E[0:TS, h, 384:416], bank(f"st{h}")[0:TS, 384:416], E[0:TS, h, 384:416], ALU.mult), f"st{h}")

            for h in range(H):
                e_arg(h)
                e_prob(h)
            for x in range(2):
                await_fill(dve, f"ys{x}")
                drains(STT(out=xc[:, x, :], in0=uT[:, x, :], scalar=vec("s5_d", x), in1=bank(f"ys{x}")[:, 0:T],
                           op0=ALU.mult, op1=ALU.add), f"ys{x}")
            gelu_arg(xc[:], rt[:], "s5_poly")
            dve.wait_ge(sem("c0_loaded"), 64)
            dv(V.tensor_copy(c0[:, :, :, 128], parT[:, 128:160].rearrange("p (b h) -> p h b", h=H)))
            dve.wait_ge(*at("s5_turned", J5))
            for h in range(H):
                await_fill(dve, f"sc{h}")
                drains(TT(qm[:, h], bank(f"sc{h}")[:, 0:NB * TS].rearrange("p (b t) -> p b t", b=NB),
                          spread(qT[:, h, TP:T].unsqueeze(1), 1, NB), ALU.mult), f"sc{h}")
            dve.sem_inc(says_now("qm_ready"), 1)
            dve.wait_ge(*at("s5_tanh", 1))
            dv(STT(out=rt[:], in0=rt[:], scalar=1.0, in1=xc[:], op0=ALU.add, op1=ALU.mult))
            says(TSC(rt[:], rt[:], 0.5, None, ALU.mult), "s5_gelu", 1)
            dv(V.memset(rsm[:, 16:28], 1.0))
            dv(V.memset(rsm[:, 48:60], 1.0))
            rc, rv = rsm[:, 48:60], rsm[:, 32:44]
            for i, (t0, n) in enumerate(TILES):
                for hh in range(2):
                    await_fill(dve, f"nu{i}{hh}")
                    den, out = bank(f"nu{i}{hh}")[0:n, 128:258:129], rc[0:n, 4 * i + 2 * hh:4 * i + 2 * hh + 2]
                    dv(V.tensor_copy(out, den))
                    dv(STT(out=out, in0=den, scalar=-1.0, in1=out, op0=ALU.mult, op1=ALU.max))
                    ins_ = TT(out, out, rtok[0:n, i, 32 + 2 * hh:34 + 2 * hh], ALU.max)
                    says(ins_, "den_read", i + 1) if hh else dv(ins_)
            dv(V.reciprocal(rc, rc))

            def new_memory(h):
                dve.wait_ge(*at("c_decayed", h + 1))
                for gidx, (b0, b1) in enumerate(CB):
                    name = f"cu{h}{gidx}"
                    await_fill(dve, name)
                    drains(TT(c0[:, h, b0:b1, :], c0[:, h, b0:b1, :],
                              bank(name)[:, 0:(b1 - b0) * 129].rearrange("p (b v) -> p b v", v=129), ALU.add), name)
                says(V.tensor_copy(nbuf[:, 0:32].rearrange("p (b h) -> p h b", h=H)[:, h, :], c0[:, h, :, 128]), "c_new", h + 1)

            dve.wait_ge(*at("nsq_ready", 12))
            dv(TT(rv, rc, rc, ALU.mult))
            dv(TT(rv, rv, rsm[:, 16:28], ALU.mult))
            says(TSC(rv, rv, 1.0 / DK, EPS, ALU.mult, ALU.add), "nvar_ready", 1)
            dve.wait_ge(*at("nroot_ready", 1))
            dv(V.reciprocal(rv, rv))
            dv(TT(rv, rv, rc, ALU.mult))
            for h in range(H):
                for i, (t0, n) in enumerate(TILES):
                    name = f"nu{i}{h // 2}"
                    ot = o_tok[0:n, i, 128 * h:128 * h + 128]
                    ins_ = STT(out=ot, in0=bank(name)[0:n, 129 * (h % 2):129 * (h % 2) + 128], scalar=rv[0:n, 4 * i + h:4 * i + h + 1],
                               in1=ot, op0=ALU.mult, op1=ALU.mult)
                    if h % 2:
                        drains(ins_, name)
                    else:
                        dv(ins_)
                dve.sem_inc(says_now("y3_ready"), 1)
            for x in range(2):
                fgl = FILLS[f"glu{x}"]
                dve.wait_ge(drained[fgl[0]], fgl[1] + 1)
            says(TT(hT[:, 0:2, :], rt[:], ri[:], ALU.mult), "rg_used", 1)
            for h in range(H):
                new_memory(h)
            dve.wait_ge(sem("x1_loaded"), 32)
            for m, i in enumerate((0, 2, 1)):
                t0, n = TILES[i]
                if i < 2:
                    for c in range(2):
                        name = f"wo{i}{c}"
                        await_fill(dve, name)
                        xs = x1[0:n, i, 512 * c:512 * c + 512]
                        drains(TT(xs, xs, bank(name)[0:n, :], ALU.add), name)
                else:
                    await_fill(dve, "wo2")
                    for c in range(4):
                        xs = x1[0:n, i, 256 * c:256 * c + 256]
                        ins_ = TT(xs, xs, bank("wo2")[n * c:n * c + n, 0:256], ALU.add)
                        drains(ins_, "wo2") if c == 3 else dv(ins_)
                dve.sem_inc(says_now("x1_added"), 1)
                sq = st2[0:n, 4 + i:5 + i]
                dve.wait_ge(*at("root2_ready", m + 1))
                dv(V.reciprocal(sq, sq))
                if i == 0:
                    dve.wait_ge(sem("router_loaded"), 48)
                says(STT(out=xn[0:n, i, :], in0=x1[0:n, i, :], scalar=sq, in1=g2b[0:n, :],
                         op0=ALU.mult, op1=ALU.mult), "x2_ready", m + 1)
            dv(V.memset(lg[:], 0.0))
            dv(V.memset(slot[:], -1.0))
            dv(V.memset(sgate[:], 0.0))
            dv(V.memset(yb[:], 0.0))
            dv(V.memset(sgt[:], 0.0))
            await_fill(dve, "lg")
            lgp = bank("lg")[:, 0:96].rearrange("p (i e) -> p i e", i=3)
            dv(TT(lg[:, 0:2, :], lgp[:, 0:2, :], spread(rbias[:].unsqueeze(1), 1, 2), ALU.add))
            drains(TT(lg[0:TS, 2, :], lgp[0:TS, 2, :], rbias[0:TS, :], ALU.add), "lg")
            for i in range(3):
                dv(V.max(top[:, i, :], lg[:, i, :]))
                dv(V.max_index(topi[:, i, :], top[:, i, :], lg[:, i, :]))
            dv(V.tensor_copy(topf[:], topi[:]))
            says(TT(gk[:, :, 0:TOPK], top[:, :, 0:TOPK], spread(top[:, :, 0:1], 2, TOPK), ALU.subtract), "top_diff", 1)
            dve.wait_ge(*at("top_exp", 1))
            dv(V.tensor_reduce(gk[:, :, 4:5], gk[:, :, 0:TOPK], AX.X, ALU.add))
            dv(V.reciprocal(gk[:, :, 4:5], gk[:, :, 4:5]))
            dv(TT(gk[:, :, 0:TOPK], gk[:, :, 0:TOPK], spread(gk[:, :, 4:5], 2, TOPK), ALU.mult))
            dve.wait_ge(*at("bias_ready", 1))
            ie = spread(iota_e[:].unsqueeze(1), 1, 3)
            for k in range(TOPK):
                of = lambda v: spread(v[:, :, k:k + 1], 2, NE)
                if k == 0:
                    dv(TT(msk[:], ie, of(topf), ALU.is_equal))
                    dv(TT(gts[:], msk[:], of(gk), ALU.mult))
                else:
                    dv(TT(tmp3[:], ie, of(topf), ALU.is_equal))
                    dv(TT(msk[:], msk[:], tmp3[:], ALU.add))
                    dv(TT(tmp3[:], tmp3[:], of(gk), ALU.mult))
                    dv(TT(gts[:], gts[:], tmp3[:], ALU.add))
            says(V.tensor_copy(mskb[:], msk[:]), "mask_ready", 1)
            await_fill(dve, "cum")
            cp = bank("cum")[:, 0:96].rearrange("p (i e) -> p i e", i=3)
            dv(TT(tmp3[:, 0:2, :], cp[:, 0:2, :], msk[:, 0:2, :], ALU.mult))
            dv(TT(tmp3[0:TS, 2, :], cp[0:TS, 2, :], msk[0:TS, 2, :], ALU.mult))
            dv(V.tensor_reduce(st2[:, 8:9], bank("cum")[:, 96:128], AX.X, ALU.max))
            says(V.tensor_copy(cnt[:], st2[:, 8:9]), "count_ready", 1)
            for i, (t0, n) in enumerate(TILES):
                pairs = lambda v: v[0:n, 0:NPAIR, i, :]
                src = lambda v: v[0:n, i, :].rearrange("p (q x) -> p q x", x=2)
                dv(TSC(pairs(slot), src(tmp3), -1.0, None, ALU.add))
                dv(V.tensor_copy(pairs(sgate), src(gts)))

            def wide(v, p):
                return spread(v[:, bass.ds(p, 1), :, :].rearrange("p a i x -> p (a i) x").unsqueeze(3), 3, SLOTS)

            slots4 = spread(spread(iota_s[:].unsqueeze(1).unsqueeze(1), 1, 3), 2, 2)

            def select(p):
                return TT(S[:], wide(slot, p), slots4, ALU.is_equal)

            def select_bias(p):
                return TSC(selb[0:96], half[0:96], selid[0:96, bass.ds(p, 1)], None, ALU.is_equal)

            def add_combined(c):
                i, nn = c // 2, c % 2
                n = TILES[i][1]
                dst = x1[0:n, i, 512 * nn:512 * nn + 512]
                return TT(dst, dst, psum[0:n, 6 + c % 2, :], ALU.add)

            STEPS = 6

            def pair_steps(p, gp, extra):
                k = [0]

                def dl(ins):
                    k[0] += 1
                    ins.then_inc(sem("dve_loop"), 1)
                    dve.wait_ge(sem("dve_loop"), gp * STEPS + k[0])

                dve.wait_ge(sem("sgt_ready"), gp)
                dl(TT(SG[:], S[:], wide(sgate, p), ALU.mult))
                dve.sem_inc(sem("sg_ready"), 1)
                dve.wait_ge(sem("gather_ready"), gp * 2 + 2)
                dl(select(p + 1))
                dve.sem_inc(sem("s_ready"), 1)
                for x in range(2):
                    for c in (range(0, 2) if x == 0 else range(4, 6)):
                        dve.wait_ge(sem("combine_ready"), gp * 6 + c + 1 + extra * 6)
                        add_combined(c).then_inc(sem("combine_added"), 1)
                    dve.wait_ge(sem("block_done"), gp * BLOCKS + 2 * x + 1)
                    dve.wait_ge(sem("aT_ready"), gp * 2 - 0) if x == 0 else None
                    TSC(gact[:, x, :], psum[:, 2 * x, :], 7.0, None, ALU.min).then_inc(sem("g_clipped"), 1)
                    if x == 0:
                        for c in range(2, 4):
                            dve.wait_ge(sem("combine_ready"), gp * 6 + c + 1 + extra * 6)
                            add_combined(c).then_inc(sem("combine_added"), 1)
                    dve.wait_ge(sem("block_done"), gp * BLOCKS + 2 * x + 2)
                    dl(TSC(uact[:, x, :], psum[:, 2 * x + 1, :], 7.0, -7.0, ALU.min, ALU.max))
                    dve.wait_ge(sem("g_clipped"), gp * 2 + 1 + x)
                    dl(STT(out=uact[:, x, :], in0=uact[:, x, :], scalar=1.0, in1=gact[:, x, :], op0=ALU.add, op1=ALU.mult))
                    dve.wait_ge(sem("sig_ready"), gp * 2 + 1 + x)
                    TT(gact[:, x, :], uact[:, x, :], sg1[:, x, :], ALU.mult).then_inc(sem("act_ready"), 1)
                dve.wait_ge(sem("bias_used"), gp + 1)
                select_bias(p + 1).then_inc(sem("selb_ready"), 1)
                assert k[0] == STEPS

            def sweep(base, extra):
                with dve.Fori(0, NPAIR // 2) as q:
                    for u in range(2):
                        pair_steps(q * 2 + u, base + q * 2 + u, extra)
                for c in range(6):
                    dve.wait_ge(sem("combine_ready"), base * 6 + NPAIR * 6 + extra * 6 + c + 1)
                    add_combined(c).then_inc(sem("combine_added"), 1)
                V.memset(sgt[:], 0.0).then_inc(sem("sgt_cleared"), 1)

            says(select(0), "s_ready", 1)
            says(select_bias(0), "selb_ready", 1)
            sweep(0, 0)
            most = dve.value_load(cnt[0:1, 0:1], min_val=0, max_val=T)
            with dve.If(most > SLOTS):
                with dve.Fori(1, SWEEPS) as r:
                    with dve.If(most > r * SLOTS):
                        TSC(iota_s[:], iota_s[:], float(SLOTS), None, ALU.add).then_inc(sem("slots_moved"), 1)
                        dve.wait_ge(sem("slots_moved"), r)
                        dve.wait_ge(sem("gather_ready"), r * (2 * NPAIR) + 2)
                        dve.wait_ge(sem("selb_ready"), r * NPAIR + 1)
                        select(0).then_inc(sem("reselected"), 1)
                        select_bias(0).then_inc(sem("reselected"), 1)
                        dve.wait_ge(sem("reselected"), r * 2)
                        dve.wait_ge(sem("regather_ready"), r * 2)
                        dve.sem_inc(sem("sweep_entered"), 1)
                        sweep(r * NPAIR, r)
            V.tensor_copy(st2[0:1, 13:14], x1[0:1, 0, 0:1]).then_inc(sem("sums_done"), 1)
            dve.wait_ge(sem("gf_loaded"), 16)
            for i, (t0, n) in enumerate(TILES):
                dve.wait_ge(sem("root3_ready"), i + 1)
                dv(V.reciprocal(st2[0:n, 4 + i:5 + i], st2[0:n, 4 + i:5 + i]))
                STT(out=x1[0:n, i, :], in0=x1[0:n, i, :], scalar=st2[0:n, 4 + i:5 + i], in1=gfb[0:n, :],
                    op0=ALU.mult, op1=ALU.mult).then_inc(sem("y_final"), 1)

        @block.tensor
        def _(pe):
            M, TR = nc.tensor.matmul, nc.tensor.transpose

            pe.wait_ge(*at("ident_ready", 1))
            pe.wait_ge(sem("vec_loaded"), 16 * 11)
            ends_fill(TR(bank("vec")[:, 0:NVEC], vrow[0:NVEC, :], ident[0:NVEC, 0:NVEC]), "vec")
            for k in range(6):
                i, hf = k // 2, k % 2
                t0, n = TILES[i]
                pe.wait_ge(*at("xn_ready", i + 1))
                await_bank(pe, f"hT{k}")
                for c in range(4):
                    m = TR(bank(f"hT{k}")[:, 128 * c:128 * c + n], xn[0:n, i, (4 * hf + c) * 128:(4 * hf + c + 1) * 128], ident[0:n, 0:n])
                ends_fill(m, f"hT{k}")
            pe.wait_ge(filled[FILLS["hT5"][0]], FILLS["hT5"][1] + 1)
            pe.sem_inc(says_now("xn_used"), 1)
            for k in range(6):
                b, f = FILLS[f"hT{k}"]
                pe.wait_ge(drained[b], f + 1)

            def channels(name, c, col):
                await_bank(pe, name)
                w = slot_view(c % 3, WCH[c][1])
                for k in range(KD):
                    m = M(bank(name)[:, 0:T], w[:, k, col:col + 128], hT[:, k, :], start=(k == 0), stop=(k == KD - 1))
                ends_fill(m, name)

            def tokens(name, c, col, i):
                await_bank(pe, name)
                t0, n = TILES[i]
                w = slot_view(c % 3, WCH[c][1])
                for k in range(KD):
                    if i < 2:
                        m = M(bank(name)[0:n, 0:256], hT[:, k, t0:t0 + n], w[:, k, col:col + 256], start=(k == 0), stop=(k == KD - 1))
                    else:
                        for x in range(2):
                            m = M(bank(name)[n * x:n * x + n, 0:128], hT[:, k, t0:t0 + n], w[:, k, col + 128 * x:col + 128 * x + 128],
                                  start=(k == 0), stop=(k == KD - 1))
                ends_fill(m, name)

            def used(name, count):
                b, f = FILLS[name]
                pe.wait_ge(filled[b], f + 1)
                pe.sem_inc(says_now("w_in_used"), 1)

            def s5_in(j):
                r0, tt = 32 * (j % 4), j // 4
                for x, name in enumerate((f"bu{j}r", f"bu{j}i")):
                    await_bank(pe, name)
                    ends_fill(M(bank(name)[:, 0:T], wB[r0:r0 + 32, 2 * x + tt, :], uT[r0:r0 + 32, tt, :], start=True, stop=True), name)

            def s5_out(j):
                r0, tt = 32 * (j % 4), j // 4
                pe.wait_ge(*at("s5_turned", j + 1))
                out = bank(f"ys{tt}")[r0:r0 + 32, 0:T]
                M(out, wC[:, tt, r0:r0 + 32], s_r[:, j % 2, :], start=True, stop=False)
                M(out, wC[:, 2 + tt, r0:r0 + 32], s_i[:, j % 2, :], start=False, stop=True).then_inc(says_now("s5_used"), 1)
                if j % 4 == 3:
                    pe.wait_ge(*at("s5_used", j + 1))
                    pe.sem_inc(filled[FILLS[f"ys{tt}"][0]], 1)

            pe.wait_ge(sem("w_in0"), 16)
            for n, name in enumerate(("u0", "u1", "xr0", "xr1")):
                channels(name, 0, 128 * n)
            used("xr1", 1)
            pe.wait_ge(sem("wgate_loaded"), 32)
            await_bank(pe, "gates")
            for k in range(KD):
                m = M(bank("gates")[0:36, 0:T], wgate[:, k, :], hT[:, k, :], start=(k == 0), stop=(k == KD - 1))
            ends_fill(m, "gates")
            pe.wait_ge(sem("par_loaded"), 16 * 5)
            await_bank(pe, "par")
            TR(bank("par")[:, 0:128], srow[:], ident[:])
            ends_fill(TR(bank("par")[:, 128:224], prow[0:96, :], ident[0:96, 0:96]), "par")
            pe.wait_ge(*at("bb_ready", 4))
            await_bank(pe, "bt")
            for x in range(4):
                m = TR(bank("bt")[:, 128 * x:128 * x + 128], BB[:, 4 * x:4 * x + 4].rearrange("p j g c -> p (j g c)"), ident[:])
            ends_fill(m, "bt")
            pe.wait_ge(*at("cb_ready", 2))
            await_bank(pe, "ct")
            for x in range(4):
                m = TR(bank("ct")[:, 128 * x:128 * x + 128], CBk[:, x, :], ident[:])
            ends_fill(m, "ct")
            pe.wait_ge(sem("w_in1"), 16)
            for n, name in enumerate(("gr0", "gr1", "q0", "q1")):
                channels(name, 1, 128 * n)
            used("q1", 2)
            pe.sem_inc(says_now("cb_used"), 1)
            for n in ("u0", "u1", "bt"):
                pe.wait_ge(drained[FILLS[n][0]], FILLS[n][1] + 1)
            s5_in(0)
            s5_in(1)
            pe.wait_ge(sem("w_in2"), 16)
            for n, name in enumerate(("q2", "q3", "k0", "k1")):
                channels(name, 2, 128 * n)
            used("k1", 3)
            pe.wait_ge(sem("wax_loaded"), 16 * 16)
            pe.wait_ge(*at("xc_ready", 2))
            for x, nm in enumerate(("r", "i")):
                for tt in range(2):
                    await_bank(pe, f"{nm}{tt}")
                    ends_fill(M(bank(f"{nm}{tt}")[:, 0:T], wax[:, x, tt, :], xc[:, tt, :], start=True, stop=True), f"{nm}{tt}")
            pe.wait_ge(sem("w_in3"), 16)
            channels("k2", 3, 0)
            channels("k3", 3, 128)
            for i in range(3):
                tokens(f"va{i}", 3, 256, i)
            used("va2", 4)
            s5_in(2)
            s5_in(3)
            pe.wait_ge(drained[FILLS["ct"][0]], FILLS["ct"][1] + 1)
            s5_out(0)
            s5_out(1)
            pe.wait_ge(sem("w_in4"), 16)
            for i in range(3):
                tokens(f"vb{i}", 4, 0, i)
            for i in range(3):
                tokens(f"oa{i}", 4, 256, i)
            used("oa2", 5)
            s5_in(4)
            s5_in(5)
            s5_out(2)
            s5_out(3)
            pe.wait_ge(sem("w_in5"), 16)
            for i in range(3):
                tokens(f"ob{i}", 5, 0, i)
            used("ob2", 6)
            s5_in(6)
            s5_in(7)
            s5_out(4)
            s5_out(5)
            pe.wait_ge(*at("gate_rows_exp", 3))
            await_bank(pe, "rows")
            for i, (t0, n) in enumerate(TILES):
                m = TR(bank("rows")[0:n, 128 * i:128 * i + 128], rows[:, t0:t0 + n], ident[:])
            ends_fill(m, "rows")
            for h in range(H):
                b, f = FILLS[f"k{h}"]
                pe.wait_ge(drained[b], f + 1)

            def scores(h):
                await_bank(pe, f"mb{h}")
                ends_fill(M(bank(f"mb{h}")[:, 0:T], sel4[:, h, :], gsm[0:H, 4, :], start=True, stop=True), f"mb{h}")
                await_bank(pe, f"st{h}")
                sb_ = bank(f"st{h}")
                M(sb_[:, 0:256], kT[:, h, 0:128], qT[:, h, 0:256], start=True, stop=True)
                M(sb_[:, 256:384], kT[:, h, 128:256], qT[:, h, 128:256], start=True, stop=True)
                ends_fill(M(sb_[0:TS, 384:416], kT[:, h, TP:T], qT[:, h, TP:T], start=True, stop=True), f"st{h}")

            pe.wait_ge(*at("sel4_ready", 1))
            pe.wait_ge(*at("m_rows", 1))
            for h in range(3):
                scores(h)
            s5_out(6)
            s5_out(7)
            for i, (t0, n) in enumerate(TILES):
                await_bank(pe, f"kt{i}")
                for h in range(H):
                    m = TR(bank(f"kt{i}")[0:n, 128 * h:128 * h + 128], kT[:, h, t0:t0 + n], ident[:])
                ends_fill(m, f"kt{i}")
            scores(3)
            await_bank(pe, "dec")
            for h in range(H):
                m = M(bank("dec")[:, NB * h:NB * h + NB], sel4[:, h, :], gsm[0:H, 6, TS:TS + NB], start=True, stop=True)
            ends_fill(m, "dec")
            pe.wait_ge(*at("scm_ready", NB))
            for h in range(H):
                await_bank(pe, f"sc{h}")
                ends_fill(M(bank(f"sc{h}")[:, 0:NB * TS], sel4[:, h, :], scm[:].rearrange("h b t -> h (b t)"), start=True, stop=True), f"sc{h}")
            pe.wait_ge(*at("rgfin_ready", 1))
            await_bank(pe, "rgT")
            for x in range(2):
                TR(bank("rgT")[0:9, 128 * x:128 * x + 128], rgfin[:, x, :], ident[:])
            for x in range(2):
                m = TR(bank("rgT")[0:27, 256 + 128 * x:384 + 128 * x], cvfin[:, x, :], ident[:])
            ends_fill(m, "rgT")
            await_bank(pe, "s5T")
            for x in range(2):
                m = TR(bank("s5T")[0:72, 128 * x:128 * x + 128], fin5[:, x].rearrange("p s j -> p (s j)"), ident[:])
            ends_fill(m, "s5T")
            pe.wait_ge(*at("ones_ready", 1))
            for n in ("vb2", "vb1", "vb0", "va2", "va1", "va0"):
                pe.wait_ge(drained[FILLS[n][0]], FILLS[n][1] + 1)
            pe.wait_ge(*at("kw_ready", 1))
            for hh in range(2):
                await_bank(pe, f"cp{hh}")
                for x in range(2):
                    h = 2 * hh + x
                    for i in range(2):
                        m = M(bank(f"cp{hh}")[:, 129 * x:129 * x + 129], kw[:, i, h, :], v_tok[:, i, h, :], start=(i == 0), stop=(i == 1))
                ends_fill(m, f"cp{hh}")
            for h in range(H):
                b, f = FILLS[f"st{h}"]
                pe.wait_ge(drained[b], f + 1)
            for i in range(3):
                n = TILES[i][1]
                if i == 2:
                    pe.wait_ge(*at("qm_ready", 1))
                for hh in range(2):
                    name = f"nu{i}{hh}"
                    await_bank(pe, name)
                    for x in range(2):
                        h = 2 * hh + x
                        out = bank(name)[0:n, 129 * x:129 * x + 129]
                        if i == 2:
                            M(out, E[0:TS, h, 384:416], v_tok[0:TS, 2, h, :], start=True, stop=False)
                            for b in range(NB):
                                m = M(out, qm[:, h, b, :], c0[:, h, b, :], start=False, stop=(b == NB - 1))
                        elif i == 0:
                            m = M(out, E[:, h, 0:128], v_tok[:, 0, h, :], start=True, stop=True)
                        else:
                            M(out, E[:, h, 128:256], v_tok[:, 0, h, :], start=True, stop=False)
                            m = M(out, E[:, h, 256:384], v_tok[:, 1, h, :], start=False, stop=True)
                    ends_fill(m, name)
            pe.wait_ge(filled[FILLS["nu21"][0]], FILLS["nu21"][1] + 1)
            pe.sem_inc(says_now("c0_used"), 1)
            pe.wait_ge(*at("s5_gelu", 1))
            pe.wait_ge(sem("glw_loaded"), 16)
            for x in range(2):
                await_bank(pe, f"glu{x}")
                for k in range(2):
                    m = M(bank(f"glu{x}")[:, 0:T], glw[:, k, 128 * x:128 * x + 128], rt[:, k, :], start=(k == 0), stop=(k == 1))
                ends_fill(m, f"glu{x}")

            def memory_update(h):
                pe.wait_ge(*at("vw_ready", h + 1))
                for gidx, (b0, b1) in enumerate(CB):
                    name = f"cu{h}{gidx}"
                    await_bank(pe, name)
                    ends_fill(M(bank(name)[:, 0:(b1 - b0) * 129], k_tok[0:TS, 2, 128 * h:128 * h + 128],
                                vw[:, h, b0:b1, :].rearrange("p b v -> p (b v)"), start=True, stop=True), name)

            def output(i, c, k0, k1):
                t0, n = TILES[i]
                name = f"wo{i}{c}"
                if k0 == 0:
                    await_bank(pe, name)
                w = slot_view(2 + c, 512)
                for k in range(k0, k1):
                    m = M(bank(name)[0:n, :], hT[:, k, t0:t0 + n], w[:, k, :], start=(k == 0), stop=(k == KD - 1))
                if k1 == KD:
                    ends_fill(m, name)

            for h in range(H):
                memory_update(h)
            for h in range(H):
                pe.wait_ge(*at("y3_ready", h + 1))
                await_bank(pe, f"yT{h}")
                for i, (t0, n) in enumerate(TILES):
                    m = TR(bank(f"yT{h}")[:, t0:t0 + n], o_tok[0:n, i, 128 * h:128 * h + 128], ident[0:n, 0:n])
                ends_fill(m, f"yT{h}")
            b, f = FILLS["yT3"]
            pe.wait_ge(filled[b], f + 1)
            pe.sem_inc(says_now("y_turned"), 1)
            pe.sem_inc(says_now("mlstm_done"), 1)
            pe.wait_ge(*at("rg_used", 1))
            pe.wait_ge(*at("mix_ready", 1))
            for n in range(2):
                pe.wait_ge(sem(f"w_out{n}"), 16)
            for i in range(2):
                if i == 1:
                    await_bank(pe, "wo2")
                    for k in range(KD):
                        for c in range(4):
                            m = M(bank("wo2")[TS * c:TS * c + TS, 0:256], hT[:, k, TP:T],
                                  slot_view(2 + c // 2, 512)[:, k, 256 * (c % 2):256 * (c % 2) + 256], start=(k == 0), stop=(k == KD - 1))
                    ends_fill(m, "wo2")
                for c in range(2):
                    output(i, c, 0, 4)
                    if i == 0 and c == 0:
                        for h in range(H):
                            b, f = FILLS[f"yT{h}"]
                            pe.wait_ge(drained[b], f + 1)
                    output(i, c, 4, KD)
                    if i == 0 and c == 0:
                        pe.wait_ge(*at("c_new", H))
                        pe.wait_ge(*at("c_prompt", 2))
                        await_bank(pe, "nT")
                        ends_fill(TR(bank("nT")[0:36, 0:128], nbuf[:], ident[:]), "nT")

            def turn_rows(i):
                t0, n = TILES[i]
                pe.wait_ge(*at("x2_ready", (1, 3, 2)[i]))
                for hf in range(2):
                    name = f"h2T{2 * i + hf}"
                    await_bank(pe, name)
                    for c in range(4):
                        m = TR(bank(name)[:, 128 * c:128 * c + n], xn[0:n, i, (4 * hf + c) * 128:(4 * hf + c + 1) * 128], ident[0:n, 0:n])
                    ends_fill(m, name)

            def logits(i):
                t0, n = TILES[i]
                for hf in range(2):
                    b, f = FILLS[f"h2T{2 * i + hf}"]
                    pe.wait_ge(drained[b], f + 1)
                for k in range(KD):
                    m = M(bank("lg")[0:n, NE * i:NE * i + NE], h2T[:, k, t0:t0 + n], rw[:, k, :], start=(k == 0), stop=(k == KD - 1))
                return m

            turn_rows(0)
            turn_rows(2)
            pe.wait_ge(filled[FILLS["wo11"][0]], FILLS["wo11"][1] + 1)
            pe.sem_inc(says_now("w_out_used"), 1)
            pe.wait_ge(sem("router_loaded"), 48)
            await_bank(pe, "lg")
            logits(0)
            logits(2)
            turn_rows(1)
            m = logits(1)
            ends_fill(m, "lg")
            pe.wait_ge(*at("mask_ready", 1))
            await_bank(pe, "cum")
            for i, (t0, n) in enumerate(TILES):
                for j in range(i + 1):
                    nj = TILES[j][1]
                    lhs = upper[0:nj, 0:n] if j == i else ones_bf[0:nj, 0:n]
                    M(bank("cum")[0:n, NE * i:NE * i + NE], lhs, mskb[0:nj, j, :], start=(j == 0), stop=(j == i))
            for i, (t0, n) in enumerate(TILES):
                m = M(bank("cum")[:, 96:128], ones_bf[0:n, :], mskb[0:n, i, :], start=(i == 0), stop=(i == 2))
            ends_fill(m, "cum")

            W1COL = [0, 2, 1, 3]

            def gather(name, inc_count):
                for c in range(KD):
                    for i, (t0, n) in enumerate(TILES):
                        m = M(psum[:, 6 + c // 4, 128 * (c % 4):128 * (c % 4) + 128], xn[0:n, i, 128 * c:128 * c + 128],
                              S[0:n, i].rearrange("p x s -> p (x s)"), start=(i == 0), stop=(i == 2))
                    if c % 4 == 3:
                        m.then_inc(sem(name), 1)

            def combine(c):
                i, nn = c // 2, c % 2
                t0, n = TILES[i]
                M(psum[0:n, 6 + c % 2, :], sgt[:, t0:t0 + n], yb[:, nn, :], start=True, stop=True).then_inc(sem("combine_ready"), 1)

            def bias(bk, col):
                return M(psum[:, bk, :], selb[0:96].rearrange("p x s -> p (x s)"), bsplit[0:96, col:col + 512], start=True, stop=False)

            def pair_steps(gp, twos, u, extra):
                def await_chunks(w):
                    for x in range(2):
                        s, _ = ring_slot(BLOCKS * u + w, x)
                        pe.wait_ge(sem(f"expert_chunk{s}"), twos * 48 + 16 * ((BLOCKS * u + w) // DEPTH) + 16)

                pe.wait_ge(sem("selb_ready"), gp + 1)
                pe.wait_ge(sem("xg_copied"), gp * 2 + 2)
                for w in range(4):
                    if w < 2:
                        pe.wait_ge(sem("aT_copied"), gp * 2 + 0)
                    bias(w, [0, FF, 512, FF + 512][w])
                    await_chunks(w)
                    for k in range(KD):
                        for x in range(2):
                            m = M(psum[64 * x:64 * x + 64, w, :], xg[:, k, 64 * x:64 * x + 64],
                                  ring_slot(BLOCKS * u + w, x)[1][:, 512 * k:512 * k + 512], start=False, stop=(k == KD - 1))
                    m.then_inc(sem("block_done"), 1)
                    if w < 3:
                        for c in (2 * w, 2 * w + 1):
                            if c < 2:
                                if c == 0:
                                    pe.wait_ge(sem("y_copied"), gp * 2)
                                    pe.wait_ge(sem("sgt_copied"), gp)
                            else:
                                pe.wait_ge(sem("combine_added"), gp * 6 + c - 1 + extra * 6)
                            combine(c)
                pe.wait_ge(sem("combine_added"), gp * 6 + 6 + extra * 6)
                pe.wait_ge(sem("s_ready"), gp + 2)
                gather("gather_ready", None)
                for x in range(2):
                    pe.wait_ge(sem("act_ready"), gp * 2 + 1 + x)
                    for c in range(4):
                        m = TR(psum[:, x, 128 * c:128 * c + 128], gact[:, x, 128 * c:128 * c + 128], ident[:])
                    m.then_inc(sem("aT_ready"), 1)
                pe.wait_ge(sem("sg_ready"), gp + 1)
                pe.wait_ge(sem("xg_copied"), gp * 2 + 3)
                for i, (t0, n) in enumerate(TILES):
                    m = TR(psum[:, 6, t0:t0 + n], SG[0:n, i].rearrange("p x s -> p (x s)"), ident[0:n, 0:n])
                m.then_inc(sem("sgt_ready"), 1)
                for nn in range(2):
                    m = bias(4 + nn, 2 * FF + 512 * nn)
                m.then_inc(sem("bias_used"), 1)
                for hf in range(2):
                    await_chunks(4 + hf)
                    pe.wait_ge(sem("aT_copied"), gp * 2 + 1 + hf)
                    for k in range(4):
                        if hf == 1 and k == 2:
                            pe.wait_ge(sem("last_half"), gp * 32 + 32)
                        for nn in range(2):
                            for x in range(2):
                                m = M(psum[64 * x:64 * x + 64, 4 + nn, :], aT[:, 4 * hf + k, 64 * x:64 * x + 64],
                                      ring_slot(BLOCKS * u + 4 + hf, x)[1][:, 1024 * k + 512 * nn:1024 * k + 512 * nn + 512],
                                      start=False, stop=(hf == 1 and k == 3))
                    m.then_inc(sem("block_done"), 1)

            def sweep(base, base_twos, extra):
                with pe.Fori(0, NPAIR // 2) as q:
                    for u in range(2):
                        pair_steps(base + q * 2 + u, base_twos + q, u, extra)
                pe.wait_ge(sem("y_copied"), base * 2 + NPAIR * 2)
                pe.wait_ge(sem("sgt_copied"), base + NPAIR)
                pe.wait_ge(sem("xg_copied"), base * 2 + NPAIR * 2 + 2)
                for c in range(6):
                    if c >= 2:
                        pe.wait_ge(sem("combine_added"), base * 6 + NPAIR * 6 + extra * 6 + c - 1)
                    combine(c)

            pe.wait_ge(sem("s_ready"), 1)
            pe.wait_ge(*at("bias_ready", 1))
            gather("gather_ready", None)
            sweep(0, 0, 0)
            pe.wait_ge(*at("count_ready", 1))
            most = pe.value_load(cnt[0:1, 0:1], min_val=0, max_val=T)
            with pe.If(most > SLOTS):
                with pe.Fori(1, SWEEPS) as r:
                    with pe.If(most > r * SLOTS):
                        pe.wait_ge(sem("sgt_cleared"), r)
                        pe.wait_ge(sem("reselected"), r * 2)
                        gather("regather_ready", None)
                        pe.wait_ge(sem("xg_recopied"), r * 2)
                        pe.sem_inc(sem("sweep_entered"), 1)
                        sweep(r * NPAIR, r * (NPAIR // 2), r)


_INS = ["x_prompt", "x_sample", "state_s5_re", "state_s5_im", "state_rg_h", "state_rg_conv", "state_ml_c",
        "state_ml_n", "state_ml_m", "norm1_g", "w_in", "s5_lambda_re", "s5_lambda_im", "s5_log_step", "s5_b_re",
        "s5_b_im", "s5_c_re", "s5_c_im", "s5_d", "s5_glu_w", "s5_glu_b", "rg_conv_w", "rg_conv_b", "rg_wa", "rg_ba",
        "rg_wx", "rg_bx", "rg_lambda", "ml_gate_bias", "ml_norm_g", "w_out", "norm2_g", "router_w", "router_b",
        "exp_w1", "exp_b1", "exp_w2", "exp_b2", "final_norm_g"]
_STATES = lambda b: [(1, b, G5, P5), (1, b, G5, P5), (1, b, 256), (1, b, 3, 256), (1, b, H, DK, DK), (1, b, H, DK), (1, b, H)]
_OUTS = [(1, TP, D), (NB, NT, D)] + _STATES(1) + _STATES(NB)


def kernel(**inputs):
    import numpy as _np
    import concourse.bacc as _bacc
    from concourse.bass_utils import run_bass_kernel_spmd as _run

    nc = _bacc.Bacc("TRN2", target_bir_lowering=False, num_devices=1)
    arrays, args = {}, {}
    for name in _INS:
        v = _np.ascontiguousarray(inputs[name])
        arrays[f"in_{name}_dram"] = v
        args[name] = nc.dram_tensor(f"in_{name}_dram", v.shape, mybir.dt.from_np(v.dtype), kind="ExternalInput").ap()
    outs = [nc.dram_tensor(f"out_{i}_dram", shape, F32, kind="ExternalOutput").ap() for i, shape in enumerate(_OUTS)]
    build_program(nc, args, outs)
    r = _run(nc, [arrays], core_ids=[0])
    return tuple(r.results[0][f"out_{i}_dram"] for i in range(len(_OUTS)))
```

```python
from contextlib import ExitStack
import math

import concourse.bass as bass
from concourse import mybir

ALU = mybir.AluOpType
ACT = mybir.ActivationFunctionType
AX = mybir.AxisListType
F32 = mybir.dt.float32
BF16 = mybir.dt.bfloat16
I32 = mybir.dt.int32
U32 = mybir.dt.uint32

D = 1024
KD = D // 128
TP, NB, NT = 256, 8, 4
TS = NB * NT
T = TP + TS
TILES = [(0, 128), (128, 128), (256, 32)]
G5, P5, C5 = 16, 64, 16
J5 = G5 * P5 // 128
RC = 8.0
H, DK = 4, 128
NE, TOPK, FF = 32, 4, 1024
NPAIR = NE // 2
SLOTS = 64
SWEEPS = -(-T // SLOTS)
EPS = 1e-5
CH = 4096

U0, XR0, GR0, Q0, K0, V0, O0, GI0 = 0, 256, 512, 768, 1280, 1792, 2304, 2816
VEC = {}
_row = 0
for _name, _n in (("norm1_g", 8), ("s5_d", 2), ("s5_glu_b", 2), ("rg_conv_w", 8), ("rg_conv_b", 2), ("rg_ba", 2),
                  ("rg_bx", 2), ("rg_lambda", 2), ("ml_norm_g", 4), ("s5_lambda_re", 8), ("s5_lambda_im", 8)):
    VEC[_name] = (_row, _n)
    _row += _n
NVEC = _row

CB = [(0, 3), (3, 6), (6, 8)]
FILLS, _fills_of = {}, [0] * 8


def _place(names, banks):
    for i, name in enumerate(names):
        b = banks[i % len(banks)]
        FILLS[name] = (b, _fills_of[b])
        _fills_of[b] += 1


_place(["vec"] + [f"hT{i}" for i in range(6)] + ["u0", "u1", "xr0", "xr1", "gates", "gr0", "gr1", "par", "bt", "ct",
       "q0", "q1", "q2", "q3", "k0", "k1", "r0", "r1", "i0", "i1", "bu0r", "bu0i", "bu1r", "bu1i",
       "k2", "k3", "bu2r", "bu2i", "va0", "va1", "va2", "bu3r", "bu3i", "vb0", "vb1", "bu4r", "bu4i",
       "vb2", "oa0", "bu5r", "bu5i", "oa1", "oa2", "bu6r", "bu6i", "ob0", "bu7r", "bu7i", "ob1", "ob2",
       "rows", "mb0", "st0", "mb1", "st1", "mb2", "st2",
       "mb3", "st3", "kt0", "kt1", "kt2", "dec"] + [f"sc{h}" for h in range(H)] + ["rgT", "s5T"], range(6))
_place(["ys0", "ys1", "cp0", "cp1", "glu0", "glu1"] + [f"yT{h}" for h in range(H)], (6, 7))
_place(["nu00", "nu01", "nu10", "nu11", "nu20", "nu21"], range(6))
_place([f"cu{h}{g}" for h in range(H) for g in range(len(CB))], range(4))
_place(["wo00", "wo01"], (4, 5))
_place(["nT", "wo2", "wo10", "h2T0", "h2T1", "h2T4", "h2T5", "wo11", "h2T2", "lg", "h2T3", "cum"], range(6))
SAID = {
    "dve_said": [("nst_set", 1), ("xn_ready", 3), ("angle_reduced", 1), ("bb_ready", 4), ("cb_ready", 2),
        ("gate_abs", 1), ("rg_decay", 1), ("m_rows", 1), ("gate_rows", 1), ("xc_ready", 2), ("scm_ready", 8),
        ("gate_poly", 1), ("gate_ready", 1), ("s5_scanned", 3), ("rg_ratio", 1), ("s5_scanned", 1),
        ("rgfin_ready", 1), ("s5_scanned", 4), ("mix_ready", 1), ("ones_ready", 1), ("wsm_ready", 1), ("e_arg", 4),
        ("qm_ready", 1), ("s5_poly", 1), ("den_read", 2), ("nvar_ready", 1), ("s5_gelu", 1), ("den_read", 1),
        ("nvar_ready", 1), ("y3_ready", 4), ("rg_used", 1), ("c_new", 4), ("x2_ready", 1), ("x1_added", 1),
        ("x2_ready", 1), ("x1_added", 1), ("x2_ready", 3), ("x1_added", 1), ("x2_ready", 1), ("top_diff", 1),
        ("mask_ready", 1), ("count_ready", 1)],
    "act_said": [("table_loaded", 1), ("ms_ready", 1), ("root_ready", 1), ("ms_ready", 1), ("root_ready", 1),
        ("ms_ready", 1), ("root_ready", 1), ("step_ready", 1), ("mag_ready", 1), ("act_rg", 2), ("angle_ready", 2),
        ("gate_exp", 1), ("xp_ready", 2), ("wc_ready", 1), ("bias_rounded", 1), ("gate_rows_exp", 3),
        ("gate_tanh", 1), ("v_half", 2), ("rg_tanh", 2), ("rg_a", 2), ("rg_root", 1), ("v_half", 2), ("o_half", 2),
        ("bias_rounded", 1), ("o_half", 2), ("rtok_ready", 1), ("e_exp", 4), ("bias_rounded", 1), ("s5_tanh", 1),
        ("rg_staged", 2), ("s5_staged", 1), ("nsq_ready", 8), ("nroot_ready", 1), ("bias_rounded", 1),
        ("nsq_ready", 4), ("nroot_ready", 1), ("c_prompt", 2), ("bias_rounded", 1), ("bias_ready", 1),
        ("n_staged", 1), ("ms2_ready", 1), ("root2_ready", 1), ("ms2_ready", 1), ("root2_ready", 1),
        ("ms2_ready", 1), ("root2_ready", 1), ("top_exp", 1)],
    "pool_said": [("ident_ready", 1), ("weights_zero", 1), ("bb_zero", 1), ("seg_ready", 1), ("causal_ready", 1),
        ("sel4_ready", 1), ("ind_ready", 1), ("rows_zero", 1), ("table_ready", 1), ("e_zero", 1), ("s5_turned", 4),
        ("bias_rest", 1), ("s5_turned", 4), ("bias_rest", 1), ("kw_ready", 1), ("vw_ready", 4), ("bias_rest", 1),
        ("c_decayed", 4), ("bias_rest", 1)],
    "pe_said": [("xn_used", 1), ("w_in_used", 2), ("cb_used", 1), ("w_in_used", 2), ("s5_used", 3), ("w_in_used", 1),
        ("s5_used", 2), ("w_in_used", 1), ("s5_used", 3), ("c0_used", 1), ("y_turned", 1), ("mlstm_done", 1),
        ("w_out_used", 1)],
}
SAID_BY, VALUES = {}, {}
for _line, _said in SAID.items():
    _at = 0
    for _name, _times in _said:
        for _ in range(_times):
            _at += 1
            SAID_BY[_name] = _line
            VALUES.setdefault(_name, []).append(_at)


def spread(v, axis, n):
    shape = list(v.shape)
    shape[axis] = n
    return v.broadcast_to(shape)


def build_program(nc, a, o):
    ctx = ExitStack()
    with ctx:
        def sb(name, shape, dt=F32):
            return ctx.enter_context(nc.sbuf_tensor(name, shape, dt))

        ring_a = sb("ring_a", [128, 6 * CH + 2 * H * NB])
        ring = ring_a[:, H * NB:H * NB + 6 * CH].rearrange("p (s n) -> p s n", s=6)
        xn = sb("xn", [128, 3, D])
        x1 = sb("x1", [128, 3, D])
        bsplit = sb("bsplit", [128, 3 * D], BF16)
        ident = sb("ident", [128, 128])
        upper = sb("upper", [128, 128], BF16)
        ones_bf = sb("ones_bf", [128, 128], BF16)
        iota_e = sb("iota_e", [128, NE])
        iota_s = sb("iota_s", [128, SLOTS])
        half = sb("half", [128, 2, SLOTS])
        selid = sb("selid", [128, NPAIR + 1])
        cnt = sb("cnt", [128, 1], I32)
        st2 = sb("st2", [128, 16])
        psum = ctx.enter_context(nc.psum_tensor("psum", [128, 8, 512], F32))

        def carve(base, shape):
            region, at = base
            n = math.prod(shape[1:])
            v = region[0:shape[0], at:at + n]
            if len(shape) == 3:
                v = v.rearrange("p (x y) -> p x y", x=shape[1])
            if len(shape) == 4:
                v = v.rearrange("p (x y z) -> p x y z", x=shape[1], y=shape[2])
            base[1] += n
            assert base[1] <= region.shape[1], (shape, base[1])
            return v

        mx = ExitStack()

        def ms(name, shape, dt=F32):
            return mx.enter_context(nc.sbuf_tensor(name, shape, dt))

        tabc = ms("tabc", [128, 2, J5, T])
        tab_r, tab_i = tabc[:, 0], tabc[:, 1]
        uT = ms("uT", [128, 2, T])
        xpP = ms("xpP", [128, 2, 3 + TP])
        qT = ms("qT", [128, H, T])
        kT = ms("kT", [128, H, T])
        causal = ms("causal", [128, 416])
        rgb = ms("rgb", [128, 5 * 2 * T])
        rb = [rgb[:], 0]
        xc, rr, ri, rt, gate = (carve(rb, [128, 2, T]) for _ in range(5))
        gsm = ms("gsm", [128, 8, T])
        seg = ms("seg", [128, T])
        t_pool = ms("t_pool", [128, T])
        wC = ms("wC", [128, 4, 128])
        parT = ms("parT", [128, 256])
        sm = ms("sm", [128, 26, J5])
        sel4 = ms("sel4", [H, H, 128])
        scm = ms("scm", [H, NB, TS])
        gb = ms("gb", [H, 2])
        m0 = ms("m0", [H, NB])
        wsm = ms("wsm", [TS, H, NB])
        glw = ms("glw", [128, 2, 256])
        hT = ms("hT", [128, KD, T])
        t_dve = ms("t_dve", [128, T])
        vecs = ms("vecs", [128, 128])
        fin5 = ms("fin5", [128, 2, 1 + NB, J5])
        rsm = ms("rsm", [128, 64])
        dec = ms("dec", [128, H, NB])
        nbuf = ms("nbuf", [128, 36])
        rgfin = ms("rgfin", [128, 2, 9])
        cvfin = ms("cvfin", [128, 2, 27])
        nst = ms("nst", [128, 16])
        ra = [ring[:, 4:6, :].rearrange("p s n -> p (s n)"), 0]
        v_tok = carve(ra, [128, 3, H, 129])
        E = carve(ra, [128, H, 416])
        assert ra[1] <= CH
        rb = [ring_a[:], 6 * CH + 2 * H * NB - H * NB * 129]
        vw = carve(rb, [TS, H * NB, 129]).rearrange("p (h b) v -> p h b v", h=H)
        rb = [ra[0], H * 129 * 3]
        pt1, pt2 = carve(rb, [128, J5, 128]), carve(rb, [128, J5, 128])
        b_in = carve(rb, [128, 2, J5, C5])
        b_t = carve(rb, [128, 2, J5, C5])
        BB = carve(rb, [128, 2 * J5, 2, C5])
        c_in = carve(rb, [128, 4, P5])
        CBk = carve(rb, [128, 4, 2 * P5])
        vrow, srow, prow = carve(rb, [128, 128]), carve(rb, [128, 128]), carve(rb, [128, 128])
        rb = [tabc[:].rearrange("p x j t -> p (x j t)"), 0]
        k_tok, kw, qm = carve(rb, [128, 3, 512]), carve(rb, [128, 2, H, 128]), carve(rb, [128, H, NB, TS])
        assert rb[1] <= CH
        rb = [ring_a[:], 0]
        c0 = carve(rb, [128, H * NB, 129]).rearrange("p (h b) v -> p h b v", h=H)
        rb = [ring[:, 3, :], 0]
        w_r, w_i, s_r, s_i = (carve(rb, [128, 2, T]) for _ in range(4))
        wB, wax = carve(rb, [128, 4, 128]), carve(rb, [128, 2, 2, 128])
        d0s, xpS, wgate = carve(rb, [128, J5, TS]), carve(rb, [128, 2, NB, 3 + NT]), carve(rb, [128, KD, 36])
        rb = [x1[:].rearrange("p i n -> p (i n)"), 0]
        bias_in = carve(rb, [128, 3 * D // 2])
        o_tok = carve(rb, [128, 3, 512])
        rb = [xn[:].rearrange("p i n -> p (i n)"), 0]
        cP = carve(rb, [128, H, 129])
        rb[1] = 3 * D - (T + 10 * 128)
        rows, rtok, stage = carve(rb, [128, T]), carve(rb, [128, 3, 128]), carve(rb, [128, 7, 128])
        mx.close()

        ring_b = sb("ring_b", [128, 2, CH])
        acts = sb("acts", [128, 3 * 1024])
        rb = [acts[:], 0]
        h2T, rw, rbias = carve(rb, [128, KD, T]), carve(rb, [128, KD, NE]), carve(rb, [128, NE])
        rb = [acts[:], 0]
        gact, sg1, uact = (carve(rb, [128, 2, 512]) for _ in range(3))
        g2b, gfb = sb("g2b", [128, D]), sb("gfb", [128, D])
        lg = sb("lg", [128, 3, NE])
        top = sb("top", [128, 3, 8])
        topi = sb("topi", [128, 3, 8], U32)
        topf = sb("topf", [128, 3, 8])
        gk = sb("gk", [128, 3, 8])
        msk, gts, tmp3 = sb("msk", [128, 3, NE]), sb("gts", [128, 3, NE]), sb("tmp3", [128, 3, NE])
        mskb = sb("mskb", [128, 3, NE], BF16)
        slot = sb("slot", [128, NPAIR + 1, 3, 2])
        sgate = sb("sgate", [128, NPAIR + 1, 3, 2])
        selb = sb("selb", [128, 2, SLOTS], BF16)
        xg = sb("xg", [128, KD, 128])
        aT = sb("aT", [128, 8, 128])
        sgt = sb("sgt", [128, T])
        S = sb("S", [128, 3, 2, SLOTS])
        SG = sb("SG", [128, 3, 2, SLOTS])
        yb = sb("yb", [128, 2, 512])

        sems = {}

        def sem(name):
            if name not in sems:
                sems[name] = ctx.enter_context(nc.semaphore(name))
            return sems[name]

        counted = {}

        def at(name, n):
            return (sem(SAID_BY.get(name)), VALUES[name][n - 1]) if name in VALUES else (sem(name), n)

        def says_now(name):
            if name not in VALUES:
                return sem(name)
            line = SAID_BY[name]
            for k in (name, line):
                counted[k] = counted.get(k, 0) + 1
            assert counted[line] == VALUES[name][counted[name] - 1], (line, name)
            return sem(line)

        filled = [sem(f"filled{b}") for b in range(8)]
        drained = [sem(f"drained{b}") for b in range(8)]

        def bank(name):
            return psum[:, FILLS[name][0], :]

        def await_fill(eng, name):
            eng.wait_ge(filled[FILLS[name][0]], FILLS[name][1] + 1)

        def await_bank(pe, name):
            if FILLS[name][1]:
                pe.wait_ge(drained[FILLS[name][0]], FILLS[name][1])

        def ends_fill(ins, name):
            ins.then_inc(filled[FILLS[name][0]], 1)

        def vec(name, k=None):
            r, n = VEC[name]
            return vecs[:, r:r + n] if k is None else vecs[:, r + k:r + k + 1]

        ctx.enter_context(nc.allow_non_contiguous_dma(reason="a few rows of single values"))
        block = ctx.enter_context(nc.Block())

        def w_in_cols(c0_, n):
            return a["w_in"][0][:, c0_:c0_ + n].rearrange("(k p) n -> p k n", p=128)

        def slot_view(s, n):
            return ring[:, s, 0:KD * n].rearrange("p (k n) -> p k n", k=KD)

        WCH = [(U0, 512), (GR0, 512), (1024, 512), (1536, 512), (2048, 512), (2560, 256)]
        BLOCKS = 6
        DEPTH = 4

        def ring_slot(b, x):
            s = 2 * (b % DEPTH) + x
            return s, (ring[:, s, :] if s < 6 else ring_b[:, s - 6, :])

        VECTORS = [(name, a[name][0].rearrange("(k p) -> k p", p=128)) for name in
                   ("norm1_g", "s5_d", "s5_glu_b", "rg_conv_b", "rg_ba", "rg_bx", "rg_lambda", "ml_norm_g")]
        VECTORS += [("rg_conv_w", a["rg_conv_w"][0].rearrange("t (k p) -> (t k) p", p=128))]
        VECTORS += [(name, a[name][0].rearrange("(j g) p -> j (g p)", g=2)) for name in ("s5_lambda_re", "s5_lambda_im")]

        def load_vector(eng, name, src):
            r, n = VEC[name]
            eng.dma_start(vrow[r:r + n, :], src).then_inc(sem("vec_loaded"), 16)

        @block.sync
        def _(sp):
            def load_block(pair, b, experts=(0, 1)):
                which = b % BLOCKS
                late = []
                for x in experts:
                    s, place = ring_slot(b, x)
                    if which < 4:
                        n0 = [0, FF, 512, FF + 512][which]
                        dst = place.rearrange("p (k n) -> p k n", k=KD)
                        src = a["exp_w1"][0][pair * 2 + x].rearrange("(k p) n -> p k n", p=128)[:, :, n0:n0 + 512]
                    else:
                        f0 = (which - 4) * 4
                        dst = place.rearrange("p (k n) -> p k n", k=4)
                        src = a["exp_w2"][0][pair * 2 + x].rearrange("(k p) n -> p k n", p=128)[:, f0:f0 + 4, :]
                    if which == 5:
                        late.append((dst[:, 2:4], src[:, 2:4]))
                        dst, src = dst[:, 0:2], src[:, 0:2]
                    sp.dma_start(dst, src).then_inc(sem(f"expert_chunk{s}"), 16)
                for dst, src in late:
                    sp.dma_start(dst, src).then_inc(sem("last_half"), 16)

            for i in range(2):
                sp.dma_start(xn[:, i, :], a["x_prompt"][0, 128 * i:128 * i + 128, :]).then_inc(sem(f"x_loaded{i}"), 16)
            sp.dma_start(xn[0:TS, 2, :], a["x_sample"].rearrange("b t n -> (b t) n")).then_inc(sem("x_loaded2"), 16)
            for name, src in VECTORS[4:]:
                load_vector(sp, name, src)
            for c in range(6):
                if c == 1:
                    for x, name in enumerate(("s5_b_re", "s5_b_im")):
                        for gg in range(2):
                            sp.dma_start(b_in[64 * gg:64 * gg + 64, x], a[name][0].rearrange("(j g) p c -> g p j c", g=2)[gg]).then_inc(sem("b_loaded"), 16)
                    for gg in range(2):
                        sp.dma_start(sm[64 * gg:64 * gg + 64, 0, :], spread(a["s5_log_step"][0:1].rearrange("l (j g) -> l g j", g=2)[:, gg, :], 0, 64)).then_inc(sem("step_loaded"), 16)
                    for x, name in enumerate(("s5_c_re", "s5_c_im")):
                        for tt in range(2):
                            sp.dma_start(c_in[:, 2 * x + tt, :], a[name][0, 8 * tt:8 * tt + 8].rearrange("g c p -> (g c) p")).then_inc(sem("c_loaded"), 16)
                    for x, name in enumerate(("state_s5_re", "state_s5_im")):
                        sp.dma_start(srow[64 * x:64 * x + 64, :], a[name][0].rearrange("b (j g) p -> (b j) (g p)", g=2)).then_inc(sem("par_loaded"), 16)
                    sp.dma_start(prow[0:32, :], a["state_ml_n"][0].rearrange("b h k -> (b h) k")).then_inc(sem("par_loaded"), 16)
                    sp.dma_start(prow[32:48, :], a["state_rg_h"][0].rearrange("b (x n) -> (b x) n", x=2)).then_inc(sem("par_loaded"), 16)
                    sp.dma_start(prow[48:96, :], a["state_rg_conv"][0].rearrange("b t (x n) -> (b t x) n", x=2)).then_inc(sem("par_loaded"), 16)
                    sp.dma_start(gb[:], a["ml_gate_bias"][0].rearrange("(x h) -> h x", x=2)).then_inc(sem("gb_loaded"), 16)
                    sp.dma_start(m0[:], a["state_ml_m"][0].rearrange("b h -> h b")).then_inc(sem("gb_loaded"), 16)
                    sp.dma_start(glw[:], a["s5_glu_w"][0].rearrange("(k p) n -> p k n", p=128)).then_inc(sem("glw_loaded"), 16)
                    sp.wait_ge(*at("weights_zero", 1))
                    for x in range(2):
                        sp.dma_start(wgate[:, :, 32 * x:32 * x + H], w_in_cols(GI0 + H * x, H)).then_inc(sem("wgate_loaded"), 16)
                if c == 3:
                    for x, name in enumerate(("rg_wa", "rg_wx")):
                        for n in range(8):
                            q = slice(32 * (n % 4), 32 * (n % 4) + 32)
                            sp.dma_start(wax[q, x, n // 4, q], a[name][0, n]).then_inc(sem("wax_loaded"), 16)
                if c >= 3:
                    sp.wait_ge(*at("w_in_used", c - 2))
                sp.dma_start(slot_view(c % 3, WCH[c][1]), w_in_cols(*WCH[c])).then_inc(sem(f"w_in{c}"), 16)
            sp.wait_ge(*at("w_in_used", 5))
            for h in range(H):
                sp.dma_start(c0[:, h, :, 0:128], a["state_ml_c"][0, :, h].rearrange("b k v -> k b v")).then_inc(sem("c0_loaded"), 16)
            sp.dma_start(o[8].rearrange("l b h -> (l h) b"), gsm[0:H, 7, TP - 1:TP]).then_inc(sem("m_stored"), 16)
            sp.dma_start(o[15][0].rearrange("b h -> h b"), gsm[0:H, 7, TP + NT - 1:T:NT]).then_inc(sem("m_stored"), 16)
            load_block(0, 0, (1,))
            sp.wait_ge(*at("w_in_used", 6))
            for n in range(2):
                if n == 1:
                    sp.wait_ge(*at("s5_used", J5))
                sp.dma_start(slot_view(2 + n, 512), a["w_out"][0][:, n * 512:(n + 1) * 512].rearrange(
                    "(k p) n -> p k n", p=128)).then_inc(sem(f"w_out{n}"), 16)
            sp.wait_ge(*at("rg_staged", 2))
            sp.dma_start(o[4][0, 0].rearrange("(a x n) -> a x n", a=1, x=2), stage[0:1, 1:3, :]).then_inc(sem("stored"), 16)
            sp.dma_start(o[11][0].rearrange("b (x n) -> b x n", x=2), stage[1:9, 1:3, :]).then_inc(sem("stored"), 16)
            sp.dma_start(o[5][0, 0].rearrange("t (x n) -> t x n", x=2), stage[0:3, 3:5, :]).then_inc(sem("stored"), 16)
            sp.dma_start(o[12][0].rearrange("b t (x n) -> (b t) x n", x=2), stage[3:27, 3:5, :]).then_inc(sem("stored"), 16)
            sp.wait_ge(*at("s5_staged", 1))
            for x in range(2):
                src = stage[:, 5 + x, :]
                sp.dma_start(o[2 + x][0, 0].rearrange("(j g) p -> j (g p)", g=2), src[0:J5, :]).then_inc(sem("stored"), 16)
                sp.dma_start(o[9 + x][0].rearrange("b (j g) p -> (b j) (g p)", g=2), src[J5:9 * J5, :]).then_inc(sem("stored"), 16)
            sp.wait_ge(*at("s5_poly", 1))
            sp.wait_ge(*at("kw_ready", 1))
            load_block(0, 3, (1,))
            sp.wait_ge(*at("c0_used", 1))
            sp.wait_ge(*at("vw_ready", H))
            load_block(0, 2, (0,))
            sp.wait_ge(*at("c_prompt", 2))
            sp.dma_start(o[6][0, 0].rearrange("h k v -> k h v"), cP[:, :, 0:128]).then_inc(sem("cp_stored"), 16)
            sp.wait_ge(*at("y_turned", 1))
            sp.wait_ge(*at("bias_ready", 1))
            sp.dma_start(x1[:, 0:2, :], a["x_prompt"][0].rearrange("(i p) n -> p i n", p=128)).then_inc(sem("x1_loaded"), 16)
            sp.dma_start(x1[0:TS, 2, :], a["x_sample"].rearrange("b t n -> (b t) n")).then_inc(sem("x1_loaded"), 16)
            for h in range(H):
                sp.wait_ge(*at("c_new", h + 1))
                sp.dma_start(o[13][0, :, h].rearrange("b k v -> k b v"), c0[:, h, :, 0:128]).then_inc(sem("c_stored"), 16)
            sp.wait_ge(*at("mlstm_done", 1))
            sp.wait_ge(sem("m_stored"), 32)
            sp.dma_start(g2b[:], spread(a["norm2_g"][0:1, :], 0, 128)).then_inc(sem("router_loaded"), 16)
            sp.dma_start(rw[:], a["router_w"][0].rearrange("(k p) e -> p k e", p=128)).then_inc(sem("router_loaded"), 16)
            sp.dma_start(rbias[:], spread(a["router_b"][0:1, :], 0, 128)).then_inc(sem("router_loaded"), 16)
            sp.wait_ge(*at("n_staged", 1))
            sp.dma_start(o[14][0].rearrange("b h k -> (b h) k"), stage[0:32, 0, :]).then_inc(sem("stored"), 16)
            sp.dma_start(o[7][0, 0], stage[32:36, 0, :]).then_inc(sem("stored"), 16)
            load_block(0, 2, (1,))
            sp.wait_ge(sem("cp_stored"), 16)
            sp.wait_ge(*at("rg_used", 1))
            load_block(0, 3, (0,))
            sp.wait_ge(sem("c_stored"), 64)
            load_block(0, 0, (0,))
            stored = 16 * 10
            sp.wait_ge(*at("w_out_used", 1))
            load_block(0, 1)
            sp.wait_ge(*at("ms2_ready", 3))
            sp.dma_start(gfb[:], spread(a["final_norm_g"].rearrange("(a n) -> a n", a=1), 0, 128)).then_inc(sem("gf_loaded"), 16)
            for b in range(DEPTH, 2 * BLOCKS):
                sp.wait_ge(sem("block_done"), b + 1 - DEPTH)
                load_block(b // BLOCKS, b)
            with sp.Fori(1, NPAIR // 2) as q:
                for b in range(2 * BLOCKS):
                    sp.wait_ge(sem("block_done"), q * (2 * BLOCKS) + (b + 1 - DEPTH))
                    load_block(q * 2 + b // BLOCKS, b)
            sp.wait_ge(*at("count_ready", 1))
            most = sp.value_load(cnt[0:1, 0:1], min_val=0, max_val=T)
            with sp.If(most > SLOTS):
                with sp.Fori(1, SWEEPS) as r:
                    with sp.If(most > r * SLOTS):
                        with sp.Fori(0, NPAIR // 2) as q:
                            for b in range(2 * BLOCKS):
                                sp.wait_ge(sem("block_done"), r * (NPAIR * BLOCKS) + q * (2 * BLOCKS) + (b + 1 - DEPTH))
                                load_block(q * 2 + b // BLOCKS, b)
            for i in range(2):
                sp.wait_ge(sem("y_final"), i + 1)
                sp.dma_start(o[0][0, 128 * i:128 * i + 128, :], x1[:, i, :]).then_inc(sem("stored"), 16)
            sp.wait_ge(sem("y_final"), 3)
            sp.dma_start(o[1].rearrange("b t n -> (b t) n"), x1[0:TS, 2, :]).then_inc(sem("stored"), 16)
            sp.wait_ge(sem("stored"), stored + 48)

        @block.gpsimd
        def _(pool):
            n_self = [0]

            def po(ins, name=None):
                if name is None:
                    n_self[0] += 1
                    ins.then_inc(sem("pool_self"), 1)
                    pool.wait_ge(sem("pool_self"), n_self[0])
                else:
                    ins.then_inc(says_now(name), 1)

            g = nc.gpsimd
            po(g.memset(ident[:], 0.0))
            po(g.affine_select(out=ident[:], in_=ident[:], compare_op=ALU.not_equal, fill=1.0, base=0,
                               pattern=[[-1, 128]], channel_multiplier=1), "ident_ready")
            po(g.memset(wgate[:], 0.0))
            po(g.memset(wax[:], 0.0), "weights_zero")
            g.memset(BB[:], 0.0).then_inc(says_now("bb_zero"), 1)
            po(g.memset(seg[:], 1.0))
            po(g.memset(seg[:, 0:1], 0.0))
            po(g.memset(seg[:, TP:T:NT], 0.0), "seg_ready")
            po(g.memset(causal[:], 1.0))
            for c in (0, 256):
                po(g.affine_select(out=causal[:, c:c + 128], in_=causal[:, c:c + 128], compare_op=ALU.is_ge, fill=0.0,
                                   base=0, pattern=[[1, 128]], channel_multiplier=-1))
            po(g.affine_select(out=causal[:, 384:416], in_=causal[:, 384:416], compare_op=ALU.is_ge, fill=0.0,
                               base=0, pattern=[[1, TS]], channel_multiplier=-1))
            cs = causal[:, 384:416].rearrange("p (b t) -> p b t", b=NB)
            po(g.affine_select(out=cs, in_=cs, compare_op=ALU.is_ge, fill=0.0, base=0, pattern=[[-NT, NB], [0, NT]],
                               channel_multiplier=1), "causal_ready")
            po(g.memset(sel4[:], 0.0))
            po(g.affine_select(out=sel4[:], in_=sel4[:], compare_op=ALU.not_equal, fill=1.0, base=0,
                               pattern=[[-1, H], [0, 128]], channel_multiplier=1), "sel4_ready")
            po(g.memset(scm[:], 0.0))
            po(g.memset(wsm[:], 1.0))
            po(g.affine_select(out=wsm[:], in_=wsm[:], compare_op=ALU.is_ge, fill=0.0, base=0,
                               pattern=[[0, H], [-NT, NB]], channel_multiplier=1))
            po(g.affine_select(out=wsm[:], in_=wsm[:], compare_op=ALU.is_ge, fill=0.0, base=NT - 1,
                               pattern=[[0, H], [NT, NB]], channel_multiplier=-1), "ind_ready")
            po(g.iota(iota_e[:], pattern=[[1, NE]], base=0, channel_multiplier=0, allow_small_or_imprecise_dtypes=True))
            po(g.iota(iota_s[:], pattern=[[1, SLOTS]], base=1, channel_multiplier=0, allow_small_or_imprecise_dtypes=True))
            po(g.iota(half[:], pattern=[[1, 2], [0, SLOTS]], base=0, channel_multiplier=0, allow_small_or_imprecise_dtypes=True))
            for x in range(3):
                po(g.iota(selid[32 * x:32 * x + 32, :], pattern=[[-2, NPAIR + 1]], base=0, channel_multiplier=1,
                          allow_small_or_imprecise_dtypes=True))
            po(g.memset(ones_bf[:], 1.0))
            po(g.affine_select(out=upper[:], in_=ones_bf[:], compare_op=ALU.is_ge, fill=0.0, base=0,
                               pattern=[[1, 128]], channel_multiplier=-1))
            bias_cols = [[("exp_b1", 0, 1536, 0)], [("exp_b1", 1536, 512, 0), ("exp_b2", 0, 1024, 512)]]

            def load_bias(part):
                for x in range(3):
                    for name, c_, n_, at_ in bias_cols[part]:
                        pool.dma_start(bias_in[32 * x:32 * x + 32, at_:at_ + n_], a[name][0][:, c_:c_ + n_]).then_inc(sem("bias_loaded"), 16)

            def bias_rest(part, step):
                pool.wait_ge(*at("bias_rounded", 3 * part + step + 1))
                r = slice(0, 96 if step == 0 else 32)
                po(g.tensor_tensor(bias_in[r], bias_in[r], bsplit[r, 1536 * part:1536 * part + 1536], ALU.subtract), "bias_rest")

            pool.wait_ge(*at("ms_ready", 3))
            load_bias(0)
            pool.wait_ge(*at("xn_used", 1))
            po(g.memset(rows[:], 0.0), "rows_zero")
            pool.wait_ge(*at("angle_ready", 2))
            po(g.memset(tab_r[:, :, 0:1], 1.0))
            po(g.memset(tab_i[:, :, 0:1], 0.0))
            po(g.tensor_copy(tab_r[:, :, 1:2], sm[:, 6, :].unsqueeze(2)))
            po(g.tensor_copy(tab_i[:, :, 1:2], sm[:, 7, :].unsqueeze(2)))
            pr, pi, q1, q2, q3 = sm[:, 20, :], sm[:, 21, :], sm[:, 22, :], sm[:, 23, :], sm[:, 24, :]
            po(g.tensor_copy(pr, sm[:, 6, :]))
            po(g.tensor_copy(pi, sm[:, 7, :]))
            n = 2
            while n < TP:
                po(g.tensor_tensor(q1, pr, pr, ALU.mult))
                po(g.tensor_tensor(q2, pi, pi, ALU.mult))
                po(g.tensor_tensor(q3, pr, pi, ALU.mult))
                po(g.tensor_tensor(pr, q1, q2, ALU.subtract))
                po(g.tensor_tensor(pi, q3, q3, ALU.add))
                prb, pib = (spread(v.unsqueeze(2), 2, n) for v in (pr, pi))
                po(g.tensor_tensor(pt1[:, :, 0:n], tab_r[:, :, 0:n], prb, ALU.mult))
                po(g.tensor_tensor(pt2[:, :, 0:n], tab_i[:, :, 0:n], pib, ALU.mult))
                po(g.tensor_tensor(tab_r[:, :, n:2 * n], pt1[:, :, 0:n], pt2[:, :, 0:n], ALU.subtract))
                po(g.tensor_tensor(pt1[:, :, 0:n], tab_r[:, :, 0:n], pib, ALU.mult))
                po(g.tensor_tensor(pt2[:, :, 0:n], tab_i[:, :, 0:n], prb, ALU.mult))
                po(g.tensor_tensor(tab_i[:, :, n:2 * n], pt1[:, :, 0:n], pt2[:, :, 0:n], ALU.add))
                n *= 2
            for k, tb in enumerate((tab_r, tab_i)):
                for j in range(J5):
                    ins = g.tensor_copy(tb[:, j, TP:T].rearrange("p (b t) -> p b t", b=NB),
                                        spread(tb[:, j, 0:NT].unsqueeze(1), 1, NB))
            po(ins, "table_ready")
            pool.wait_ge(*at("table_ready", 1))
            po(g.memset(E[:], 0.0), "e_zero")
            for j in range(J5):
                pool.wait_ge(*at("s5_scanned", j + 1))
                if j >= 2:
                    pool.wait_ge(*at("s5_used", j - 1))
                b = j % 2
                po(g.tensor_tensor(s_r[:, b, :], tab_r[:, j, :], w_r[:, b, :], ALU.mult))
                po(g.tensor_tensor(t_pool[:], tab_i[:, j, :], w_i[:, b, :], ALU.mult))
                po(g.tensor_tensor(s_r[:, b, :], s_r[:, b, :], t_pool[:], ALU.subtract))
                po(g.tensor_tensor(s_i[:, b, :], tab_i[:, j, :], w_r[:, b, :], ALU.mult))
                po(g.tensor_tensor(t_pool[:], tab_r[:, j, :], w_i[:, b, :], ALU.mult))
                po(g.tensor_tensor(s_i[:, b, :], s_i[:, b, :], t_pool[:], ALU.add))
                for x, s in enumerate((s_r, s_i)):
                    g.tensor_copy(fin5[:, x, 0, j:j + 1], s[:, b, TP - 1:TP])
                    ins = g.tensor_copy(fin5[:, x, 1:, j:j + 1], s[:, b, TP + NT - 1:T:NT].unsqueeze(2))
                po(ins, "s5_turned")
                if j == 3:
                    bias_rest(0, 0)
            bias_rest(0, 1)
            for i in range(3):
                b, f = FILLS[f"kt{i}"]
                pool.wait_ge(drained[b], f + 1)
            pool.wait_ge(*at("rtok_ready", 1))
            pool.wait_ge(drained[FILLS["rows"][0]], FILLS["rows"][1] + 1)
            pool.wait_ge(*at("s5_turned", J5))
            po(g.tensor_tensor(kw[:], k_tok[:, 0:2, :].rearrange("p i (h k) -> p i h k", h=H),
                               spread(rtok[:, 0:2, 64:64 + H].unsqueeze(3), 3, DK), ALU.mult), "kw_ready")
            pool.wait_ge(*at("wsm_ready", 1))
            pool.wait_ge(*at("cb_used", 1))
            for n in ("va2", "vb2"):
                b, f = FILLS[n]
                pool.wait_ge(drained[b], f + 1)
            pool.wait_ge(*at("ones_ready", 1))
            for h in range(H):
                po(g.tensor_tensor(vw[:, h], spread(v_tok[0:TS, 2, h, :].unsqueeze(1), 1, NB),
                                   spread(wsm[:, h, :].unsqueeze(2), 2, 129), ALU.mult), "vw_ready")
            pool.wait_ge(*at("bias_rounded", 3))
            load_bias(1)
            bias_rest(1, 0)
            pool.wait_ge(*at("c0_used", 1))
            b, f = FILLS["dec"]
            pool.wait_ge(drained[b], f + 1)
            for h in range(H):
                g.tensor_tensor(c0[:, h], c0[:, h], spread(dec[:, h, :].unsqueeze(2), 2, 129),
                                ALU.mult).then_inc(says_now("c_decayed"), 1)
            bias_rest(1, 1)

        @block.scalar
        def _(act):
            A = nc.scalar.activation

            def copy_out(name, out, view, scale=1.0):
                await_fill(act, name)
                nc.scalar.activation(out, view, ACT.Copy, scale=scale).then_inc(drained[FILLS[name][0]], 1)

            for name, src in VECTORS[:4]:
                load_vector(act, name, src)
            act.wait_ge(*at("nst_set", 1))
            A(nst[:, 12:13], nst[:, 8:9], ACT.Sqrt).then_inc(says_now("table_loaded"), 1)
            for i, (t0, n) in enumerate(TILES):
                act.wait_ge(sem(f"x_loaded{i}"), 16)
                A(x1[0:n, i, :], xn[0:n, i, :], ACT.Square, accum_out=nst[0:n, i:i + 1]).then_inc(says_now("ms_ready"), 1)
                act.wait_ge(*at("ms_ready", i + 1))
                A(nst[:, 4 + i:5 + i], nst[:, i:i + 1], ACT.Sqrt, scale=1.0 / D, bias=nst[:, 8:9]).then_inc(says_now("root_ready"), 1)
            await_fill(act, "vec")
            A(vecs[:, 0:NVEC], bank("vec")[:, 0:NVEC], ACT.Copy).then_inc(drained[FILLS["vec"][0]], 1)
            act.wait_ge(drained[FILLS["vec"][0]], 1)
            act.wait_ge(sem("step_loaded"), 32)
            A(sm[:, 1, :], sm[:, 0, :], ACT.Exp).then_inc(says_now("step_ready"), 1)
            act.wait_ge(*at("angle_reduced", 1))
            A(sm[:, 5, :], sm[:, 2, :], ACT.Exp).then_inc(says_now("mag_ready"), 1)
            A(rsm[:, 0:2], vec("rg_lambda"), ACT.Abs).then_inc(says_now("act_rg"), 1)
            act.wait_ge(*at("act_rg", 1))
            A(rsm[:, 0:2], rsm[:, 0:2], ACT.Exp, scale=-1.0).then_inc(says_now("act_rg"), 1)
            A(sm[:, 6, :], sm[:, 9, :], ACT.Sin).then_inc(says_now("angle_ready"), 1)
            A(sm[:, 7, :], sm[:, 8, :], ACT.Sin).then_inc(says_now("angle_ready"), 1)
            for x in range(2):
                copy_out(f"u{x}", uT[:, x, :], bank(f"u{x}")[:, 0:T])
            act.wait_ge(*at("gate_abs", 1))
            A(gsm[0:H, 2, :], gsm[0:H, 2, :], ACT.Exp, scale=-1.0).then_inc(says_now("gate_exp"), 1)
            for x in range(2):
                await_fill(act, f"xr{x}")
                A(xpP[:, x, 3:], bank(f"xr{x}")[:, 0:TP], ACT.Copy).then_inc(says_now("xp_ready"), 1)
                A(xpS[:, x, :, 3:], bank(f"xr{x}")[:, TP:T].rearrange("p (b t) -> p b t", b=NB), ACT.Copy).then_inc(drained[FILLS[f"xr{x}"][0]], 1)
            for x in range(2):
                copy_out(f"gr{x}", gate[:, x, :], bank(f"gr{x}")[:, 0:T])
            copy_out("par", parT[:, 0:224], bank("par")[:, 0:224])
            def bias_round(part, step):
                if step == 0:
                    act.wait_ge(sem("bias_loaded"), 48 + 96 * part)
                else:
                    act.wait_ge(*at("bias_rest", 2 * part + step))
                r = slice(0, (96, 64, 32)[step])
                last = part == 1 and step == 2
                A(bsplit[r, 1536 * part:1536 * part + 1536], bias_in[r], ACT.Copy).then_inc(
                    says_now("bias_ready" if last else "bias_rounded"), 1)

            copy_out("bt", wB[:], bank("bt").rearrange("p (x n) -> p x n", x=4))
            await_fill(act, "ct")
            A(wC[:, 0:2, :], bank("ct")[:, 0:256].rearrange("p (x n) -> p x n", x=2), ACT.Copy).then_inc(says_now("wc_ready"), 1)
            A(wC[:, 2:4, :], bank("ct")[:, 256:512].rearrange("p (x n) -> p x n", x=2), ACT.Copy, scale=-1.0).then_inc(drained[FILLS["ct"][0]], 1)
            for h in range(2):
                copy_out(f"q{h}", qT[:, h, :], bank(f"q{h}")[:, 0:T])
            bias_round(0, 0)
            act.wait_ge(*at("gate_rows", 1))
            act.wait_ge(*at("rows_zero", 1))
            A(rows[32:32 + H, :], gsm[0:H, 7, :], ACT.Exp, scale=-1.0).then_inc(says_now("gate_rows_exp"), 1)
            A(rows[64:64 + H, :], gsm[0:H, 5, :], ACT.Exp).then_inc(says_now("gate_rows_exp"), 1)
            A(gsm[0:H, 6, 0:TS + NB], gsm[0:H, 6, 0:TS + NB], ACT.Exp).then_inc(says_now("gate_rows_exp"), 1)
            for h in range(2, H):
                copy_out(f"q{h}", qT[:, h, :], bank(f"q{h}")[:, 0:T])
            for h in range(2):
                copy_out(f"k{h}", kT[:, h, :], bank(f"k{h}")[:, 0:T], scale=DK ** -0.5)
            act.wait_ge(*at("gate_poly", 1))
            A(rt[:], rt[:], ACT.Tanh, scale=math.sqrt(2.0 / math.pi)).then_inc(says_now("gate_tanh"), 1)
            for x in range(2):
                await_fill(act, f"r{x}")
                A(rr[:, x, :], bank(f"r{x}")[:, 0:T], ACT.Sigmoid, bias=vec("rg_ba", x)).then_inc(drained[FILLS[f"r{x}"][0]], 1)
            for x in range(2):
                await_fill(act, f"i{x}")
                A(ri[:, x, :], bank(f"i{x}")[:, 0:T], ACT.Sigmoid, bias=vec("rg_bx", x)).then_inc(drained[FILLS[f"i{x}"][0]], 1)
            for h in range(2, H):
                copy_out(f"k{h}", kT[:, h, :], bank(f"k{h}")[:, 0:T], scale=DK ** -0.5)

            def v_out(name, i, n, c):
                await_fill(act, name)
                if i < 2:
                    A(v_tok[0:n, i, 2 * c:2 * c + 2, 0:128], bank(name)[0:n, 0:256].rearrange("p (h v) -> p h v", h=2), ACT.Copy).then_inc(
                        drained[FILLS[name][0]], 1)
                else:
                    A(v_tok[0:n, i, 2 * c, 0:128], bank(name)[0:n, 0:128], ACT.Copy).then_inc(says_now("v_half"), 1)
                    A(v_tok[0:n, i, 2 * c + 1, 0:128], bank(name)[n:2 * n, 0:128], ACT.Copy).then_inc(says_now("v_half"), 1)
                    act.wait_ge(*at("v_half", 2 * c + 2))
                    act.sem_inc(drained[FILLS[name][0]], 1)

            def o_out(name, i, n, c):
                await_fill(act, name)
                if i < 2:
                    A(o_tok[0:n, i, 256 * c:256 * c + 256], bank(name)[0:n, 0:256], ACT.Sigmoid).then_inc(drained[FILLS[name][0]], 1)
                else:
                    for x in range(2):
                        A(o_tok[0:n, i, 256 * c + 128 * x:256 * c + 128 * x + 128], bank(name)[n * x:n * x + n, 0:128],
                          ACT.Sigmoid).then_inc(says_now("o_half"), 1)
                    act.wait_ge(*at("o_half", 2 * c + 2))
                    act.sem_inc(drained[FILLS[name][0]], 1)

            for i, (t0, n) in enumerate(TILES):
                v_out(f"va{i}", i, n, 0)
            act.wait_ge(*at("rg_decay", 1))
            act.wait_ge(*at("gate_ready", 1))
            for x in range(2):
                act.wait_ge(drained[FILLS["r1"][0]], FILLS["r1"][1] + 1)
                act.wait_ge(drained[FILLS["r0"][0]], FILLS["r0"][1] + 1)
                A(rt[:, x, :], rr[:, x, :], ACT.Tanh, scale=rsm[:, 4 + x:5 + x]).then_inc(says_now("rg_tanh"), 1)
            act.wait_ge(*at("rg_tanh", 2))
            for x in range(2):
                A(rr[:, x, :], rr[:, x, :], ACT.Exp, scale=rsm[:, 6 + x:7 + x]).then_inc(says_now("rg_a"), 1)
            for i, (t0, n) in enumerate(TILES):
                v_out(f"vb{i}", i, n, 1)
                if i == 0:
                    act.wait_ge(*at("rg_ratio", 1))
                    A(rt[:], rt[:], ACT.Sqrt).then_inc(says_now("rg_root"), 1)
            for i, (t0, n) in enumerate(TILES):
                o_out(f"oa{i}", i, n, 0)
            bias_round(0, 1)
            for i, (t0, n) in enumerate(TILES):
                o_out(f"ob{i}", i, n, 1)
            act.wait_ge(*at("ones_ready", 1))
            await_fill(act, "rows")
            A(rtok[:, 0:2, :], bank("rows")[:, 0:256].rearrange("p (i n) -> p i n", i=2), ACT.Copy).then_inc(says_now("rtok_ready"), 1)
            A(rtok[0:TS, 2, :], bank("rows")[0:TS, 256:384], ACT.Copy).then_inc(drained[FILLS["rows"][0]], 1)
            for h in range(H):
                act.wait_ge(*at("e_arg", h + 1))
                A(E[:, h, :], E[:, h, :], ACT.Exp, scale=-1.0).then_inc(says_now("e_exp"), 1)
            act.wait_ge(*at("s5_turned", J5))
            for i, (t0, n) in enumerate(TILES):
                copy_out(f"kt{i}", k_tok[0:n, i, :], bank(f"kt{i}")[0:n, :])
            copy_out("dec", dec[:], bank("dec")[:, 0:H * NB].rearrange("p (h b) -> p h b", h=H))
            bias_round(0, 2)
            act.wait_ge(*at("s5_poly", 1))
            A(rt[:], rt[:], ACT.Tanh, scale=math.sqrt(2.0 / math.pi)).then_inc(says_now("s5_tanh"), 1)
            await_fill(act, "rgT")
            A(stage[0:9, 1:3, :], bank("rgT")[0:9, 0:256].rearrange("p (x n) -> p x n", x=2), ACT.Copy).then_inc(says_now("rg_staged"), 1)
            A(stage[0:27, 3:5, :], bank("rgT")[0:27, 256:512].rearrange("p (x n) -> p x n", x=2), ACT.Copy).then_inc(says_now("rg_staged"), 1)
            act.wait_ge(*at("rg_staged", 2))
            act.sem_inc(drained[FILLS["rgT"][0]], 1)
            await_fill(act, "s5T")
            A(stage[0:72, 5:7, :], bank("s5T")[0:72, 0:256].rearrange("p (x n) -> p x n", x=2), ACT.Copy).then_inc(says_now("s5_staged"), 1)
            act.wait_ge(*at("s5_staged", 1))
            act.sem_inc(drained[FILLS["s5T"][0]], 1)
            for i, (t0, n) in enumerate(TILES):
                if i == 2:
                    bias_round(1, 0)
                    for hh in range(2):
                        await_fill(act, f"cp{hh}")
                        A(cP[:, 2 * hh:2 * hh + 2, :], bank(f"cp{hh}")[:, 0:258].rearrange("p (h v) -> p h v", h=2), ACT.Copy).then_inc(drained[FILLS[f"cp{hh}"][0]], 1)
                act.wait_ge(*at("den_read", i + 1))
                for hh in range(2):
                    await_fill(act, f"nu{i}{hh}")
                    if hh or i:
                        act.wait_ge(*at("nsq_ready", 4 * i + 2 * hh))
                    for x in range(2):
                        A(t_dve[0:n, 128 * x:128 * x + 128], bank(f"nu{i}{hh}")[0:n, 129 * x:129 * x + 128], ACT.Square,
                          accum_out=rsm[0:n, 16 + 4 * i + 2 * hh + x:17 + 4 * i + 2 * hh + x]).then_inc(says_now("nsq_ready"), 1)
                if i >= 1:
                    c = slice(32, 40) if i == 1 else slice(40, 44)
                    act.wait_ge(*at("nvar_ready", i))
                    A(rsm[0:n, c], rsm[0:n, c], ACT.Sqrt).then_inc(says_now("nroot_ready"), 1)
            for x in range(2):
                await_fill(act, f"glu{x}")
                A(ri[:, x, :], bank(f"glu{x}")[:, 0:T], ACT.Sigmoid, bias=vec("s5_glu_b", x)).then_inc(drained[FILLS[f"glu{x}"][0]], 1)
            for hh in range(2):
                b, f = FILLS[f"cp{hh}"]
                act.wait_ge(drained[b], f + 1)
            for hh in range(2):
                A(nbuf[:, 32 + 2 * hh:34 + 2 * hh], cP[:, 2 * hh:2 * hh + 2, 128], ACT.Copy).then_inc(says_now("c_prompt"), 1)
            bias_round(1, 1)
            for h in range(H):
                await_fill(act, f"yT{h}")
                A(hT[:, 4 + h, :], bank(f"yT{h}")[:, 0:T], ACT.Copy, scale=vec("ml_norm_g", h)).then_inc(drained[FILLS[f"yT{h}"][0]], 1)
            bias_round(1, 2)
            await_fill(act, "nT")
            A(stage[0:36, 0, :], bank("nT")[0:36, 0:128], ACT.Copy).then_inc(says_now("n_staged"), 1)
            act.wait_ge(*at("n_staged", 1))
            act.sem_inc(drained[FILLS["nT"][0]], 1)
            for m, i in enumerate((0, 2, 1)):
                t0, n = TILES[i]
                act.wait_ge(*at("x1_added", m + 1))
                A(gfb[0:n, :], x1[0:n, i, :], ACT.Square, accum_out=st2[0:n, i:i + 1]).then_inc(says_now("ms2_ready"), 1)
                act.wait_ge(*at("ms2_ready", m + 1))
                A(st2[0:n, 4 + i:5 + i], st2[0:n, i:i + 1], ACT.Sqrt, scale=1.0 / D, bias=st2[0:n, 12:13]).then_inc(says_now("root2_ready"), 1)
                for hf in range(2):
                    name = f"h2T{2 * i + hf}"
                    copy_out(name, h2T[:, 4 * hf:4 * hf + 4, t0:t0 + n],
                             bank(name)[:, 0:4 * 128].rearrange("p (k n) -> p k n", k=4)[:, :, 0:n])
            act.wait_ge(*at("top_diff", 1))
            A(gk[:, :, 0:TOPK], gk[:, :, 0:TOPK], ACT.Exp).then_inc(says_now("top_exp"), 1)

            def first_gathered():
                for x in range(2):
                    act.wait_ge(sem("gather_ready"), 1 + x)
                    A(xg[:, 4 * x:4 * x + 4, :], psum[:, 6 + x, :].rearrange("p (k n) -> p k n", k=4), ACT.Copy).then_inc(sem("xg_copied"), 1)

            def pair_steps(gp):
                for x in range(2):
                    act.wait_ge(sem("g_clipped"), gp * 2 + 1 + x)
                    A(sg1[:, x, :], gact[:, x, :], ACT.Sigmoid, scale=1.702).then_inc(sem("sig_ready"), 1)
                act.wait_ge(sem("block_done"), gp * BLOCKS + 4)
                for x in range(2):
                    act.wait_ge(sem("gather_ready"), gp * 2 + 3 + x)
                    A(xg[:, 4 * x:4 * x + 4, :], psum[:, 6 + x, :].rearrange("p (k n) -> p k n", k=4), ACT.Copy).then_inc(sem("xg_copied"), 1)
                for x in range(2):
                    act.wait_ge(sem("aT_ready"), gp * 2 + 1 + x)
                    A(aT[:, 4 * x:4 * x + 4, :], psum[:, x, :].rearrange("p (k n) -> p k n", k=4), ACT.Copy).then_inc(sem("aT_copied"), 1)
                act.wait_ge(sem("sgt_ready"), gp + 1)
                A(sgt[:], psum[:, 6, 0:T], ACT.Copy).then_inc(sem("sgt_copied"), 1)
                act.wait_ge(sem("block_done"), gp * BLOCKS + 6)
                for x in range(2):
                    A(yb[:, x, :], psum[:, 4 + x, :], ACT.Copy).then_inc(sem("y_copied"), 1)

            def sweep(base):
                with act.Fori(0, NPAIR // 2) as q:
                    for u in range(2):
                        pair_steps(base + q * 2 + u)

            first_gathered()
            sweep(0)
            act.wait_ge(*at("count_ready", 1))
            most = act.value_load(cnt[0:1, 0:1], min_val=0, max_val=T)
            with act.If(most > SLOTS):
                with act.Fori(1, SWEEPS) as r:
                    with act.If(most > r * SLOTS):
                        for x in range(2):
                            act.wait_ge(sem("regather_ready"), r * 2 - 1 + x)
                            A(xg[:, 4 * x:4 * x + 4, :], psum[:, 6 + x, :].rearrange("p (k n) -> p k n", k=4), ACT.Copy).then_inc(sem("xg_recopied"), 1)
                        sweep(r * NPAIR)
            A(st2[:, 14:15], st2[:, 12:13], ACT.Sqrt).then_inc(sem("table_reloaded"), 1)
            act.wait_ge(sem("sums_done"), 1)
            for i, (t0, n) in enumerate(TILES):
                A(xn[0:n, i, :], x1[0:n, i, :], ACT.Square, accum_out=st2[0:n, i:i + 1]).then_inc(sem("ms3_ready"), 1)
                act.wait_ge(sem("ms3_ready"), i + 1)
                A(st2[0:n, 4 + i:5 + i], st2[0:n, i:i + 1], ACT.Sqrt, scale=1.0 / D, bias=st2[0:n, 12:13]).then_inc(sem("root3_ready"), 1)

        @block.vector
        def _(dve):
            n_self = [0]
            V = nc.vector

            def dv(ins, s=None):
                if s is None:
                    n_self[0] += 1
                    ins.then_inc(sem("dve_self"), 1)
                    dve.wait_ge(sem("dve_self"), n_self[0])
                else:
                    ins.then_inc(s, 1)

            def drains(ins, name):
                b, n = FILLS[name]
                ins.then_inc(drained[b], 1)
                dve.wait_ge(drained[b], n + 1)

            def says(ins, name, n):
                ins.then_inc(says_now(name), 1)
                dve.wait_ge(*at(name, n))

            TT, TSC, STT = V.tensor_tensor, V.tensor_scalar, V.scalar_tensor_tensor

            def log1p(out, y, tmp1, tmp2):
                dv(TSC(tmp1, y, 2.0, None, ALU.add))
                dv(V.reciprocal(tmp1, tmp1))
                dv(TT(tmp1, tmp1, y, ALU.mult))
                dv(TT(tmp2, tmp1, tmp1, ALU.mult))
                dv(TSC(out, tmp2, 1.0 / 19.0, None, ALU.mult))
                for k in range(8, 0, -1):
                    dv(STT(out=out, in0=out, scalar=1.0 / (2 * k + 1), in1=tmp2, op0=ALU.add, op1=ALU.mult))
                dv(STT(out=out, in0=out, scalar=1.0, in1=tmp1, op0=ALU.add, op1=ALU.mult))
                dv(TSC(out, out, 2.0, None, ALU.mult))

            dv(V.memset(st2[:], 1.0))
            dv(V.memset(st2[:, 12:13], EPS))
            dv(V.memset(nst[:], 1.0))
            says(V.memset(nst[:, 8:9], EPS), "nst_set", 1)
            for i, (t0, n) in enumerate(TILES):
                dve.wait_ge(*at("root_ready", i + 1))
                dv(V.reciprocal(nst[:, 4 + i:5 + i], nst[:, 4 + i:5 + i]))
                says(TSC(xn[0:n, i, :], xn[0:n, i, :], nst[0:n, 4 + i:5 + i], None, ALU.mult), "xn_ready", i + 1)
            dve.wait_ge(drained[FILLS["vec"][0]], 1)
            for k in range(6):
                i, hf = k // 2, k % 2
                t0, n = TILES[i]
                await_fill(dve, f"hT{k}")
                drains(TT(hT[:, 4 * hf:4 * hf + 4, t0:t0 + n], bank(f"hT{k}").rearrange("p (k n) -> p k n", k=4)[:, :, 0:n],
                          spread(vec("norm1_g")[:, 4 * hf:4 * hf + 4].unsqueeze(2), 2, n), ALU.mult), f"hT{k}")
            lr, li = vec("s5_lambda_re"), vec("s5_lambda_im")
            dve.wait_ge(*at("step_ready", 1))
            dv(TT(sm[:, 2, :], lr, sm[:, 1, :], ALU.mult))
            dv(TT(sm[:, 3, :], li, sm[:, 1, :], ALU.mult))
            magic = 12582912.0
            dv(TSC(sm[:, 4, :], sm[:, 3, :], 1.0 / (2 * math.pi), None, ALU.mult))
            dv(TSC(sm[:, 4, :], sm[:, 4, :], magic, None, ALU.add))
            dv(TSC(sm[:, 4, :], sm[:, 4, :], magic, None, ALU.subtract))
            p1, p2 = 6.28125, 0.0019350051879882812
            p3 = 2 * math.pi - p1 - p2
            dv(STT(out=sm[:, 8, :], in0=sm[:, 4, :], scalar=-p1, in1=sm[:, 3, :], op0=ALU.mult, op1=ALU.add))
            dv(STT(out=sm[:, 8, :], in0=sm[:, 4, :], scalar=-p2, in1=sm[:, 8, :], op0=ALU.mult, op1=ALU.add))
            dv(STT(out=sm[:, 8, :], in0=sm[:, 4, :], scalar=-p3, in1=sm[:, 8, :], op0=ALU.mult, op1=ALU.add))
            dv(TSC(sm[:, 8, :], sm[:, 8, :], 3.1415925, -3.1415925, ALU.min, ALU.max))
            dv(STT(out=sm[:, 9, :], in0=sm[:, 8, :], scalar=-1.0, in1=sm[:, 8, :], op0=ALU.mult, op1=ALU.min))
            says(TSC(sm[:, 9, :], sm[:, 9, :], math.pi / 2, None, ALU.add), "angle_reduced", 1)
            dve.wait_ge(*at("mag_ready", 1))
            dve.wait_ge(*at("angle_ready", 2))
            mag = sm[:, 5, :]
            dv(TT(sm[:, 10, :], mag, sm[:, 6, :], ALU.mult))
            dv(TT(sm[:, 11, :], mag, sm[:, 7, :], ALU.mult))
            dv(TT(sm[:, 14, :], lr, lr, ALU.mult))
            dv(TT(sm[:, 15, :], li, li, ALU.mult))
            dv(TT(sm[:, 14, :], sm[:, 14, :], sm[:, 15, :], ALU.add))
            dv(V.reciprocal(sm[:, 14, :], sm[:, 14, :]))
            dv(TSC(sm[:, 15, :], sm[:, 10, :], -1.0, None, ALU.add))
            dv(TT(sm[:, 16, :], sm[:, 15, :], lr, ALU.mult))
            dv(TT(sm[:, 17, :], sm[:, 11, :], li, ALU.mult))
            dv(TT(sm[:, 12, :], sm[:, 16, :], sm[:, 17, :], ALU.add))
            dv(TT(sm[:, 12, :], sm[:, 12, :], sm[:, 14, :], ALU.mult))
            dv(TT(sm[:, 16, :], sm[:, 11, :], lr, ALU.mult))
            dv(TT(sm[:, 17, :], sm[:, 15, :], li, ALU.mult))
            dv(TT(sm[:, 13, :], sm[:, 16, :], sm[:, 17, :], ALU.subtract))
            dv(TT(sm[:, 13, :], sm[:, 13, :], sm[:, 14, :], ALU.mult))
            dve.wait_ge(sem("b_loaded"), 64)
            dve.wait_ge(*at("bb_zero", 1))
            zr, zi = (spread(sm[:, k, :].unsqueeze(2), 2, C5) for k in (12, 13))
            for x, (za, zb, op) in enumerate(((zr, zi, ALU.subtract), (zi, zr, ALU.add))):
                dv(TT(b_t[:, 0], b_in[:, 0], za, ALU.mult))
                dv(TT(b_t[:, 1], b_in[:, 1], zb, ALU.mult))
                for gg in range(2):
                    q = slice(64 * gg, 64 * gg + 64)
                    says(TT(BB[q, x * J5:(x + 1) * J5, gg, :], b_t[q, 0], b_t[q, 1], op), "bb_ready", 2 * x + gg + 1)
            dve.wait_ge(sem("c_loaded"), 64)
            dve.wait_ge(*at("ident_ready", 1))
            for gg in range(2):
                dv(V.tensor_reduce(rsm[:, 10 + gg:11 + gg],
                                   ident[:].rearrange("p (j g c) -> p g j c", g=2, c=C5)[:, gg], AX.XY, ALU.add))
            for gg in range(2):
                says(TSC(CBk[:, :, 64 * gg:64 * gg + 64], c_in[:], rsm[:, 10 + gg:11 + gg], None, ALU.mult), "cb_ready", gg + 1)
            ig, fg, ge, s3, s4, wd, sd, mt = (gsm[0:H, k, :] for k in range(8))
            dve.wait_ge(sem("gb_loaded"), 32)
            await_fill(dve, "gates")
            dv(TSC(ig, bank("gates")[0:H, 0:T], gb[:, 0:1], None, ALU.add))
            drains(V.tensor_copy(fg, bank("gates")[32:32 + H, 0:T]), "gates")
            dv(TSC(fg, fg, gb[:, 1:2], None, ALU.add))
            says(STT(out=ge, in0=fg, scalar=-1.0, in1=fg, op0=ALU.mult, op1=ALU.max), "gate_abs", 1)
            dve.wait_ge(*at("act_rg", 2))
            log1p(rsm[:, 2:4], rsm[:, 0:2], rsm[:, 8:10], rsm[:, 12:14])
            dv(TSC(rsm[:, 8:10], vec("rg_lambda"), -1.0, 0.0, ALU.mult, ALU.max))
            dv(TT(rsm[:, 2:4], rsm[:, 2:4], rsm[:, 8:10], ALU.add))
            dv(TSC(rsm[:, 4:6], rsm[:, 2:4], RC, None, ALU.mult))
            says(TSC(rsm[:, 6:8], rsm[:, 2:4], -RC, None, ALU.mult), "rg_decay", 1)
            dve.wait_ge(*at("gate_exp", 1))
            log1p(s3, ge, s4, wd)
            dv(TSC(fg, fg, 0.0, None, ALU.min))
            dv(TT(fg, fg, s3, ALU.subtract))
            dve.wait_ge(*at("seg_ready", 1))
            dve.wait_ge(*at("rows_zero", 1))
            bb, aa, mm = s3, rows[0:H, :], s4
            dv(V.tensor_tensor_scan(bb, seg[0:H, :], fg, 0.0, ALU.mult, ALU.add))
            dv(TT(aa, ig, bb, ALU.subtract))
            dv(V.tensor_tensor_scan(mm[:, 0:TP], aa[:, 0:TP], aa[:, 0:TP], 0.0, ALU.max, ALU.max))
            dv(TT(mm[:, TP:T:NT], aa[:, TP:T:NT], m0[:], ALU.max))
            for t in range(1, NT):
                dv(TT(mm[:, TP + t:T:NT], aa[:, TP + t:T:NT], mm[:, TP + t - 1:T:NT], ALU.max))
            says(TT(mt, bb, mm, ALU.add), "m_rows", 1)
            dv(TSC(wd[:, 0:TP], aa[:, 0:TP], mm[:, TP - 1:TP], None, ALU.subtract))
            mlast = mm[:, TP + NT - 1:T:NT]
            by_b = lambda v: v.rearrange("p (b t) -> p b t", b=NB)
            dv(TT(by_b(wd[:, TP:T]), by_b(aa[:, TP:T]), spread(mlast.unsqueeze(2), 2, NT), ALU.subtract))
            dv(TT(by_b(sd[:, 0:TS]), spread(m0[:].unsqueeze(2), 2, NT), by_b(mm[:, TP:T]), ALU.subtract))
            says(TT(sd[:, TS:TS + NB], m0[:], mlast, ALU.subtract), "gate_rows", 1)
            ip = FILLS["par"]
            dve.wait_ge(drained[ip[0]], ip[1] + 1)
            dv(V.memset(xpP[:, :, 0:3], 0.0))
            for x in range(2):
                dv(V.tensor_copy(xpS[:, x, :, 0:3], parT[:, 128 + 48:128 + 96].rearrange("p (b t x) -> p x b t", t=3, x=2)[:, x]))
            s0 = [parT[:, 64 * x:64 * x + 64].rearrange("p (b j) -> p b j", b=NB) for x in range(2)]
            ar, ai = (spread(sm[:, k, :].unsqueeze(1), 1, NB) for k in (10, 11))
            as5 = [stage[:, x, 0:64].rearrange("p (b j) -> p b j", b=NB) for x in range(4)]
            dv(TT(as5[0], s0[0], ar, ALU.mult))
            dv(TT(as5[1], s0[1], ai, ALU.mult))
            dv(TT(as5[2], as5[0], as5[1], ALU.subtract))
            dv(TT(as5[0], s0[1], ar, ALU.mult))
            dv(TT(as5[1], s0[0], ai, ALU.mult))
            dv(TT(as5[3], as5[0], as5[1], ALU.add))
            dv(TT(d0s[:], spread(seg[:, TP:T].unsqueeze(1), 1, J5), spread(mag.unsqueeze(2), 2, TS), ALU.mult))
            for x in range(2):
                fx = FILLS[f"xr{x}"]
                dve.wait_ge(*at("xp_ready", x + 1))
                dve.wait_ge(drained[fx[0]], fx[1] + 1)
                cw = lambda t: vec("rg_conv_w", 2 * t + x)
                outs = (xc[:, x, 0:TP], by_b(xc[:, x, TP:T]))
                ins = (lambda t: xpP[:, x, t:t + TP], lambda t: xpS[:, x, :, t:t + NT])
                for k in range(2):
                    dv(TSC(outs[k], ins[k](0), cw(0), vec("rg_conv_b", x), ALU.mult, ALU.add))
                for t in range(1, 4):
                    for k in range(2):
                        ins_ = STT(out=outs[k], in0=ins[k](t), scalar=cw(t), in1=outs[k], op0=ALU.mult, op1=ALU.add)
                        if t == 3 and k == 1:
                            says(ins_, "xc_ready", x + 1)
                        else:
                            dv(ins_)
            for x in range(2):
                dv(V.tensor_copy(cvfin[:, x, 0:3], xpP[:, x, TP:TP + 3]))
                dv(V.tensor_copy(cvfin[:, x, 3:27].rearrange("p (b t) -> p b t", b=NB), xpS[:, x, :, NT:NT + 3]))
            dve.wait_ge(*at("gate_rows_exp", 3))
            dve.wait_ge(*at("ind_ready", 1))
            for b in range(NB):
                V.tensor_copy(scm[:, b, NT * b:NT * b + NT], sd[:, NT * b:NT * b + NT]).then_inc(says_now("scm_ready"), 1)
            def gelu_arg(y, tmp, name):
                dv(TT(tmp, y, y, ALU.mult))
                dv(TSC(tmp, tmp, 0.044715, 1.0, ALU.mult, ALU.add))
                says(TT(tmp, tmp, y, ALU.mult), name, 1)

            for x in range(2):
                b, f = FILLS[f"gr{x}"]
                dve.wait_ge(drained[b], f + 1)
            gelu_arg(gate[:], rt[:], "gate_poly")
            def s5_scan(j):
                b = j % 2
                if j == 0:
                    dve.wait_ge(*at("table_ready", 1))
                if j >= 2:
                    dve.wait_ge(*at("s5_turned", j - 1))
                for n in (f"bu{j}r", f"bu{j}i"):
                    await_fill(dve, n)
                br, bi = bank(f"bu{j}r")[:, 0:T], bank(f"bu{j}i")[:, 0:T]
                dv(TT(w_r[:, b, :], br, tab_r[:, j, :], ALU.mult))
                dv(TT(t_dve[:], bi, tab_i[:, j, :], ALU.mult))
                dv(TT(w_r[:, b, :], w_r[:, b, :], t_dve[:], ALU.add))
                drains(TT(w_i[:, b, :], bi, tab_r[:, j, :], ALU.mult), f"bu{j}i")
                drains(TT(t_dve[:], br, tab_i[:, j, :], ALU.mult), f"bu{j}r")
                dv(TT(w_i[:, b, :], w_i[:, b, :], t_dve[:], ALU.subtract))
                for x, w in enumerate((w_r, w_i)):
                    dv(TT(w[:, b, TP:T:NT], w[:, b, TP:T:NT], as5[2 + x][:, :, j], ALU.add))
                for x, w in enumerate((w_r, w_i)):
                    dv(V.tensor_tensor_scan(w[:, b, 0:TP], spread(mag[:, j:j + 1], 1, TP), w[:, b, 0:TP], 0.0, ALU.mult, ALU.add))
                    ins_ = V.tensor_tensor_scan(w[:, b, TP:T], d0s[:, j, :], w[:, b, TP:T], 0.0, ALU.mult, ALU.add)
                    if x == 0:
                        dv(ins_)
                    else:
                        says(ins_, "s5_scanned", j + 1)

            dve.wait_ge(*at("gate_tanh", 1))
            says(STT(out=gate[:], in0=rt[:], scalar=1.0, in1=gate[:], op0=ALU.add, op1=ALU.mult), "gate_ready", 1)
            s5_scan(0)
            s5_scan(1)
            for x in range(2):
                f1 = FILLS[f"i{x}"]
                dve.wait_ge(drained[f1[0]], f1[1] + 1)
            dv(TT(xc[:], xc[:], ri[:], ALU.mult))
            s5_scan(2)
            dve.wait_ge(*at("rg_tanh", 2))
            dve.wait_ge(*at("rg_a", 2))
            dv(TT(ri[:], rr[:], rr[:], ALU.mult))
            says(STT(out=rt[:], in0=ri[:], scalar=1.0, in1=rt[:], op0=ALU.add, op1=ALU.mult), "rg_ratio", 1)
            s5_scan(3)
            dve.wait_ge(*at("rg_root", 1))
            dv(TT(xc[:], xc[:], rt[:], ALU.mult))
            h0 = parT[:, 128 + 32:128 + 48].rearrange("p (b x) -> p x b", x=2)
            dv(TT(rsm[:, 48:64].rearrange("p (x b) -> p x b", x=2), rr[:, :, TP:T:NT], h0, ALU.mult))
            dv(TT(xc[:, :, TP:T:NT], xc[:, :, TP:T:NT], rsm[:, 48:64].rearrange("p (x b) -> p x b", x=2), ALU.add))
            dv(TT(rr[:], rr[:], spread(seg[:].unsqueeze(1), 1, 2), ALU.mult))
            for x in range(2):
                dv(V.tensor_tensor_scan(ri[:, x, :], rr[:, x, :], xc[:, x, :], 0.0, ALU.mult, ALU.add))
            dv(V.tensor_copy(rgfin[:, :, 0:1], ri[:, :, TP - 1:TP]))
            says(V.tensor_copy(rgfin[:, :, 1:9], ri[:, :, TP + NT - 1:T:NT]), "rgfin_ready", 1)

            s5_scan(4)
            s5_scan(5)
            s5_scan(6)
            s5_scan(7)
            dve.wait_ge(*at("w_in_used", 6))
            says(STT(out=hT[:, 2:4, :], in0=gate[:], scalar=0.5, in1=ri[:], op0=ALU.mult, op1=ALU.mult), "mix_ready", 1)
            says(V.memset(v_tok[:, :, :, 128:129], 1.0), "ones_ready", 1)
            dve.wait_ge(*at("e_zero", 1))
            dve.wait_ge(*at("causal_ready", 1))
            fr = FILLS["rows"]
            dve.wait_ge(drained[fr[0]], fr[1] + 1)
            dve.wait_ge(*at("rtok_ready", 1))
            dve.wait_ge(*at("ind_ready", 1))
            dv(TT(wsm[:], wsm[:], spread(rtok[0:TS, 2, 64:64 + H].unsqueeze(2), 2, NB), ALU.mult), says_now("wsm_ready"))

            def e_arg(h):
                await_fill(dve, f"mb{h}")
                mb = bank(f"mb{h}")
                dv(TSC(E[:, h, 0:256], mb[:, 0:256], rtok[:, 0, h:h + 1], 0.0, ALU.subtract, ALU.max))
                dv(TSC(E[:, h, 256:384], mb[:, 128:256], rtok[:, 1, h:h + 1], 0.0, ALU.subtract, ALU.max))
                drains(TSC(E[0:TS, h, 384:416], mb[0:TS, 256:288], rtok[0:TS, 2, h:h + 1], 0.0, ALU.subtract, ALU.max), f"mb{h}")
                dve.sem_inc(says_now("e_arg"), 1)

            def e_prob(h):
                dve.wait_ge(*at("e_exp", h + 1))
                dv(TT(E[:, h, :], E[:, h, :], causal[:], ALU.mult))
                await_fill(dve, f"st{h}")
                dv(TT(E[:, h, 0:384], bank(f"st{h}")[:, 0:384], E[:, h, 0:384], ALU.mult))
                drains(TT(E[0:TS, h, 384:416], bank(f"st{h}")[0:TS, 384:416], E[0:TS, h, 384:416], ALU.mult), f"st{h}")

            e_arg(0)
            for h in range(H):
                if h + 1 < H:
                    e_arg(h + 1)
                e_prob(h)
            dve.wait_ge(sem("c0_loaded"), 64)
            dv(V.tensor_copy(c0[:, :, :, 128], parT[:, 128:160].rearrange("p (b h) -> p h b", h=H)))
            dve.wait_ge(*at("s5_turned", J5))
            for h in range(H):
                await_fill(dve, f"sc{h}")
                drains(TT(qm[:, h], bank(f"sc{h}")[:, 0:NB * TS].rearrange("p (b t) -> p b t", b=NB),
                          spread(qT[:, h, TP:T].unsqueeze(1), 1, NB), ALU.mult), f"sc{h}")
            dve.sem_inc(says_now("qm_ready"), 1)
            for x in range(2):
                await_fill(dve, f"ys{x}")
                drains(STT(out=xc[:, x, :], in0=uT[:, x, :], scalar=vec("s5_d", x), in1=bank(f"ys{x}")[:, 0:T],
                           op0=ALU.mult, op1=ALU.add), f"ys{x}")
            gelu_arg(xc[:], rt[:], "s5_poly")
            dv(V.memset(rsm[:, 16:28], 1.0))
            dv(V.memset(rsm[:, 48:60], 1.0))
            def denominators(i):
                n, rc = TILES[i][1], rsm[:, 48 + 4 * i:52 + 4 * i]
                for hh in range(2):
                    await_fill(dve, f"nu{i}{hh}")
                    den, out = bank(f"nu{i}{hh}")[0:n, 128:258:129], rc[0:n, 2 * hh:2 * hh + 2]
                    dv(V.tensor_copy(out, den))
                    dv(STT(out=out, in0=den, scalar=-1.0, in1=out, op0=ALU.mult, op1=ALU.max))
                    ins_ = TT(out, out, rtok[0:n, i, 32 + 2 * hh:34 + 2 * hh], ALU.max)
                    says(ins_, "den_read", i + 1) if hh else dv(ins_)

            def outputs(tiles, part):
                n = TILES[tiles[0]][1]
                c0_, c1_ = 4 * tiles[0], 4 * tiles[-1] + 4
                rc, rv, sq = (rsm[0:n, at_ + c0_:at_ + c1_] for at_ in (48, 32, 16))
                dv(V.reciprocal(rc, rc))
                dve.wait_ge(*at("nsq_ready", c1_))
                dv(TT(rv, rc, rc, ALU.mult))
                dv(TT(rv, rv, sq, ALU.mult))
                says(TSC(rv, rv, 1.0 / DK, EPS, ALU.mult, ALU.add), "nvar_ready", part)
                dve.wait_ge(*at("nroot_ready", part))
                dv(V.reciprocal(rv, rv))
                dv(TT(rv, rv, rc, ALU.mult))
                for h in range(H):
                    for i in tiles:
                        name = f"nu{i}{h // 2}"
                        ot = o_tok[0:n, i, 128 * h:128 * h + 128]
                        ins_ = STT(out=ot, in0=bank(name)[0:n, 129 * (h % 2):129 * (h % 2) + 128],
                                   scalar=rv[:, 4 * (i - tiles[0]) + h:4 * (i - tiles[0]) + h + 1], in1=ot, op0=ALU.mult, op1=ALU.mult)
                        if h % 2:
                            drains(ins_, name)
                        else:
                            dv(ins_)
                    if part == 2:
                        dve.sem_inc(says_now("y3_ready"), 1)

            denominators(0)
            denominators(1)
            outputs((0, 1), 1)
            dve.wait_ge(*at("s5_tanh", 1))
            dv(STT(out=rt[:], in0=rt[:], scalar=1.0, in1=xc[:], op0=ALU.add, op1=ALU.mult))
            says(TSC(rt[:], rt[:], 0.5, None, ALU.mult), "s5_gelu", 1)
            denominators(2)
            outputs((2,), 2)
            for x in range(2):
                fgl = FILLS[f"glu{x}"]
                dve.wait_ge(drained[fgl[0]], fgl[1] + 1)
            says(TT(hT[:, 0:2, :], rt[:], ri[:], ALU.mult), "rg_used", 1)
            def new_memory(h):
                dve.wait_ge(*at("c_decayed", h + 1))
                for gidx, (b0, b1) in enumerate(CB):
                    name = f"cu{h}{gidx}"
                    await_fill(dve, name)
                    drains(TT(c0[:, h, b0:b1, :], c0[:, h, b0:b1, :],
                              bank(name)[:, 0:(b1 - b0) * 129].rearrange("p (b v) -> p b v", v=129), ALU.add), name)
                says(V.tensor_copy(nbuf[:, 0:32].rearrange("p (b h) -> p h b", h=H)[:, h, :], c0[:, h, :, 128]), "c_new", h + 1)

            for h in range(H):
                new_memory(h)
            dve.wait_ge(sem("x1_loaded"), 32)
            dve.wait_ge(sem("router_loaded"), 48)
            dve.wait_ge(sem("stored"), 16 * 10)

            def weighted_half(i, c):
                n, cols = TILES[i][1], slice(512 * c, 512 * c + 512)
                TT(xn[0:n, i, cols], x1[0:n, i, cols], g2b[0:n, cols], ALU.mult).then_inc(says_now("x2_ready"), 1)

            def scale_rows(m, i):
                n, rs = TILES[i][1], st2[0:TILES[i][1], 4 + i:5 + i]
                dve.wait_ge(*at("root2_ready", m + 1))
                dv(V.reciprocal(rs, rs))
                for hf in range(2):
                    await_fill(dve, f"h2T{2 * i + hf}")
                dv(TSC(xn[0:n, i, :], xn[0:n, i, :], rs, None, ALU.mult))

            for m, i in enumerate((0, 2, 1)):
                t0, n = TILES[i]
                if i < 2:
                    for c in range(2):
                        name = f"wo{i}{c}"
                        await_fill(dve, name)
                        xs = x1[0:n, i, 512 * c:512 * c + 512]
                        drains(TT(xs, xs, bank(name)[0:n, :], ALU.add), name)
                        if c == 1:
                            dve.sem_inc(says_now("x1_added"), 1)
                        weighted_half(i, c)
                        if i == 1 and c == 0:
                            scale_rows(0, 0)
                            scale_rows(1, 2)
                else:
                    await_fill(dve, "wo2")
                    for c in range(4):
                        xs = x1[0:n, i, 256 * c:256 * c + 256]
                        ins_ = TT(xs, xs, bank("wo2")[n * c:n * c + n, 0:256], ALU.add)
                        drains(ins_, "wo2") if c == 3 else dv(ins_)
                    dve.sem_inc(says_now("x1_added"), 1)
                    for c in range(2):
                        weighted_half(i, c)
            dv(V.memset(lg[:], 0.0))
            dv(V.memset(slot[:], 0.0))
            dv(V.memset(sgate[:], 0.0))
            dv(V.memset(yb[:], 0.0))
            dv(V.memset(sgt[:], 0.0))
            scale_rows(2, 1)
            await_fill(dve, "lg")
            for i, n in ((0, 128), (2, TS), (1, 128)):
                ins_ = STT(out=lg[0:n, i, :], in0=bank("lg")[0:n, NE * i:NE * i + NE], scalar=st2[0:n, 4 + i:5 + i],
                           in1=rbias[0:n, :], op0=ALU.mult, op1=ALU.add)
                drains(ins_, "lg") if i == 1 else dv(ins_)
            for i in range(3):
                dv(V.max(top[:, i, :], lg[:, i, :]))
                dv(V.max_index(topi[:, i, :], top[:, i, :], lg[:, i, :]))
            dv(V.tensor_copy(topf[:], topi[:]))
            says(TT(gk[:, :, 0:TOPK], top[:, :, 0:TOPK], spread(top[:, :, 0:1], 2, TOPK), ALU.subtract), "top_diff", 1)
            chosen, weighted = (v[:].rearrange("p i x s -> p i (x s)").rearrange("p i (k e) -> p i k e", k=TOPK) for v in (S, SG))
            by_choice = lambda v: spread(v[:, :, 0:TOPK].unsqueeze(3), 3, NE)
            dv(TT(chosen, spread(spread(iota_e[:].unsqueeze(1).unsqueeze(1), 1, 3), 2, TOPK), by_choice(topf), ALU.is_equal))
            dv(V.tensor_reduce(msk[:], chosen.rearrange("p i k e -> p i e k"), AX.X, ALU.add))
            says(V.tensor_copy(mskb[:], msk[:]), "mask_ready", 1)
            dve.wait_ge(*at("top_exp", 1))
            dv(V.tensor_reduce(gk[:, :, 4:5], gk[:, :, 0:TOPK], AX.X, ALU.add))
            dv(V.reciprocal(gk[:, :, 4:5], gk[:, :, 4:5]))
            dv(TT(gk[:, :, 0:TOPK], gk[:, :, 0:TOPK], spread(gk[:, :, 4:5], 2, TOPK), ALU.mult))
            dv(TT(weighted, chosen, by_choice(gk), ALU.mult))
            dv(V.tensor_reduce(gts[:], weighted.rearrange("p i k e -> p i e k"), AX.X, ALU.add))
            parts = ((0, 2, 128), (2, 3, TS))
            pairs = lambda v, i0, i1, n: v[0:n, 0:NPAIR, i0:i1, :]
            src = lambda v: v.rearrange("p i (q x) -> p q i x", x=2)
            for i0, i1, n in parts:
                dv(V.tensor_copy(pairs(sgate, i0, i1, n), src(gts[0:n, i0:i1, :])))
            await_fill(dve, "cum")
            cum = bank("cum")[:, 0:96].rearrange("p (i e) -> p i e", i=3)
            for i0, i1, n in parts:
                dv(TT(pairs(slot, i0, i1, n), src(cum[0:n, i0:i1, :]), src(msk[0:n, i0:i1, :]), ALU.mult))

            def wide(v, p):
                return spread(v[:, bass.ds(p, 1), :, :].rearrange("p a i x -> p (a i) x").unsqueeze(3), 3, SLOTS)

            slots4 = spread(spread(iota_s[:].unsqueeze(1).unsqueeze(1), 1, 3), 2, 2)

            def select(p):
                return TT(S[:], wide(slot, p), slots4, ALU.is_equal)

            def select_bias(p):
                return TSC(selb[0:96], half[0:96], selid[0:96, bass.ds(p, 1)], None, ALU.is_equal)

            def add_combined(c):
                i, nn = c // 2, c % 2
                n = TILES[i][1]
                dst = x1[0:n, i, 512 * nn:512 * nn + 512]
                return TT(dst, dst, psum[0:n, 6 + c % 2, :], ALU.add)

            STEPS = 6

            def pair_steps(p, gp, extra):
                k = [0]

                def dl(ins):
                    k[0] += 1
                    ins.then_inc(sem("dve_loop"), 1)
                    dve.wait_ge(sem("dve_loop"), gp * STEPS + k[0])

                dve.wait_ge(sem("sgt_ready"), gp)
                dl(TT(SG[:], S[:], wide(sgate, p), ALU.mult))
                dve.sem_inc(sem("sg_ready"), 1)
                dve.wait_ge(sem("gather_ready"), gp * 2 + 2)
                dl(select(p + 1))
                dve.sem_inc(sem("s_ready"), 1)
                for x in range(2):
                    for c in (range(0, 2) if x == 0 else range(4, 6)):
                        dve.wait_ge(sem("combine_ready"), gp * 6 + c + 1 + extra * 6)
                        add_combined(c).then_inc(sem("combine_added"), 1)
                    dve.wait_ge(sem("block_done"), gp * BLOCKS + 2 * x + 1)
                    if x == 0:
                        dve.wait_ge(sem("aT_ready"), gp * 2)
                    TSC(gact[:, x, :], psum[:, 2 * x, :], 7.0, None, ALU.min).then_inc(sem("g_clipped"), 1)
                    if x == 0:
                        for c in range(2, 4):
                            dve.wait_ge(sem("combine_ready"), gp * 6 + c + 1 + extra * 6)
                            add_combined(c).then_inc(sem("combine_added"), 1)
                    dve.wait_ge(sem("block_done"), gp * BLOCKS + 2 * x + 2)
                    dl(TSC(uact[:, x, :], psum[:, 2 * x + 1, :], 7.0, -7.0, ALU.min, ALU.max))
                    dve.wait_ge(sem("g_clipped"), gp * 2 + 1 + x)
                    dl(STT(out=uact[:, x, :], in0=uact[:, x, :], scalar=1.0, in1=gact[:, x, :], op0=ALU.add, op1=ALU.mult))
                    dve.wait_ge(sem("sig_ready"), gp * 2 + 1 + x)
                    TT(gact[:, x, :], uact[:, x, :], sg1[:, x, :], ALU.mult).then_inc(sem("act_ready"), 1)
                dve.wait_ge(sem("bias_used"), gp + 1)
                select_bias(p + 1).then_inc(sem("selb_ready"), 1)
                assert k[0] == STEPS

            def sweep(base, extra):
                with dve.Fori(0, NPAIR // 2) as q:
                    for u in range(2):
                        pair_steps(q * 2 + u, base + q * 2 + u, extra)
                for c in range(6):
                    dve.wait_ge(sem("combine_ready"), base * 6 + NPAIR * 6 + extra * 6 + c + 1)
                    add_combined(c).then_inc(sem("combine_added"), 1)
                V.memset(sgt[:], 0.0).then_inc(sem("sgt_cleared"), 1)

            says(select(0), "s_ready", 1)
            dv(V.tensor_reduce(st2[:, 8:9], bank("cum")[:, 96:128], AX.X, ALU.max))
            says(V.tensor_copy(cnt[:], st2[:, 8:9]), "count_ready", 1)
            says(select_bias(0), "selb_ready", 1)
            sweep(0, 0)
            most = dve.value_load(cnt[0:1, 0:1], min_val=0, max_val=T)
            with dve.If(most > SLOTS):
                with dve.Fori(1, SWEEPS) as r:
                    with dve.If(most > r * SLOTS):
                        TSC(iota_s[:], iota_s[:], float(SLOTS), None, ALU.add).then_inc(sem("slots_moved"), 1)
                        dve.wait_ge(sem("slots_moved"), r)
                        dve.wait_ge(sem("gather_ready"), r * (2 * NPAIR) + 2)
                        dve.wait_ge(sem("selb_ready"), r * NPAIR + 1)
                        select(0).then_inc(sem("reselected"), 1)
                        select_bias(0).then_inc(sem("reselected"), 1)
                        dve.wait_ge(sem("reselected"), r * 2)
                        dve.wait_ge(sem("regather_ready"), r * 2)
                        dve.sem_inc(sem("sweep_entered"), 1)
                        sweep(r * NPAIR, r)
            V.tensor_copy(st2[0:1, 13:14], x1[0:1, 0, 0:1]).then_inc(sem("sums_done"), 1)
            dve.wait_ge(sem("gf_loaded"), 16)
            for i, (t0, n) in enumerate(TILES):
                dve.wait_ge(sem("root3_ready"), i + 1)
                dv(V.reciprocal(st2[0:n, 4 + i:5 + i], st2[0:n, 4 + i:5 + i]))
                STT(out=x1[0:n, i, :], in0=x1[0:n, i, :], scalar=st2[0:n, 4 + i:5 + i], in1=gfb[0:n, :],
                    op0=ALU.mult, op1=ALU.mult).then_inc(sem("y_final"), 1)

        @block.tensor
        def _(pe):
            M, TR = nc.tensor.matmul, nc.tensor.transpose

            pe.wait_ge(*at("ident_ready", 1))
            pe.wait_ge(sem("vec_loaded"), 16 * 11)
            ends_fill(TR(bank("vec")[:, 0:NVEC], vrow[0:NVEC, :], ident[0:NVEC, 0:NVEC]), "vec")
            for k in range(6):
                i, hf = k // 2, k % 2
                t0, n = TILES[i]
                pe.wait_ge(*at("xn_ready", i + 1))
                await_bank(pe, f"hT{k}")
                for c in range(4):
                    m = TR(bank(f"hT{k}")[:, 128 * c:128 * c + n], xn[0:n, i, (4 * hf + c) * 128:(4 * hf + c + 1) * 128], ident[0:n, 0:n])
                ends_fill(m, f"hT{k}")
            pe.wait_ge(filled[FILLS["hT5"][0]], FILLS["hT5"][1] + 1)
            pe.sem_inc(says_now("xn_used"), 1)
            for k in range(6):
                b, f = FILLS[f"hT{k}"]
                pe.wait_ge(drained[b], f + 1)

            def channels(name, c, col):
                await_bank(pe, name)
                w = slot_view(c % 3, WCH[c][1])
                for k in range(KD):
                    m = M(bank(name)[:, 0:T], w[:, k, col:col + 128], hT[:, k, :], start=(k == 0), stop=(k == KD - 1))
                ends_fill(m, name)

            def tokens(name, c, col, i):
                await_bank(pe, name)
                t0, n = TILES[i]
                w = slot_view(c % 3, WCH[c][1])
                for k in range(KD):
                    if i < 2:
                        m = M(bank(name)[0:n, 0:256], hT[:, k, t0:t0 + n], w[:, k, col:col + 256], start=(k == 0), stop=(k == KD - 1))
                    else:
                        for x in range(2):
                            m = M(bank(name)[n * x:n * x + n, 0:128], hT[:, k, t0:t0 + n], w[:, k, col + 128 * x:col + 128 * x + 128],
                                  start=(k == 0), stop=(k == KD - 1))
                ends_fill(m, name)

            def used(name, count):
                b, f = FILLS[name]
                pe.wait_ge(filled[b], f + 1)
                pe.sem_inc(says_now("w_in_used"), 1)

            def s5_in(j):
                r0, tt = 32 * (j % 4), j // 4
                for x, name in enumerate((f"bu{j}r", f"bu{j}i")):
                    await_bank(pe, name)
                    ends_fill(M(bank(name)[:, 0:T], wB[r0:r0 + 32, 2 * x + tt, :], uT[r0:r0 + 32, tt, :], start=True, stop=True), name)

            def s5_out(j):
                r0, tt = 32 * (j % 4), j // 4
                pe.wait_ge(*at("s5_turned", j + 1))
                out = bank(f"ys{tt}")[r0:r0 + 32, 0:T]
                M(out, wC[:, tt, r0:r0 + 32], s_r[:, j % 2, :], start=True, stop=False)
                M(out, wC[:, 2 + tt, r0:r0 + 32], s_i[:, j % 2, :], start=False, stop=True).then_inc(says_now("s5_used"), 1)
                if j % 4 == 3:
                    pe.wait_ge(*at("s5_used", j + 1))
                    pe.sem_inc(filled[FILLS[f"ys{tt}"][0]], 1)

            pe.wait_ge(sem("w_in0"), 16)
            for n, name in enumerate(("u0", "u1", "xr0", "xr1")):
                channels(name, 0, 128 * n)
            used("xr1", 1)
            pe.wait_ge(sem("wgate_loaded"), 32)
            await_bank(pe, "gates")
            for k in range(KD):
                m = M(bank("gates")[0:36, 0:T], wgate[:, k, :], hT[:, k, :], start=(k == 0), stop=(k == KD - 1))
            ends_fill(m, "gates")
            pe.wait_ge(sem("w_in1"), 16)
            for n, name in enumerate(("gr0", "gr1", "q0", "q1")):
                channels(name, 1, 128 * n)
                if n == 1:
                    pe.wait_ge(sem("par_loaded"), 16 * 5)
                    await_bank(pe, "par")
                    TR(bank("par")[:, 0:128], srow[:], ident[:])
                    ends_fill(TR(bank("par")[:, 128:224], prow[0:96, :], ident[0:96, 0:96]), "par")
                    pe.wait_ge(*at("bb_ready", 4))
                    await_bank(pe, "bt")
                    for x in range(4):
                        m = TR(bank("bt")[:, 128 * x:128 * x + 128], BB[:, 4 * x:4 * x + 4].rearrange("p j g c -> p (j g c)"), ident[:])
                    ends_fill(m, "bt")
                    pe.wait_ge(*at("cb_ready", 2))
                    await_bank(pe, "ct")
                    for x in range(4):
                        m = TR(bank("ct")[:, 128 * x:128 * x + 128], CBk[:, x, :], ident[:])
                    ends_fill(m, "ct")
            used("q1", 2)
            pe.sem_inc(says_now("cb_used"), 1)
            pe.wait_ge(sem("w_in2"), 16)
            for n, name in enumerate(("q2", "q3", "k0", "k1")):
                channels(name, 2, 128 * n)
            used("k1", 3)
            pe.wait_ge(sem("wax_loaded"), 16 * 16)
            pe.wait_ge(*at("xc_ready", 2))
            for x, nm in enumerate(("r", "i")):
                for tt in range(2):
                    await_bank(pe, f"{nm}{tt}")
                    ends_fill(M(bank(f"{nm}{tt}")[:, 0:T], wax[:, x, tt, :], xc[:, tt, :], start=True, stop=True), f"{nm}{tt}")
            for n in ("u0", "u1", "bt", "ct"):
                pe.wait_ge(drained[FILLS[n][0]], FILLS[n][1] + 1)
            s5_in(0)
            s5_in(1)
            pe.wait_ge(sem("w_in3"), 16)
            channels("k2", 3, 0)
            channels("k3", 3, 128)
            s5_in(2)
            for i in range(3):
                tokens(f"va{i}", 3, 256, i)
            used("va2", 4)
            s5_in(3)
            s5_out(0)
            pe.wait_ge(sem("w_in4"), 16)
            tokens("vb0", 4, 0, 0)
            tokens("vb1", 4, 0, 1)
            s5_out(1)
            s5_in(4)
            tokens("vb2", 4, 0, 2)
            tokens("oa0", 4, 256, 0)
            s5_out(2)
            s5_in(5)
            tokens("oa1", 4, 256, 1)
            tokens("oa2", 4, 256, 2)
            used("oa2", 5)
            s5_out(3)
            s5_in(6)
            pe.wait_ge(sem("w_in5"), 16)
            tokens("ob0", 5, 0, 0)
            s5_out(4)
            s5_in(7)
            tokens("ob1", 5, 0, 1)
            tokens("ob2", 5, 0, 2)
            used("ob2", 6)
            s5_out(5)
            pe.wait_ge(*at("gate_rows_exp", 3))
            await_bank(pe, "rows")
            for i, (t0, n) in enumerate(TILES):
                m = TR(bank("rows")[0:n, 128 * i:128 * i + 128], rows[:, t0:t0 + n], ident[:])
            ends_fill(m, "rows")
            for h in range(H):
                b, f = FILLS[f"k{h}"]
                pe.wait_ge(drained[b], f + 1)

            def scores(h):
                await_bank(pe, f"mb{h}")
                ends_fill(M(bank(f"mb{h}")[:, 0:T], sel4[:, h, :], gsm[0:H, 4, :], start=True, stop=True), f"mb{h}")
                await_bank(pe, f"st{h}")
                sb_ = bank(f"st{h}")
                M(sb_[:, 0:256], kT[:, h, 0:128], qT[:, h, 0:256], start=True, stop=True)
                M(sb_[:, 256:384], kT[:, h, 128:256], qT[:, h, 128:256], start=True, stop=True)
                ends_fill(M(sb_[0:TS, 384:416], kT[:, h, TP:T], qT[:, h, TP:T], start=True, stop=True), f"st{h}")

            pe.wait_ge(*at("sel4_ready", 1))
            pe.wait_ge(*at("m_rows", 1))
            for h in range(H):
                scores(h)
            s5_out(6)
            s5_out(7)
            for i, (t0, n) in enumerate(TILES):
                await_bank(pe, f"kt{i}")
                for h in range(H):
                    m = TR(bank(f"kt{i}")[0:n, 128 * h:128 * h + 128], kT[:, h, t0:t0 + n], ident[:])
                ends_fill(m, f"kt{i}")
            await_bank(pe, "dec")
            for h in range(H):
                m = M(bank("dec")[:, NB * h:NB * h + NB], sel4[:, h, :], gsm[0:H, 6, TS:TS + NB], start=True, stop=True)
            ends_fill(m, "dec")
            pe.wait_ge(*at("scm_ready", NB))
            for h in range(H):
                await_bank(pe, f"sc{h}")
                ends_fill(M(bank(f"sc{h}")[:, 0:NB * TS], sel4[:, h, :], scm[:].rearrange("h b t -> h (b t)"), start=True, stop=True), f"sc{h}")
            pe.wait_ge(*at("rgfin_ready", 1))
            await_bank(pe, "rgT")
            for x in range(2):
                TR(bank("rgT")[0:9, 128 * x:128 * x + 128], rgfin[:, x, :], ident[:])
            for x in range(2):
                m = TR(bank("rgT")[0:27, 256 + 128 * x:384 + 128 * x], cvfin[:, x, :], ident[:])
            ends_fill(m, "rgT")
            await_bank(pe, "s5T")
            for x in range(2):
                m = TR(bank("s5T")[0:72, 128 * x:128 * x + 128], fin5[:, x].rearrange("p s j -> p (s j)"), ident[:])
            ends_fill(m, "s5T")
            pe.wait_ge(*at("ones_ready", 1))
            for n in ("vb2", "vb1", "vb0", "va2", "va1", "va0"):
                pe.wait_ge(drained[FILLS[n][0]], FILLS[n][1] + 1)
            for h in range(H):
                b, f = FILLS[f"st{h}"]
                pe.wait_ge(drained[b], f + 1)
            for i in range(3):
                n = TILES[i][1]
                if i == 2:
                    pe.wait_ge(*at("kw_ready", 1))
                    for hh in range(2):
                        await_bank(pe, f"cp{hh}")
                        for x in range(2):
                            h = 2 * hh + x
                            for j in range(2):
                                m = M(bank(f"cp{hh}")[:, 129 * x:129 * x + 129], kw[:, j, h, :], v_tok[:, j, h, :], start=(j == 0), stop=(j == 1))
                        ends_fill(m, f"cp{hh}")
                    pe.wait_ge(*at("qm_ready", 1))
                for hh in range(2):
                    name = f"nu{i}{hh}"
                    await_bank(pe, name)
                    for x in range(2):
                        h = 2 * hh + x
                        out = bank(name)[0:n, 129 * x:129 * x + 129]
                        if i == 2:
                            M(out, E[0:TS, h, 384:416], v_tok[0:TS, 2, h, :], start=True, stop=False)
                            for b in range(NB):
                                m = M(out, qm[:, h, b, :], c0[:, h, b, :], start=False, stop=(b == NB - 1))
                        elif i == 0:
                            m = M(out, E[:, h, 0:128], v_tok[:, 0, h, :], start=True, stop=True)
                        else:
                            M(out, E[:, h, 128:256], v_tok[:, 0, h, :], start=True, stop=False)
                            m = M(out, E[:, h, 256:384], v_tok[:, 1, h, :], start=False, stop=True)
                    ends_fill(m, name)
            pe.wait_ge(filled[FILLS["nu21"][0]], FILLS["nu21"][1] + 1)
            pe.sem_inc(says_now("c0_used"), 1)
            pe.wait_ge(*at("s5_gelu", 1))
            pe.wait_ge(sem("glw_loaded"), 16)
            for x in range(2):
                await_bank(pe, f"glu{x}")
                for k in range(2):
                    m = M(bank(f"glu{x}")[:, 0:T], glw[:, k, 128 * x:128 * x + 128], rt[:, k, :], start=(k == 0), stop=(k == 1))
                ends_fill(m, f"glu{x}")

            def memory_update(h, g):
                b0, b1 = CB[g]
                pe.wait_ge(*at("vw_ready", h + 1))
                name = f"cu{h}{g}"
                await_bank(pe, name)
                ends_fill(M(bank(name)[:, 0:(b1 - b0) * 129], k_tok[0:TS, 2, 128 * h:128 * h + 128],
                            vw[:, h, b0:b1, :].rearrange("p b v -> p (b v)"), start=True, stop=True), name)

            def output(i, c, k):
                t0, n = TILES[i]
                name = f"wo{i}{c}"
                if k == 0:
                    await_bank(pe, name)
                m = M(bank(name)[0:n, :], hT[:, k, t0:t0 + n], slot_view(2 + c, 512)[:, k, :], start=(k == 0), stop=(k == KD - 1))
                if k == KD - 1:
                    ends_fill(m, name)

            for h in range(H):
                pe.wait_ge(*at("y3_ready", h + 1))
                await_bank(pe, f"yT{h}")
                for i, (t0, n) in enumerate(TILES):
                    m = TR(bank(f"yT{h}")[:, t0:t0 + n], o_tok[0:n, i, 128 * h:128 * h + 128], ident[0:n, 0:n])
                ends_fill(m, f"yT{h}")
            b, f = FILLS["yT3"]
            pe.wait_ge(filled[b], f + 1)
            pe.sem_inc(says_now("y_turned"), 1)
            pe.wait_ge(*at("rg_used", 1))
            pe.wait_ge(*at("mix_ready", 1))
            for n in range(2):
                pe.wait_ge(sem(f"w_out{n}"), 16)
            for m in range(2 * KD):
                k, c = m % 4 + 4 * (m // 8), m // 4 % 2
                if m == 8:
                    for h in range(H):
                        b, f = FILLS[f"yT{h}"]
                        pe.wait_ge(drained[b], f + 1)
                output(0, c, k)
                if 2 <= m < 2 + H * len(CB):
                    memory_update((m - 2) // len(CB), (m - 2) % len(CB))
            for name in ("cu30", "cu31", "cu32"):
                pe.wait_ge(filled[FILLS[name][0]], FILLS[name][1] + 1)
            pe.sem_inc(says_now("mlstm_done"), 1)
            pe.wait_ge(*at("c_new", H))
            pe.wait_ge(*at("c_prompt", 2))
            await_bank(pe, "nT")
            ends_fill(TR(bank("nT")[0:36, 0:128], nbuf[:], ident[:]), "nT")
            await_bank(pe, "wo2")
            for k in range(KD):
                for c in range(4):
                    m = M(bank("wo2")[TS * c:TS * c + TS, 0:256], hT[:, k, TP:T],
                          slot_view(2 + c // 2, 512)[:, k, 256 * (c % 2):256 * (c % 2) + 256], start=(k == 0), stop=(k == KD - 1))
            ends_fill(m, "wo2")
            def turn_rows(i, halves=(0, 1)):
                t0, n = TILES[i]
                for hf in halves:
                    pe.wait_ge(*at("x2_ready", (0, 4, 2)[i] + hf + 1))
                    name = f"h2T{2 * i + hf}"
                    await_bank(pe, name)
                    for c in range(4):
                        m = TR(bank(name)[:, 128 * c:128 * c + n], xn[0:n, i, (4 * hf + c) * 128:(4 * hf + c + 1) * 128], ident[0:n, 0:n])
                    ends_fill(m, name)

            def logits(i, hf):
                t0, n = TILES[i]
                b, f = FILLS[f"h2T{2 * i + hf}"]
                pe.wait_ge(drained[b], f + 1)
                for k in range(4 * hf, 4 * hf + 4):
                    m = M(bank("lg")[0:n, NE * i:NE * i + NE], h2T[:, k, t0:t0 + n], rw[:, k, :], start=(k == 0), stop=(k == KD - 1))
                return m

            for c in range(2):
                for k in range(KD):
                    output(1, c, k)
                if c == 0:
                    turn_rows(0)
                    turn_rows(2)
            pe.wait_ge(filled[FILLS["wo11"][0]], FILLS["wo11"][1] + 1)
            pe.sem_inc(says_now("w_out_used"), 1)
            pe.wait_ge(sem("router_loaded"), 48)
            turn_rows(1, (0,))
            await_bank(pe, "lg")
            for i in (0, 2):
                for hf in range(2):
                    logits(i, hf)
            turn_rows(1, (1,))
            logits(1, 0)
            ends_fill(logits(1, 1), "lg")

            def stay_busy(n):
                for _ in range(n):
                    M(psum[:, 7, :], ones_bf[0:96, :], bsplit[0:96, 0:512], start=True, stop=True)

            stay_busy(14)
            pe.wait_ge(*at("mask_ready", 1))
            await_bank(pe, "cum")
            for i, (t0, n) in enumerate(TILES):
                for j in range(i + 1):
                    nj = TILES[j][1]
                    lhs = upper[0:nj, 0:n] if j == i else ones_bf[0:nj, 0:n]
                    M(bank("cum")[0:n, NE * i:NE * i + NE], lhs, mskb[0:nj, j, :], start=(j == 0), stop=(j == i))
            for i, (t0, n) in enumerate(TILES):
                m = M(bank("cum")[:, 96:128], ones_bf[0:n, :], mskb[0:n, i, :], start=(i == 0), stop=(i == 2))
            ends_fill(m, "cum")

            W1COL = [0, 2, 1, 3]

            def gather(name):
                for c in range(KD):
                    for i, (t0, n) in enumerate(TILES):
                        m = M(psum[:, 6 + c // 4, 128 * (c % 4):128 * (c % 4) + 128], xn[0:n, i, 128 * c:128 * c + 128],
                              S[0:n, i].rearrange("p x s -> p (x s)"), start=(i == 0), stop=(i == 2))
                    if c % 4 == 3:
                        m.then_inc(sem(name), 1)

            def combine(c):
                i, nn = c // 2, c % 2
                t0, n = TILES[i]
                M(psum[0:n, 6 + c % 2, :], sgt[:, t0:t0 + n], yb[:, nn, :], start=True, stop=True).then_inc(sem("combine_ready"), 1)

            def bias(bk, col):
                return M(psum[:, bk, :], selb[0:96].rearrange("p x s -> p (x s)"), bsplit[0:96, col:col + 512], start=True, stop=False)

            def pair_steps(gp, twos, u, extra):
                def await_chunks(w):
                    for x in range(2):
                        s, _ = ring_slot(BLOCKS * u + w, x)
                        pe.wait_ge(sem(f"expert_chunk{s}"), twos * 48 + 16 * ((BLOCKS * u + w) // DEPTH) + 16)

                def turn_activations(x):
                    pe.wait_ge(sem("act_ready"), gp * 2 + 1 + x)
                    for c in range(4):
                        m = TR(psum[:, x, 128 * c:128 * c + 128], gact[:, x, 128 * c:128 * c + 128], ident[:])
                    m.then_inc(sem("aT_ready"), 1)

                pe.wait_ge(sem("selb_ready"), gp + 1)
                pe.wait_ge(sem("xg_copied"), gp * 2 + 2)
                for w in range(4):
                    if w < 2:
                        pe.wait_ge(sem("aT_copied"), gp * 2)
                    bias(w, [0, FF, 512, FF + 512][w])
                    await_chunks(w)
                    for k in range(KD):
                        for x in range(2):
                            m = M(psum[64 * x:64 * x + 64, w, :], xg[:, k, 64 * x:64 * x + 64],
                                  ring_slot(BLOCKS * u + w, x)[1][:, 512 * k:512 * k + 512], start=False, stop=(k == KD - 1))
                    m.then_inc(sem("block_done"), 1)
                    if w < 3:
                        for c in (2 * w, 2 * w + 1):
                            if c < 2:
                                if c == 0:
                                    pe.wait_ge(sem("y_copied"), gp * 2)
                                    pe.wait_ge(sem("sgt_copied"), gp)
                            else:
                                pe.wait_ge(sem("combine_added"), gp * 6 + c - 1 + extra * 6)
                            combine(c)
                    if w == 2:
                        pe.wait_ge(sem("combine_added"), gp * 6 + 6 + extra * 6)
                        pe.wait_ge(sem("s_ready"), gp + 2)
                        gather("gather_ready")
                turn_activations(0)
                pe.wait_ge(sem("sg_ready"), gp + 1)
                pe.wait_ge(sem("xg_copied"), gp * 2 + 3)
                for i, (t0, n) in enumerate(TILES):
                    m = TR(psum[:, 6, t0:t0 + n], SG[0:n, i].rearrange("p x s -> p (x s)"), ident[0:n, 0:n])
                m.then_inc(sem("sgt_ready"), 1)
                for nn in range(2):
                    m = bias(4 + nn, 2 * FF + 512 * nn)
                m.then_inc(sem("bias_used"), 1)
                turn_activations(1)
                for hf in range(2):
                    await_chunks(4 + hf)
                    pe.wait_ge(sem("aT_copied"), gp * 2 + 1 + hf)
                    for k in range(4):
                        if hf == 1 and k == 2:
                            pe.wait_ge(sem("last_half"), gp * 32 + 32)
                        for nn in range(2):
                            for x in range(2):
                                m = M(psum[64 * x:64 * x + 64, 4 + nn, :], aT[:, 4 * hf + k, 64 * x:64 * x + 64],
                                      ring_slot(BLOCKS * u + 4 + hf, x)[1][:, 1024 * k + 512 * nn:1024 * k + 512 * nn + 512],
                                      start=False, stop=(hf == 1 and k == 3))
                    m.then_inc(sem("block_done"), 1)

            def sweep(base, base_twos, extra):
                with pe.Fori(0, NPAIR // 2) as q:
                    for u in range(2):
                        pair_steps(base + q * 2 + u, base_twos + q, u, extra)
                pe.wait_ge(sem("y_copied"), base * 2 + NPAIR * 2)
                pe.wait_ge(sem("sgt_copied"), base + NPAIR)
                pe.wait_ge(sem("xg_copied"), base * 2 + NPAIR * 2 + 2)
                for c in range(6):
                    if c >= 2:
                        pe.wait_ge(sem("combine_added"), base * 6 + NPAIR * 6 + extra * 6 + c - 1)
                    combine(c)

            stay_busy(8)
            pe.wait_ge(sem("s_ready"), 1)
            gather("gather_ready")
            sweep(0, 0, 0)
            pe.wait_ge(*at("count_ready", 1))
            most = pe.value_load(cnt[0:1, 0:1], min_val=0, max_val=T)
            with pe.If(most > SLOTS):
                with pe.Fori(1, SWEEPS) as r:
                    with pe.If(most > r * SLOTS):
                        pe.wait_ge(sem("sgt_cleared"), r)
                        pe.wait_ge(sem("reselected"), r * 2)
                        gather("regather_ready")
                        pe.wait_ge(sem("xg_recopied"), r * 2)
                        pe.sem_inc(sem("sweep_entered"), 1)
                        sweep(r * NPAIR, r * (NPAIR // 2), r)


_INS = ["x_prompt", "x_sample", "state_s5_re", "state_s5_im", "state_rg_h", "state_rg_conv", "state_ml_c",
        "state_ml_n", "state_ml_m", "norm1_g", "w_in", "s5_lambda_re", "s5_lambda_im", "s5_log_step", "s5_b_re",
        "s5_b_im", "s5_c_re", "s5_c_im", "s5_d", "s5_glu_w", "s5_glu_b", "rg_conv_w", "rg_conv_b", "rg_wa", "rg_ba",
        "rg_wx", "rg_bx", "rg_lambda", "ml_gate_bias", "ml_norm_g", "w_out", "norm2_g", "router_w", "router_b",
        "exp_w1", "exp_b1", "exp_w2", "exp_b2", "final_norm_g"]
_STATES = lambda b: [(1, b, G5, P5), (1, b, G5, P5), (1, b, 256), (1, b, 3, 256), (1, b, H, DK, DK), (1, b, H, DK), (1, b, H)]
_OUTS = [(1, TP, D), (NB, NT, D)] + _STATES(1) + _STATES(NB)


def kernel(**inputs):
    import numpy as _np
    import concourse.bacc as _bacc
    from concourse.bass_utils import run_bass_kernel_spmd as _run

    nc = _bacc.Bacc("TRN2", target_bir_lowering=False, num_devices=1)
    arrays, args = {}, {}
    for name in _INS:
        v = _np.ascontiguousarray(inputs[name])
        arrays[f"in_{name}_dram"] = v
        args[name] = nc.dram_tensor(f"in_{name}_dram", v.shape, mybir.dt.from_np(v.dtype), kind="ExternalInput").ap()
    outs = [nc.dram_tensor(f"out_{i}_dram", shape, F32, kind="ExternalOutput").ap() for i, shape in enumerate(_OUTS)]
    build_program(nc, args, outs)
    r = _run(nc, [arrays], core_ids=[0])
    return tuple(r.results[0][f"out_{i}_dram"] for i in range(len(_OUTS)))
```
